# Optimizing a Trainium2 kernel written in Bass

```python
import jax
import jax.numpy as jnp
from jax import lax
import jax, jax.numpy as jnp
import numpy as np

D_MODEL = 1024
BATCH = 1
SEQ = 256
DEPTH = 1

HEAD_DIM = 64
NSA_HEADS = 8
NSA_KV = 2
SWA_HEADS = 8
SWA_KV = 1
CMP_STRIDE = 16
CMP_LEN = 2 * CMP_STRIDE
CMP_HIDDEN = 256
SEL_LEN = 64
SEL_TOPN = 16
SEL_LOCAL = 2
NSA_WINDOW = 512
SWA_WINDOW = 128
Q_BLOCK = 128
D_FF = 2816
ROPE_THETA = 10000.0
RMS_EPS = 1e-6
FFN_HALF = 0.5
NEG_INF = -1e30
FORCE = 1e9

NSA_Q_W = NSA_HEADS * HEAD_DIM
NSA_KV_W = NSA_KV * HEAD_DIM
NSA_GATE_W = 3 * NSA_HEADS
SWA_Q_W = SWA_HEADS * HEAD_DIM
SWA_KV_W = SWA_KV * HEAD_DIM
IN_WIDTHS = (NSA_Q_W, NSA_KV_W, NSA_KV_W, NSA_KV_W, NSA_KV_W, NSA_KV_W, NSA_KV_W, NSA_GATE_W,
             SWA_Q_W, SWA_KV_W, SWA_KV_W, D_MODEL, D_MODEL)


def _split_points():
    pts, acc = [], 0
    for w in IN_WIDTHS[:-1]:
        acc += w
        pts.append(acc)
    return pts

def _rmsnorm(x, g):
    xf = x.astype(jnp.float32)
    y = xf * lax.rsqrt(jnp.mean(xf * xf, axis=-1, keepdims=True) + RMS_EPS)
    return (y * g.astype(jnp.float32)).astype(x.dtype)

def _swiglu(x, w_gate, w_up, w_down):
    return (jax.nn.silu(x @ w_gate) * (x @ w_up)) @ w_down

def _rope(x, pos):
    half = HEAD_DIM // 2
    inv_freq = ROPE_THETA ** (-jnp.arange(half, dtype=jnp.float32) / half)
    ang = pos.astype(jnp.float32)[..., None] * inv_freq
    cos = jnp.cos(ang)[:, :, None, :]
    sin = jnp.sin(ang)[:, :, None, :]
    xf = x.astype(jnp.float32)
    x1, x2 = xf[..., :half], xf[..., half:]
    return jnp.concatenate([x1 * cos - x2 * sin, x2 * cos + x1 * sin], axis=-1).astype(x.dtype)

def _banded_attention(q, k, v, window, sink):
    B, S, H, D = q.shape
    G = k.shape[2]
    R = H // G
    nb = S // Q_BLOCK
    pad = -(-window // Q_BLOCK) * Q_BLOCK
    L = pad + Q_BLOCK
    kp = jnp.pad(k, ((0, 0), (pad, 0), (0, 0), (0, 0)))
    vp = jnp.pad(v, ((0, 0), (pad, 0), (0, 0), (0, 0)))
    idx = jnp.arange(nb)[:, None] * Q_BLOCK + jnp.arange(L)[None, :]
    kb = kp[:, idx]
    vb = vp[:, idx]
    qb = q.reshape(B, nb, Q_BLOCK, G, R, D)
    s = jnp.einsum('bnqgrd,bnkgd->bngrqk', qb, kb).astype(jnp.float32) * (D ** -0.5)
    qpos = jnp.arange(nb)[:, None] * Q_BLOCK + jnp.arange(Q_BLOCK)[None, :]
    kpos = idx - pad
    diff = qpos[:, :, None] - kpos[:, None, :]
    mask = (diff >= 0) & (diff < window) & (kpos[:, None, :] >= 0)
    s = jnp.where(mask[None, :, None, None], s, NEG_INF)
    if sink is None:
        p = jax.nn.softmax(s, axis=-1)
    else:
        sk = sink.astype(jnp.float32).reshape(G, R)[None, None, :, :, None, None]
        m = jnp.maximum(jnp.max(s, axis=-1, keepdims=True), sk)
        e = jnp.exp(s - m)
        p = e / (jnp.sum(e, axis=-1, keepdims=True) + jnp.exp(sk - m))
    o = jnp.einsum('bngrqk,bnkgd->bnqgrd', p.astype(vb.dtype), vb)
    return o.reshape(B, S, H, D)

def _compress(kv, pe, w1, w2):
    B, S, G, D = kv.shape
    c = kv.reshape(B, S // CMP_STRIDE, CMP_STRIDE, G, D)
    blocks = jnp.concatenate([c[:, :-1], c[:, 1:]], axis=2)
    blocks = blocks + pe[None, None, :, None, :]
    n_cmp = blocks.shape[1]
    flat = blocks.transpose(0, 1, 3, 2, 4).reshape(B, n_cmp, G, CMP_LEN * D)
    return jax.nn.gelu(flat @ w1) @ w2

def _nsa(q, k_cmp, v_cmp, k_slc, v_slc, k_win, v_win, gates, pos, pe_k, wk1, wk2, pe_v, wv1, wv2):
    B, S, H, D = q.shape
    G = NSA_KV
    R = H // G
    scale = D ** -0.5
    n_sel = S // SEL_LEN
    n_top = min(SEL_TOPN, n_sel)
    nb = S // Q_BLOCK
    qg = q.reshape(B, S, G, R, D)
    t = jnp.arange(S)

    kc = _compress(k_cmp, pe_k, wk1, wk2)
    vc = _compress(v_cmp, pe_v, wv1, wv2)
    n_cmp = kc.shape[1]
    kc = _rope(kc, pos[:, CMP_LEN - 1::CMP_STRIDE])
    end = jnp.arange(n_cmp) * CMP_STRIDE + CMP_LEN - 1
    vis = end[None, :] <= t[:, None]
    s = jnp.einsum('bsgrd,bcgd->bgrsc', qg, kc).astype(jnp.float32) * scale
    s = jnp.where(vis, s, NEG_INF)
    p_cmp = jnp.where(vis, jax.nn.softmax(s, axis=-1), 0.0)
    o_cmp = jnp.einsum('bgrsc,bcgd->bsgrd', p_cmp.astype(vc.dtype), vc)

    cs = jnp.arange(n_cmp) * CMP_STRIDE
    ss = jnp.arange(n_sel) * SEL_LEN
    overlap = jnp.clip(jnp.minimum(cs[:, None] + CMP_LEN, ss[None, :] + SEL_LEN)
                       - jnp.maximum(cs[:, None], ss[None, :]), 0, None).astype(jnp.float32) / CMP_LEN
    imp = jnp.einsum('bgrsc,cj->bgsj', p_cmp, overlap)
    blk = jnp.arange(n_sel)[None, :]
    tb = (t // SEL_LEN)[:, None]
    forced = (blk == 0) | ((tb - blk >= 0) & (tb - blk < SEL_LOCAL))
    imp = jnp.where(forced, FORCE, jnp.where(blk > tb, -FORCE, imp))
    _, sel = lax.top_k(imp, n_top)

    kT = k_slc.transpose(0, 2, 1, 3)
    vT = v_slc.transpose(0, 2, 1, 3)
    offs = jnp.arange(SEL_LEN)
    gather = jax.vmap(jax.vmap(lambda a, i: a[i]))

    def one_block(args):
        qb, selb, tq = args
        idx = (selb[..., None] * SEL_LEN + offs).reshape(B, G, Q_BLOCK, n_top * SEL_LEN)
        kb = gather(kT, idx)
        vb = gather(vT, idx)
        sc = jnp.einsum('bqgrd,bgqtd->bgrqt', qb, kb).astype(jnp.float32) * scale
        m = (idx <= tq[None, None, :, None])[:, :, None]
        pr = jax.nn.softmax(jnp.where(m, sc, NEG_INF), axis=-1)
        return jnp.einsum('bgrqt,bgqtd->bqgrd', pr.astype(vb.dtype), vb)

    qs = qg.reshape(B, nb, Q_BLOCK, G, R, D).transpose(1, 0, 2, 3, 4, 5)
    sels = sel.reshape(B, G, nb, Q_BLOCK, n_top).transpose(2, 0, 1, 3, 4)
    tqs = t.reshape(nb, Q_BLOCK)
    o_slc = lax.map(one_block, (qs, sels, tqs))
    o_slc = o_slc.transpose(1, 0, 2, 3, 4, 5).reshape(B, S, G, R, D)

    o_win = _banded_attention(q, k_win, v_win, NSA_WINDOW, None).reshape(B, S, G, R, D)

    g = jax.nn.sigmoid(gates.astype(jnp.float32)).reshape(B, S, 3, G, R, 1)
    o = (g[:, :, 0] * o_cmp.astype(jnp.float32) + g[:, :, 1] * o_slc.astype(jnp.float32)
         + g[:, :, 2] * o_win.astype(jnp.float32))
    return o.astype(q.dtype).reshape(B, S, H * D)

def first_inputs(seed: int = 0) -> dict:
    key = jax.random.key(seed)
    ks = jax.random.split(key, 24)
    f32 = jnp.float32

    def w(k, shape, fan_in):
        return jax.random.normal(k, shape, f32) * fan_in ** -0.5

    def gain(k, shape):
        return 1.0 + 0.02 * jax.random.normal(k, shape, f32)

    w_in_width = sum(IN_WIDTHS)
    return {
        'x': jax.random.normal(ks[0], (BATCH, SEQ, D_MODEL), f32),
        'positions': jnp.broadcast_to(jnp.arange(SEQ, dtype=jnp.int32), (BATCH, SEQ)),
        'norm_ffn1': gain(ks[1], (DEPTH, D_MODEL)),
        'ffn1_gate': w(ks[2], (DEPTH, D_MODEL, D_FF), D_MODEL),
        'ffn1_up': w(ks[3], (DEPTH, D_MODEL, D_FF), D_MODEL),
        'ffn1_down': w(ks[4], (DEPTH, D_FF, D_MODEL), D_FF),
        'norm_mix': gain(ks[5], (DEPTH, D_MODEL)),
        'w_in': w(ks[6], (DEPTH, D_MODEL, w_in_width), D_MODEL),
        'cmp_pe_k': 0.1 * jax.random.normal(ks[7], (DEPTH, CMP_LEN, HEAD_DIM), f32),
        'cmp_k_w1': w(ks[8], (DEPTH, CMP_LEN * HEAD_DIM, CMP_HIDDEN), CMP_LEN * HEAD_DIM),
        'cmp_k_w2': w(ks[9], (DEPTH, CMP_HIDDEN, HEAD_DIM), CMP_HIDDEN),
        'cmp_pe_v': 0.1 * jax.random.normal(ks[10], (DEPTH, CMP_LEN, HEAD_DIM), f32),
        'cmp_v_w1': w(ks[11], (DEPTH, CMP_LEN * HEAD_DIM, CMP_HIDDEN), CMP_LEN * HEAD_DIM),
        'cmp_v_w2': w(ks[12], (DEPTH, CMP_HIDDEN, HEAD_DIM), CMP_HIDDEN),
        'swa_sinks': jax.random.normal(ks[13], (DEPTH, SWA_HEADS), f32),
        'w_branch_a': w(ks[14], (DEPTH, NSA_Q_W, D_MODEL), NSA_Q_W),
        'w_branch_b': w(ks[15], (DEPTH, SWA_Q_W, D_MODEL), SWA_Q_W),
        'w_out': w(ks[16], (DEPTH, D_MODEL, D_MODEL), D_MODEL),
        'norm_ffn2': gain(ks[17], (DEPTH, D_MODEL)),
        'ffn2_gate': w(ks[18], (DEPTH, D_MODEL, D_FF), D_MODEL),
        'ffn2_up': w(ks[19], (DEPTH, D_MODEL, D_FF), D_MODEL),
        'ffn2_down': w(ks[20], (DEPTH, D_FF, D_MODEL), D_FF),
        'norm_final': gain(ks[21], (D_MODEL,)),
    }

def first_block(x, positions, norm_ffn1, ffn1_gate, ffn1_up, ffn1_down, norm_mix, w_in,
              cmp_pe_k, cmp_k_w1, cmp_k_w2, cmp_pe_v, cmp_v_w1, cmp_v_w2, swa_sinks,
              w_branch_a, w_branch_b, w_out, norm_ffn2, ffn2_gate, ffn2_up, ffn2_down, norm_final):
    B, S, _ = x.shape
    pts = _split_points()
    h = x
    for i in range(DEPTH):
        h = h + FFN_HALF * _swiglu(_rmsnorm(h, norm_ffn1[i]), ffn1_gate[i], ffn1_up[i], ffn1_down[i])

        u = _rmsnorm(h, norm_mix[i])
        (nq, kc, vc, ksl, vsl, kwn, vwn, ng, sq, sk, sv, ga, gb) = jnp.split(u @ w_in[i], pts, axis=-1)
        nq = _rope(nq.reshape(B, S, NSA_HEADS, HEAD_DIM), positions)
        kc = kc.reshape(B, S, NSA_KV, HEAD_DIM)
        vc = vc.reshape(B, S, NSA_KV, HEAD_DIM)
        ksl = _rope(ksl.reshape(B, S, NSA_KV, HEAD_DIM), positions)
        vsl = vsl.reshape(B, S, NSA_KV, HEAD_DIM)
        kwn = _rope(kwn.reshape(B, S, NSA_KV, HEAD_DIM), positions)
        vwn = vwn.reshape(B, S, NSA_KV, HEAD_DIM)
        o_a = _nsa(nq, kc, vc, ksl, vsl, kwn, vwn, ng, positions,
                   cmp_pe_k[i], cmp_k_w1[i], cmp_k_w2[i], cmp_pe_v[i], cmp_v_w1[i], cmp_v_w2[i])

        sq = _rope(sq.reshape(B, S, SWA_HEADS, HEAD_DIM), positions)
        sk = _rope(sk.reshape(B, S, SWA_KV, HEAD_DIM), positions)
        sv = sv.reshape(B, S, SWA_KV, HEAD_DIM)
        o_b = _banded_attention(sq, sk, sv, SWA_WINDOW, swa_sinks[i]).reshape(B, S, SWA_Q_W)

        merged = jax.nn.sigmoid(ga) * (o_a @ w_branch_a[i]) + jax.nn.sigmoid(gb) * (o_b @ w_branch_b[i])
        h = h + merged @ w_out[i]

        h = h + FFN_HALF * _swiglu(_rmsnorm(h, norm_ffn2[i]), ffn2_gate[i], ffn2_up[i], ffn2_down[i])
    return _rmsnorm(h, norm_final)


DEPTH_2 = 2

MLA_HEADS = 8
MLA_NOPE = 64
MLA_ROPE = 32
MLA_V = 64
MLA_Q_RANK = 768
MLA_KV_RANK = 256
DSA_HEADS = 4
DSA_DIM = 64
IDX_HEADS = 8
IDX_DIM = 32
DSA_TOPK_MAX = 256
RET_HEADS = 4
RET_DK = 64
RET_DV = 64
RET_CHUNK = 128
D_FF_2 = 4 * D_MODEL
EPS = 1e-6

MIX_WIDTH = MLA_HEADS * MLA_V + DSA_HEADS * DSA_DIM + RET_HEADS * RET_DV
MLA_COLS = (MLA_Q_RANK, MLA_KV_RANK, MLA_ROPE)
DSA_COLS = (DSA_HEADS * DSA_DIM, DSA_DIM, DSA_DIM, IDX_HEADS * IDX_DIM, IDX_DIM, IDX_HEADS)
RET_COLS = (RET_HEADS * RET_DK, RET_HEADS * RET_DK, RET_HEADS * RET_DV, RET_HEADS * RET_DV)
SPLITS = MLA_COLS + DSA_COLS + RET_COLS
IN_WIDTH = sum(SPLITS)


def rmsnorm(x, g):
    xf = x.astype(jnp.float32)
    y = xf * lax.rsqrt(jnp.mean(xf * xf, axis=-1, keepdims=True) + EPS)
    return (y * g.astype(jnp.float32)).astype(x.dtype)

def rope_tables(seq, dim):
    pos = jnp.arange(seq, dtype=jnp.float32)
    inv = ROPE_THETA ** (-jnp.arange(0, dim, 2, dtype=jnp.float32) / dim)
    ang = pos[:, None] * inv[None, :]
    return jnp.cos(ang), jnp.sin(ang)

def apply_rope(x, cos, sin):
    d2 = x.shape[-1] // 2
    x1, x2 = x[..., :d2], x[..., d2:]
    c = cos[:, None, :].astype(x.dtype)
    s = sin[:, None, :].astype(x.dtype)
    return jnp.concatenate([x1 * c - x2 * s, x1 * s + x2 * c], axis=-1)

def to_blocks(t):
    b, s = t.shape[0], t.shape[1]
    return t.reshape((b, s // Q_BLOCK, Q_BLOCK) + t.shape[2:]).swapaxes(0, 1)

def from_blocks(t):
    t = t.swapaxes(0, 1)
    return t.reshape(t.shape[0], t.shape[1] * t.shape[2], -1)

def mla_attention(q_nope, q_rope, k_nope, k_rope, v):
    S = q_nope.shape[1]
    nb = S // Q_BLOCK
    scale = (MLA_NOPE + MLA_ROPE) ** -0.5
    key_pos = jnp.arange(S)
    neg = jnp.finfo(jnp.float32).min

    def block(args):
        qn, qr, start = args
        s = jnp.einsum('bqhd,bkhd->bhqk', qn, k_nope) + jnp.einsum('bqhd,bkd->bhqk', qr, k_rope)
        s = s.astype(jnp.float32) * scale
        qpos = start + jnp.arange(Q_BLOCK)
        causal = key_pos[None, :] <= qpos[:, None]
        p = jax.nn.softmax(jnp.where(causal, s, neg), axis=-1).astype(v.dtype)
        return jnp.einsum('bhqk,bkhd->bqhd', p, v)

    starts = jnp.arange(nb, dtype=jnp.int32) * Q_BLOCK
    out = lax.map(block, (to_blocks(q_nope), to_blocks(q_rope), starts))
    return from_blocks(out)

def dsa_attention(q, k, v, q_idx, k_idx, w_idx, topk):
    S = q.shape[1]
    nb = S // Q_BLOCK
    scale = DSA_DIM ** -0.5
    key_pos = jnp.arange(S)
    neg = jnp.finfo(jnp.float32).min
    gather = jax.vmap(lambda table, idx: table[idx])

    def block(args):
        qb, qib, wb, start = args
        qpos = start + jnp.arange(Q_BLOCK)
        causal = key_pos[None, :] <= qpos[:, None]
        rel = jax.nn.relu(jnp.einsum('bqhd,bkd->bqhk', qib, k_idx))
        score = jnp.einsum('bqh,bqhk->bqk', wb, rel).astype(jnp.float32)
        score = jnp.where(causal[None], score, -jnp.inf)
        _, sel = lax.top_k(score, topk)
        valid = sel <= qpos[None, :, None]
        k_sel = gather(k, sel)
        v_sel = gather(v, sel)
        s = jnp.einsum('bqhd,bqjd->bhqj', qb, k_sel).astype(jnp.float32) * scale
        p = jax.nn.softmax(jnp.where(valid[:, None], s, neg), axis=-1).astype(v.dtype)
        return jnp.einsum('bhqj,bqjd->bqhd', p, v_sel)

    starts = jnp.arange(nb, dtype=jnp.int32) * Q_BLOCK
    out = lax.map(block, (to_blocks(q), to_blocks(q_idx), to_blocks(w_idx), starts))
    return from_blocks(out)

def retention(q, k, v, log_gamma):
    B, S, H, dk = q.shape
    dv = v.shape[-1]
    C = RET_CHUNK
    n = S // C
    qc = q.astype(jnp.float32).reshape(B, n, C, H, dk)
    kc = k.astype(jnp.float32).reshape(B, n, C, H, dk)
    vc = v.astype(jnp.float32).reshape(B, n, C, H, dv)
    pos = jnp.arange(C, dtype=jnp.float32)
    rel = pos[:, None] - pos[None, :]
    decay = jnp.where(rel[None] >= 0, jnp.exp(jnp.maximum(rel, 0.0)[None] * log_gamma[:, None, None]), 0.0)
    inner = jnp.einsum('bnqhd,bnchd->bnhqc', qc, kc) * decay[None, None]
    inner_out = jnp.einsum('bnhqc,bnche->bnqhe', inner, vc)
    zeta = jnp.exp((C - 1.0 - pos)[None, :] * log_gamma[:, None])
    chunk_state = jnp.einsum('bnchd,hc,bnche->bnhde', kc, zeta, vc)
    chunk_decay = jnp.exp(C * log_gamma)[None, :, None, None]

    def step(R, s_i):
        return R * chunk_decay + s_i, R

    R0 = jnp.zeros((B, H, dk, dv), jnp.float32)
    _, R_prev = lax.scan(step, R0, chunk_state.swapaxes(0, 1))
    R_prev = R_prev.swapaxes(0, 1)
    xi = jnp.exp((pos + 1.0)[None, :] * log_gamma[:, None])
    cross = jnp.einsum('bnqhd,bnhde,hq->bnqhe', qc, R_prev, xi)
    return (inner_out + cross).reshape(B, S, H, dv)

def head_groupnorm(x, g):
    mu = jnp.mean(x, axis=-1, keepdims=True)
    xc = x - mu
    var = jnp.mean(xc * xc, axis=-1, keepdims=True)
    return xc * lax.rsqrt(var + EPS) * g

def second_inputs(seed: int = 0) -> dict:
    key = jax.random.key(seed)
    ks = jax.random.split(key, 16)

    def nrm(k, shape, scale):
        return jax.random.normal(k, shape, jnp.float32) * scale

    def gain(k, shape):
        return 1.0 + 0.05 * jax.random.normal(k, shape, jnp.float32)

    return {
        'x': nrm(ks[0], (BATCH, SEQ, D_MODEL), 1.0),
        'g_mix': gain(ks[1], (DEPTH_2, D_MODEL)),
        'w_in': nrm(ks[2], (DEPTH_2, D_MODEL, IN_WIDTH), D_MODEL ** -0.5),
        'g_q': gain(ks[3], (DEPTH_2, MLA_Q_RANK)),
        'w_uq': nrm(ks[4], (DEPTH_2, MLA_Q_RANK, MLA_HEADS * (MLA_NOPE + MLA_ROPE)), MLA_Q_RANK ** -0.5),
        'g_kv': gain(ks[5], (DEPTH_2, MLA_KV_RANK)),
        'w_ukv': nrm(ks[6], (DEPTH_2, MLA_KV_RANK, MLA_HEADS * (MLA_NOPE + MLA_V)), MLA_KV_RANK ** -0.5),
        'g_ret': gain(ks[7], (DEPTH_2, RET_HEADS * RET_DV)),
        'w_out': nrm(ks[8], (DEPTH_2, MIX_WIDTH, D_MODEL), MIX_WIDTH ** -0.5),
        'g_mlp': gain(ks[9], (DEPTH_2, D_MODEL)),
        'w_ff1': nrm(ks[10], (DEPTH_2, D_MODEL, D_FF_2), D_MODEL ** -0.5),
        'w_ff2': nrm(ks[11], (DEPTH_2, D_FF_2, D_MODEL), D_FF_2 ** -0.5),
        'g_final': gain(ks[12], (D_MODEL,)),
    }

def second_block(x, g_mix, w_in, g_q, w_uq, g_kv, w_ukv, g_ret, w_out, g_mlp, w_ff1, w_ff2, g_final):
    B, S, _ = x.shape
    topk = min(DSA_TOPK_MAX, S // 4)
    cos_r, sin_r = rope_tables(S, MLA_ROPE)
    cos_a, sin_a = rope_tables(S, DSA_DIM)
    cos_i, sin_i = rope_tables(S, IDX_DIM)
    cos_t, sin_t = rope_tables(S, RET_DK)
    log_gamma = jnp.log1p(-jnp.exp2(-5.0 - jnp.arange(RET_HEADS, dtype=jnp.float32)))
    split_at = np.cumsum(SPLITS)[:-1].tolist()
    idx_scale = (IDX_HEADS ** -0.5) * (IDX_DIM ** -0.5)

    for l in range(DEPTH_2):
        h = rmsnorm(x, g_mix[l])
        (cq, ckv, kr, aq, ak, av, qi, ki, wi, rq, rk, rv, rg) = jnp.split(h @ w_in[l], split_at, axis=-1)

        q = (rmsnorm(cq, g_q[l]) @ w_uq[l]).reshape(B, S, MLA_HEADS, MLA_NOPE + MLA_ROPE)
        q_nope = q[..., :MLA_NOPE]
        q_rope = apply_rope(q[..., MLA_NOPE:], cos_r, sin_r)
        kv = (rmsnorm(ckv, g_kv[l]) @ w_ukv[l]).reshape(B, S, MLA_HEADS, MLA_NOPE + MLA_V)
        k_nope, v_mla = kv[..., :MLA_NOPE], kv[..., MLA_NOPE:]
        k_rope = apply_rope(kr[:, :, None, :], cos_r, sin_r)[:, :, 0]
        o_a = mla_attention(q_nope, q_rope, k_nope, k_rope, v_mla)

        q_b = apply_rope(aq.reshape(B, S, DSA_HEADS, DSA_DIM), cos_a, sin_a)
        k_b = apply_rope(ak[:, :, None, :], cos_a, sin_a)[:, :, 0]
        q_i = apply_rope(qi.reshape(B, S, IDX_HEADS, IDX_DIM), cos_i, sin_i)
        k_i = apply_rope(ki[:, :, None, :], cos_i, sin_i)[:, :, 0]
        o_b = dsa_attention(q_b, k_b, av, q_i, k_i, wi * idx_scale, topk)

        q_c = apply_rope(rq.reshape(B, S, RET_HEADS, RET_DK), cos_t, sin_t)
        k_c = apply_rope(rk.reshape(B, S, RET_HEADS, RET_DK), cos_t, sin_t) * (RET_DK ** -0.5)
        ret = retention(q_c, k_c, rv.reshape(B, S, RET_HEADS, RET_DV), log_gamma)
        ret = head_groupnorm(ret, g_ret[l].reshape(RET_HEADS, RET_DV).astype(jnp.float32))
        o_c = (jax.nn.silu(rg.astype(jnp.float32)) * ret.reshape(B, S, RET_HEADS * RET_DV)).astype(x.dtype)

        x = x + jnp.concatenate([o_a, o_b, o_c], axis=-1) @ w_out[l]

        hf = rmsnorm(x, g_mlp[l])
        x = x + jnp.square(jax.nn.relu(hf @ w_ff1[l])) @ w_ff2[l]

    return rmsnorm(x, g_final)


def setup_inputs(seed=0):
    out = dict(first_inputs(seed))
    for name, value in second_inputs(seed + 1).items():
        if name != "x":
            out[name + "_2"] = value
    return out


def reference(
    x, positions, norm_ffn1, ffn1_gate, ffn1_up, ffn1_down, norm_mix, w_in, cmp_pe_k, cmp_k_w1,
    cmp_k_w2, cmp_pe_v, cmp_v_w1, cmp_v_w2, swa_sinks, w_branch_a, w_branch_b, w_out, norm_ffn2,
    ffn2_gate, ffn2_up, ffn2_down, norm_final, g_mix_2, w_in_2, g_q_2, w_uq_2, g_kv_2, w_ukv_2,
    g_ret_2, w_out_2, g_mlp_2, w_ff1_2, w_ff2_2, g_final_2,
):
    x = first_block(
        x, positions, norm_ffn1, ffn1_gate, ffn1_up, ffn1_down, norm_mix, w_in, cmp_pe_k,
        cmp_k_w1, cmp_k_w2, cmp_pe_v, cmp_v_w1, cmp_v_w2, swa_sinks, w_branch_a, w_branch_b,
        w_out, norm_ffn2, ffn2_gate, ffn2_up, ffn2_down, norm_final,
    )
    return second_block(
        x, g_mix_2, w_in_2, g_q_2, w_uq_2, g_kv_2, w_ukv_2, g_ret_2, w_out_2, g_mlp_2, w_ff1_2,
        w_ff2_2, g_final_2,
    )


_drawn_inputs = setup_inputs


def setup_inputs(seed=0):
    import zlib

    import numpy as np

    out = dict(_drawn_inputs(seed))
    spreads = {}
    factors = {'norm_ffn1': 3.27,
     'norm_mix': 4.522,
     'cmp_pe_k': 6.981,
     'swa_sinks': 3.746,
     'norm_ffn2': 3.803,
     'g_q_2': 6.716,
     'g_kv_2': 3.404,
     'g_ret_2': 2.904}
    for name, (base, spread) in spreads.items():
        noise = np.random.default_rng([zlib.crc32(name.encode()), seed]).standard_normal(out[name].shape)
        drawn = base * np.exp(spread * noise) if base else spread * noise
        out[name] = jnp.asarray(drawn.astype(out[name].dtype))
    for name, factor in factors.items():
        out[name] = (out[name] * factor).astype(out[name].dtype)
    return out
```

```python
import numpy as np
import concourse.bass as bass
from concourse import mybir
from contextlib import ExitStack

P = 128
T = 256
NT = T // P
D = 1024
KD = D // P
HD = 64
RING = 3
BODY = 6
SPLIT = 3
SLAB = 2048
FF1 = 2816 // T
FF2 = 4096 // T
NCMP = T // 16 - 1
CP = 16
NEG = -1e30
TAKEN = -3e38
MLA_Q = 96
EPS = 1e-6
PI = float(np.pi)
PI_LOW = 3.1415925
TWO_PI_1 = 6.28125
TWO_PI_2 = float(np.float32(2 * np.pi - 6.28125))
TWO_PI_3 = float(2 * np.pi - 6.28125 - float(np.float32(2 * np.pi - 6.28125)))
ROUND = 12582912.0
TOPK = 64
TOP_ROUNDS = TOPK // 8

GAINS = [("norm_ffn1", 8), ("norm_mix", 8), ("norm_ffn2", 8), ("norm_final", 8), ("g_mix_2", 16),
         ("g_mlp_2", 16), ("g_final_2", 8), ("g_q_2", 12), ("g_kv_2", 4), ("cmp_pe_k", 16), ("cmp_pe_v", 16)]
GROW, _at = {}, 0
for _name, _n in GAINS:
    GROW[_name] = _at
    _at += _n
NGAIN = _at

CONST1 = [("ident", 128), ("perm64", 128), ("perm32", 128), ("perm96", 128), ("inv64", 1), ("blk", 8),
          ("causal", 256), ("band", 256), ("cmp_mask", 256), ("cmp_vis", 256), ("cos_a", 256), ("sin_a", 256)]
CONST2 = [("decay", 1024), ("cos_i", 256), ("sin_i", 256), ("cos_m", 256), ("sin_m", 256)]


def columns(table):
    out, at = {}, 0
    for name, n in table:
        out[name] = (at, n)
        at += n
    return out, at


C1, NC1 = columns(CONST1)
C2, NC2 = columns(CONST2)


def constants():
    c1, c2 = np.zeros((P, NC1), np.float32), np.zeros((P, NC2), np.float32)

    def put(name, value):
        where, (at, n) = (c1, C1[name]) if name in C1 else (c2, C2[name])
        where[:value.shape[0], at:at + n] = value

    def perm(half, first=0):
        m = np.zeros((P, P), np.float32)
        for c in range(first, P):
            if (c // half) % 2 == 0:
                m[c + half, c] = -1.0
            else:
                m[c - half, c] = 1.0
        return m

    put("ident", np.eye(P, dtype=np.float32))
    put("perm64", perm(32))
    put("perm32", perm(16))
    put("perm96", perm(16, 64))

    def inv(half):
        return (10000.0 ** (-(np.arange(half, dtype=np.float32) / np.float32(half))).astype(np.float64)).astype(np.float32)

    def angles(half, rows):
        return (np.arange(T, dtype=np.float32)[None, :] * inv(half)[rows % half][:, None]).astype(np.float64)

    rows = np.arange(P)
    put("inv64", inv(32)[rows % 32][:, None])
    put("blk", (rows[:, None] // CP == np.arange(8)[None, :]).astype(np.float32))
    q, k = np.arange(P)[:, None], np.arange(P)[None, :]
    causal = np.where(k <= q, 0.0, NEG)
    put("causal", np.concatenate([np.zeros((P, P)), causal], 1))
    put("band", np.concatenate([np.where(k > q, 0.0, NEG), causal], 1))
    c = np.arange(P)[None, :] % CP
    seen = [(c < NCMP) & (c * 16 + 31 <= q + t * P) for t in range(NT)]
    put("cmp_mask", np.concatenate([np.where(s, 0.0, NEG) for s in seen], 1))
    put("cmp_vis", np.concatenate([s.astype(np.float32) for s in seen], 1))
    put("cos_a", np.cos(angles(32, rows)))
    put("sin_a", np.sin(angles(32, rows)))
    put("cos_i", np.cos(angles(16, rows)))
    put("sin_i", np.sin(angles(16, rows)))
    turned = (rows >= 64)[:, None]
    put("cos_m", np.where(turned, np.cos(angles(16, rows)), 1.0))
    put("sin_m", np.where(turned, np.sin(angles(16, rows)), 0.0))
    gamma = np.log1p(-np.exp2(-5.0 - np.arange(4)))
    rel = q.T - k.T
    decay = [np.concatenate([np.where(rel >= 0, np.exp(np.maximum(rel, 0) * g), 0.0), np.exp((rel + P) * g)], 1)
             for g in gamma]
    put("decay", np.concatenate(decay, 1))
    return c1, c2


def schedule():
    S = [("gains",)] + [("x", b) for b in range(4)]
    S += [("norm", 0), ("ffn1", 0), ("norm", 1)]
    S += [("proj", 0, "kcvc"), ("proj", 0, "misc"), ("proj", 0, "ksl"), ("rope", 0, "sk"), ("proj", 0, "kwn"),
          ("proj", 0, "nq0"), ("rope", 0, "k"), ("proj", 0, "nq1"), ("rope", 0, "nq0"), ("proj", 0, "sq0"),
          ("rope", 0, "nq1"), ("proj", 0, "sq1"), ("rope", 0, "sq0"), ("rope", 0, "sq1")]
    fill = [("cmp1", "k"), ("cmp1", "v")] + [("gate", n) for n in range(8)]
    after = {("cmp1", "k"): [("cmp2", "k")], ("cmp1", "v"): [("cmp2", "v"), ("rope", 0, "kc")]}
    S += attention(0, [("slc", 0), ("slc", 1), ("win", 0), ("win", 1), ("swa", 0), ("swa", 1)], fill, after, 2)
    S += [("cs", 0), ("cs", 1), ("ct", 0), ("ct", 1), ("o", 0, "cmp", 0), ("o", 0, "cmp", 1)]
    S += [("ot", "a", 0), ("ot", "a", 1), ("ot", "b", 0), ("ot", "b", 1), ("branch",)]
    S += [("wout", 0, n) for n in range(4)]
    S += [("norm", 2), ("ffn1", 1), ("norm", 3)]
    for l in (1, 2):
        S += [("norm", 2 + 2 * l), ("proj", l, "misc"), ("proj", l, "qi"), ("rope", l, "ki"), ("rope", l, "ak"),
              ("proj", l, "aq"), ("rope", l, "qi"), ("proj", l, "rk"), ("idx", l, 0), ("rope", l, "aq"), ("idx", l, 1),
              ("proj", l, "rq"), ("idx", l, 2), ("idx", l, 3), ("proj", l, "rv"), ("idx", l, 4), ("idx", l, 5),
              ("rope", l, "rk"), ("idx", l, 6), ("idx", l, 7), ("topk", l, 0, 0, 8), ("proj", l, "rg"), ("rope", l, "rq"),
              ("topk", l, 1, 0, 2), ("proj", l, "cq0"), ("topk", l, 1, 2, 4), ("rope", l, "kr"),
              ("proj", l, "cq1"), ("topk", l, 1, 4, 6), ("proj", l, "cq2"), ("topk", l, 1, 6, 8),
              ("proj", l, "ckv")]
        S += [("rank", l), ("ret", l, 0), ("ret", l, 1), ("ret", l, 2), ("retv", l)]
        S += attention(l, [("dsa", 0), ("dsa", 1)], [], {}, 2)
        S += [("uq", l, 0), ("uq", l, 1), ("rope", l, "uq0"), ("uq", l, 2), ("rope", l, "uq1"), ("uq", l, 3),
              ("rope", l, "uq2"), ("ukv", l), ("rope", l, "uq3")]
        S += attention(l, [("mla", 0), ("mla", 1)], [], {}, 2)
        S += [("mixt", l, 0), ("mixt", l, 1)] + [("wout", l, n) for n in range(4)]
        S += [("norm", 3 + 2 * l), ("ffn2", l)]
    S += [("norm", 8)] + [("y", t, h) for t in range(NT) for h in range(2)]
    return S


HEADS = {"slc": 8, "win": 8, "swa": 8, "dsa": 4, "mla": 8}


def groups(a, t):
    per = 4 if t == 0 else 2
    order = list(range(HEADS[a]))
    if a in ("swa", "dsa"):
        order = order[::2] + order[1::2]
    return [order[g:g + per] for g in range(0, HEADS[a], per)]


def attention(l, tiles, fill, after, every):
    jobs = [(a, t, g) for a, t in tiles for g in range(len(groups(a, t)))]
    last = {(a, t): len(groups(a, t)) - 1 for a, t in tiles}
    fill = list(fill)
    S = [("s", l) + j for j in jobs[:2]]
    for n, job in enumerate(jobs):
        if n + 2 < len(jobs):
            S.append(("s", l) + jobs[n + 2])
        if fill and n % every == 0:
            S.append(fill[0])
            S += after.get(fill.pop(0), [])
        S.append(("t", l) + job)
        if n:
            S.append(("pv", l) + jobs[n - 1])
            if jobs[n - 1][2] == last[jobs[n - 1][:2]]:
                S.append(("o", l) + jobs[n - 1][:2])
        if fill and n % every == 1:
            S.append(fill[0])
            S += after.get(fill.pop(0), [])
    S += [("pv", l) + jobs[-1], ("o", l) + jobs[-1][:2]]
    for f in fill:
        S += [f] + after.get(f, [])
    return S


PROJ = {(0, "kcvc"): [(512, 256)], (0, "misc"): [(1816, 128), (1280, 24)], (0, "ksl"): [(768, 256)],
        (0, "kwn"): [(1024, 256)], (0, "nq0"): [(0, 64), (256, 64), (64, 64), (320, 64)],
        (0, "nq1"): [(128, 64), (384, 64), (192, 64), (448, 64)],
        (0, "sq0"): [(1304, 256)], (0, "sq1"): [(1560, 256)],
        "misc": [(1312, 64), (1696, 32), (1376, 64), (1728, 8), (1024, 32)], "qi": [(1440, 256)], "aq": [(1056, 256)],
        "rk": [(1992, 256)], "rq": [(1736, 256)], "rv": [(2248, 256)], "rg": [(2504, 256)],
        "cq0": [(0, 256)], "cq1": [(256, 256)], "cq2": [(512, 256)], "ckv": [(768, 256)]}


def pieces(l, name):
    return PROJ[(0, name)] if l == 0 else PROJ[name]


NORM_GAIN = [("norm_ffn1", 0), ("norm_mix", 0), ("norm_ffn2", 0), ("norm_final", 0), ("g_mix_2", 0), ("g_mlp_2", 0),
             ("g_mix_2", 8), ("g_mlp_2", 8), ("g_final_2", 0)]


def two_blocks(nc, A, const1, const2, out):
    f32, f32r, bf16, i32 = mybir.dt.float32, mybir.dt.float32r, mybir.dt.bfloat16, mybir.dt.int32
    ALU, ACT, AX = mybir.AluOpType, mybir.ActivationFunctionType, mybir.AxisListType
    STEPS = schedule()
    ctx = ExitStack()
    with ctx:
        def sb(name, shape, dt=f32):
            return ctx.enter_context(nc.sbuf_tensor(name, shape, dt))

        def sem(name):
            return ctx.enter_context(nc.semaphore(name))

        raw = sb("raw", [P, RING, SLAB])
        w_hi, w_lo = sb("w_hi", [P, SPLIT, SLAB], f32r), sb("w_lo", [P, SPLIT, SLAB], f32r)
        hT = sb("hT", [P, KD, T])
        n_hi, n_lo = sb("n_hi", [P, KD, T], f32r), sb("n_lo", [P, KD, T], f32r)
        work = sb("work", [P, KD, T])
        hid_hi, hid_lo = sb("hid_hi", [P, 3, 512], f32r), sb("hid_lo", [P, 3, 512], f32r)
        cst = sb("cst", [P, NC1])
        masks = sb("masks", [P, 3 * 256], bf16)
        identb, zerob = sb("identb", [P, P], bf16), sb("zerob", [P, 512], bf16)
        ones = sb("ones", [P, P])
        gains = sb("gains", [P, NGAIN])
        cos_p, sin_p = sb("cos_p", [P, T]), sb("sin_p", [P, T])
        gret = sb("gret", [P, 2, T])
        sink, nsink = sb("sink", [P, 8]), sb("nsink", [P, 8])
        xs = sb("xs", [P, 2, 512])
        xs1 = sb("xs1", [P, 1, T])
        turn_c, turn_s = sb("turn_c", [P, 2, 512]), sb("turn_s", [P, 512])
        probs, probsT = sb("probs", [P, 3, 512]), sb("probsT", [P, 2, 512])
        negm, dsink, esink = sb("negm", [P, 3, 8]), sb("dsink", [P, 2, 8]), sb("esink", [P, 2, 8])
        rsum, coef, rinv8 = sb("rsum", [P, 8, 2, 8]), sb("coef", [P, 8]), sb("rinv8", [P, 8])
        gates = sb("gates", [P, NT, 24])
        std = sb("std", [P, 2, T])
        rstd = std
        m8, cneg, gn = sb("m8", [P, 8]), sb("cneg", [P, 2, 8]), sb("gn", [P, 4, 8])
        cmp_w2k, cmp_w2v = sb("cmp_w2k", [P, 2, 2, HD]), sb("cmp_w2v", [P, 2, HD])
        bias1 = sb("bias1", [P, 2])
        gkT = sb("gkT", [P, 2, 2, CP])
        gvT = sb("gvT", [P, 2, 2, 4, CP])
        kcR = sb("kcR", [P, 2, CP])
        xpe_hi, xpe_lo = hid_hi[:, 0:2, 0:480], hid_lo[:, 0:2, 0:480]
        scr = sb("scr", [P, 9728])

        def region(at, *shape):
            n = int(np.prod(shape))
            ap = scr[:, at:at + n]
            if len(shape) == 2:
                ap = ap.rearrange("p (a b) -> p a b", a=shape[0])
            if len(shape) == 3:
                ap = ap.rearrange("p (a b c) -> p a b c", a=shape[0], b=shape[1])
            return ap

        sig_gate = region(0, 16, T)
        sq = region(0, KD, T)
        qm = region(0, 8, T)
        tables = scr[:, 2048:4096]
        nqT, sqT = region(4096, 4, T), region(5120, 4, T)
        kT, skT = region(6144, 2, T), region(6656, 1, T)
        vsl, vwn, svt = region(6912, 2, P), region(7168, 2, P), region(7424, 2, HD)
        o_sum = region(7552, 2, NT, 512)
        silu_sb, hid = region(4096, 512), region(4608, 3, 512)
        qiT, kiT = region(4096, 2, T), region(4608, 1, T)
        aqT, akT = region(4864, 2, T), region(5376, 1, T)
        kfull = region(4096, 8, T)
        rqT, rkT = region(6144, 2, T), region(6656, 2, T)
        vm = region(6144, 2, 512)
        avt, wit = region(7168, 2, HD), region(7296, 2, 8)
        krR = region(7312, 1, T)
        mix = region(7568, 2, D)
        rvt = sb("rvt", [P, 2, T])
        rgt = sb("rgt", [P, 2, T])
        o_tmp = turn_s
        selb = sb("selb", [P, NT, T], bf16)
        score = probsT
        wflat = work[:, :, :].rearrange("p a b -> p (a b)")
        x2 = wflat[:, 0:1024].rearrange("p (v g t) -> p v g t", v=2, g=2)[:, :, :, :]
        xpe = wflat[:, 1024:1024 + 480]
        vblk = wflat[:, 1536:2048]
        xin = wflat.rearrange("p (t f) -> p t f", t=NT)
        yout = raw[:, 0, :].rearrange("p (t f) -> p t f", t=NT)
        gain_rows = scr[:, 0:128]
        cmp_e = turn_c[:, 0, 0:256].rearrange("p (t c) -> p t c", t=2)
        cmp_p = turn_c[:, 1, 0:256].rearrange("p (t c) -> p t c", t=2)
        pos_i = scr[:, 4096:4096 + T].bitcast(i32)
        ang, red = scr[:, 4352:4608], scr[:, 4608:4864]
        turns = scr[:, 4864:5120]

        def con(name, rows=P):
            if name in C1:
                at, n = C1[name]
                return cst[0:rows, at:at + n]
            at, n = C2[name]
            return tables[0:rows, at:at + n]

        decay = con("decay").rearrange("p (h b q) -> p h b q", h=4, b=2)
        bank = [ctx.enter_context(nc.psum_tensor(f"bank{i}", [P, 512], f32)) for i in range(8)]
        acc = bank[0:4]

        raw_ready = [sem(f"raw_ready{i}") for i in range(RING)]
        hi_ready, lo_ready = sem("hi_ready"), sem("lo_ready")
        slab_done = sem("slab_done")
        bank_ready = [sem(f"bank_ready{i}") for i in range(8)]
        bank_free = [sem(f"bank_free{i}") for i in range(8)]
        consts_in, x_in, small_in = sem("consts_in"), sem("x_in"), sem("small_in")
        setup = sem("setup")
        pool_setup = sem("pool_setup")
        trig, tables_in = sem("trig"), sem("tables_in")
        h_ready = sem("h_ready")
        sq_ready = sem("sq_ready")
        norm_f, norm_h, norm_l = sem("norm_f"), sem("norm_h"), sem("norm_l")
        hid_ready, hidh_ready, hidl_ready = sem("hid_ready"), sem("hidh_ready"), sem("hidl_ready")
        turnc_ready, rope_done = sem("turnc_ready"), sem("rope_done")
        negm_ready, pv_done, o_free = sem("negm_ready"), sem("pv_done"), sem("o_free")
        xpe_ready, xpeh_ready, xpel_ready = sem("xpe_ready"), sem("xpeh_ready"), sem("xpel_ready")
        cs_ready, cexp_ready, cp_ready = sem("cs_ready"), sem("cexp_ready"), sem("cp_ready")
        merged = sem("merged")
        dve_step = sem("dve_step")
        act_step = sem("act_step")
        sel_ready, ret_ready, retv_done = sem("sel_ready"), sem("ret_ready"), sem("retv_done")
        kr_done = sem("kr_done")
        rows_done = sem("rows_done")
        oc_ready, ot_hi, ot_lo = sem("oc_ready"), sem("ot_hi"), sem("ot_lo")
        y_ready, y_out = sem("y_ready"), [sem("y_out0"), sem("y_out1")]

        slabs, SL = [], {}
        RAWC, _fill = [], [0] * RING

        def slab(key, loads=1):
            s = len(slabs)
            SL[key] = s
            slabs.append(key)
            _fill[s % RING] += 16 * loads
            RAWC.append(_fill[s % RING])

        JOB = {}
        READY = {}
        _use, _free, _next = [0] * 8, [0] * 8, [0]
        LASTFREE = {}

        SPECIAL = {}

        def job(key, b=None, freed_by=None, of_slab=False):
            if b is None:
                b = 4 + _next[0] % 4
                _next[0] += 1
            if of_slab:
                READY[key] = (slab_done, len(slabs))
            else:
                _use[b] += 1
                READY[key] = (bank_ready[b], _use[b])
            JOB[key] = (b, _free[b])
            if b in LASTFREE:
                SPECIAL[key] = LASTFREE.pop(b)
            if freed_by is None:
                _free[b] += 1
            else:
                LASTFREE[b] = freed_by

        XSC, RO, BUFUSE = {}, {}, {}
        ATT, PVN, ON = {}, {}, {}
        _att, _o = [0], [0]
        hcount = [0]
        HN = {}
        NB, nf, nh, nstd = {}, [0], [0], [0]
        OT, ohi, nact = {}, [0], [0]
        FF = {}
        _ao = [0]

        BEFORE = {}

        def bring(key, units, buf):
            BEFORE[key] = BUFUSE.get(buf, [])
            for u in units:
                XSC[u] = (key, buf)
            BUFUSE[buf] = list(units)

        for st in STEPS:
            kind = st[0]
            if kind == "x":
                job(st, freed_by=("h_ready", st[1] + 1))
            elif kind == "gains":
                job(st)
            elif kind == "norm":
                HN[st[1]] = hcount[0]
                hcount[0] += 4
                job(st)
                NB[st] = (nf[0], nh[0], nstd[0])
                nstd[0] += 1
                if st[1] != 3:
                    nf[0] += 8
                if st[1] not in (3, 8):
                    nh[0] += 8
            elif kind == "ffn1":
                f = st[1]
                FF[st] = (nact[0], len(FF))
                nact[0] += FF1
                for i in range(FF1 + 1):
                    if i < FF1:
                        slab(("g", f, i))
                        job(("g", f, i), of_slab=True)
                        slab(("u", f, i))
                        job(("u", f, i), of_slab=True)
                    if i:
                        slab(("d", f, i - 1))
            elif kind == "ffn2":
                l = st[1]
                FF[st] = (nact[0], len(FF))
                nact[0] += FF2
                for i in range(FF2 + 1):
                    if i < FF2:
                        slab(("f", l, i))
                        job(("f", l, i), 4 + i % 3, of_slab=True)
                    if i:
                        slab(("e", l, i - 1))
            elif kind == "proj":
                _, l, name = st
                slab(st, len(pieces(l, name)))
                job(st, of_slab=(l == 0 or name != "misc"))
                if name == "misc":
                    if l:
                        job(st + ("b",), of_slab=True)
                        bring(st, [(l, "ak"), (l, "ki")], 0)
                        bring(st + ("b",), [(l, "kr")], 2)
                        XSC[(l, "kr")] = (st, 2)
                    else:
                        bring(st, [(0, "sk")], 2)
                elif name == "kwn":
                    bring(st, [(0, "k")], 0)
                elif name in ("nq0", "nq1", "sq0", "sq1"):
                    bring(st, [(0, name)], {"nq0": 1, "nq1": 0, "sq0": 1, "sq1": 0}[name])
                elif name in ("qi", "aq", "rk", "rq"):
                    bring(st, [(l, name)], {"qi": 1, "aq": 0, "rk": 1, "rq": 0}[name])
            elif kind == "uq":
                _, l, n = st
                slab(st)
                job(st, of_slab=True)
                bring(st, [(l, f"uq{n}")], (n + 1) % 2)
            elif kind == "ukv":
                slab(st)
                for n in range(6):
                    job(st + (n,), of_slab=(n == 5))
            elif kind == "rope":
                RO[st[1:]] = len(RO)
                job(st)
            elif kind == "cmp1":
                slab(st + (0,))
                slab(st + (1,))
                job(st, of_slab=True)
            elif kind == "cmp2":
                job(st)
                if st[1] == "k":
                    bring(st, [(0, "kc")], 2)
            elif kind == "gate":
                slab(st)
                job(st, of_slab=True)
            elif kind == "s":
                ATT[st[1:]] = _att[0]
                _att[0] += 1
                job(st)
            elif kind == "t":
                job(st)
            elif kind == "pv":
                PVN[st[1:]] = len(PVN)
                if (st[1], st[2], st[3]) not in ON:
                    ON[st[1:4]] = [_o[0], 0]
                    _o[0] += 1
                ON[st[1:4]][1] = len(PVN)
            elif kind in ("cs", "ct"):
                job(st)
                if kind == "ct":
                    PVN[(0, "cmp", st[1], 0)] = len(PVN)
                    ON[(0, "cmp", st[1])] = [_o[0], len(PVN)]
                    _o[0] += 1
            elif kind in ("ot", "idx", "ret"):
                job(st)
                if kind == "ot":
                    OT[st] = ohi[0]
                    ohi[0] += 1
            elif kind == "retv":
                ON[(st[1], "ret")] = [_o[0], 0]
                _o[0] += 1
            elif kind == "rank":
                job(st + ("q",))
                job(st + ("kv",))
                NB[st] = (nf[0], nh[0], nstd[0])
                nf[0], nh[0], nstd[0] = nf[0] + 8, nh[0] + 8, nstd[0] + 2
            elif kind == "branch":
                for key in ("wa", "wb"):
                    slab((key, 0))
                    slab((key, 1))
                for b in range(4):
                    job(("wb", b), of_slab=True)
                OT[st] = ohi[0]
                ohi[0] += 4
            elif kind == "wout":
                slab(st)
                job(st, freed_by=("h_ready", hcount[0] + st[2] + 1), of_slab=True)
            elif kind == "mixt":
                for b in range(2):
                    job(st + (b,))
                    OT[st + (b,)] = ohi[0]
                    ohi[0] += 1
            elif kind == "y":
                job(st)
        NSLAB = len(slabs)
        ATTLIST = sorted(ATT, key=ATT.get)
        IDX = [(t, [j, j + 4]) for t in range(NT) for j in range(4)]
        FFSQ = {("ffn2", 1): 0, ("ffn2", 2): FF2}
        BYNAME = {"h_ready": h_ready}

        def take(pe, key):
            b, frees = JOB[key]
            if frees:
                pe.wait_ge(bank_free[b], frees)
            if key in SPECIAL:
                pe.wait_ge(BYNAME[SPECIAL[key][0]], SPECIAL[key][1])
            return bank[b]

        def filled(key):
            return READY[key][0]

        def await_bank(eng, key):
            eng.wait_ge(*READY[key])
            return bank[JOB[key][0]]

        def freed(key):
            return bank_free[JOB[key][0]]

        def free_count(key):
            b, frees = JOB[key]
            return bank_free[b], frees + 1

        def wh(s):
            return w_hi[:, s % SPLIT, :]

        def wl(s):
            return w_lo[:, s % SPLIT, :]

        def halves(ap):
            return ap.rearrange("p (a t) -> p a t", a=2)

        def split_jobs(st):
            if st[0] == "ot":
                return [(st, 0 if st[1] == "a" else 4, st[2])]
            return [(st + (b,), 4 * b, st[2]) for b in range(2)]

        def rotation(l, name):
            buf = XSC[(l, name)][1]
            src = xs1 if buf == 2 else xs[:, buf, :].rearrange("p (a t) -> p a t", a=2)
            c64 = (cos_p[:, :], sin_p[:, :]) if l == 0 else (con("cos_a"), con("sin_a"))
            c32 = (con("cos_i"), con("sin_i"))
            c96 = (con("cos_m"), con("sin_m"))
            pick = {"sk": (src, 1, P, "perm64", c64, skT), "kc": (src, 1, P, "perm64", c64, kcR), "k": (src, 2, P, "perm64", c64, kT),
                    "nq0": (src, 2, P, "perm64", c64, nqT[:, 0:2]), "nq1": (src, 2, P, "perm64", c64, nqT[:, 2:4]),
                    "sq0": (src, 2, P, "perm64", c64, sqT[:, 0:2]), "sq1": (src, 2, P, "perm64", c64, sqT[:, 2:4]),
                    "ak": (src[:, 0:1], 1, P, "perm64", c64, akT), "ki": (src[:, 1:2] if buf != 2 else src, 1, P, "perm32", c32, kiT),
                    "qi": (src, 2, P, "perm32", c32, qiT), "aq": (src, 2, P, "perm64", c64, aqT),
                    "rk": (src, 2, P, "perm64", c64, rkT), "rq": (src, 2, P, "perm64", c64, rqT),
                    "kr": (src, 1, MLA_Q, "perm96", c96, krR)}
            if name.startswith("uq"):
                n = int(name[2])
                return src[0:MLA_Q], 2, MLA_Q, con("perm96")[0:MLA_Q, 0:MLA_Q], (c96[0][0:MLA_Q], c96[1][0:MLA_Q]), qm[0:MLA_Q, 2 * n:2 * n + 2]
            a, n, rows, perm, tab, dst = pick[name]
            return a[0:rows], n, rows, con(perm)[0:rows, 0:rows], (tab[0][0:rows], tab[1][0:rows]), dst[0:rows]

        def operands(l, a, t, h):
            tok = slice(t * P, t * P + P)
            if a in ("slc", "win"):
                r = slice(64 * (h // 4), 64 * (h // 4) + 64)
                return nqT[r, h % 4, tok], kT[r, 0 if a == "slc" else 1, :]
            if a == "swa":
                r = slice(64 * (h % 2), 64 * (h % 2) + 64)
                return sqT[r, h // 2, tok], skT[r, 0, :]
            if a == "dsa":
                r = slice(64 * (h % 2), 64 * (h % 2) + 64)
                return aqT[r, h // 2, tok], akT[r, 0, :]
            return qm[0:MLA_Q, h, tok], kfull[0:MLA_Q, h, :]

        def values(a, h, blk):
            if a in ("slc", "win"):
                return (vsl if a == "slc" else vwn)[:, blk, 64 * (h // 4):64 * (h // 4) + 64]
            if a == "swa":
                return svt[:, blk, :]
            if a == "dsa":
                return avt[:, blk, :]
            return vm[:, blk, 64 * h:64 * h + 64]

        def mask_of(a, t):
            if a == "dsa":
                return selb[:, t, 0:P * (t + 1)]
            at = 256 if a == "swa" else 0
            return masks[:, at + 128:at + 256] if t == 0 else masks[:, at:at + 256]

        RSLOT = {"slc": 0, "win": 1, "swa": 2, "cmp": 3, "mla": 4, "dsa": 5}
        GATE = {"cmp": 0, "slc": 1, "win": 2}

        def load_slab(sp, s):
            if s >= RING:
                sp.wait_ge(lo_ready, s - RING + 1)
            key, slot = slabs[s], s % RING
            kind = key[0]
            if kind == "proj":
                _, l, name = key
                src = (A["w_in"][0] if l == 0 else A["w_in_2"][l - 1]).rearrange("(k p) c -> p k c", p=P)
                width = sum(n for _, n in pieces(l, name))
                dst = raw[:, slot, 0:KD * width].rearrange("p (k c) -> p k c", k=KD)
                at = 0
                for c0, n in pieces(l, name):
                    sp.dma_start(dst[:, :, at:at + n], src[:, :, c0:c0 + n]).then_inc(raw_ready[slot], 16)
                    at += n
                return
            if kind in ("g", "u", "f"):
                src = cols(key[0], key[1])[key[2]]
            elif kind in ("d", "e"):
                src = rows(key[0], key[1])[key[2]]
            elif kind == "gate":
                c0 = 1944 + 256 * key[1]
                src = A["w_in"][0].rearrange("(k p) c -> p k c", p=P)[:, :, c0:c0 + 256]
            elif kind == "cmp1":
                src = A[f"cmp_{key[1]}_w1"][0].rearrange("(k p) c -> p k c", p=P)[:, 8 * key[2]:8 * key[2] + 8, :]
            elif kind in ("wa", "wb"):
                name = "w_branch_a" if kind == "wa" else "w_branch_b"
                src = A[name][0].rearrange("(i k p) c -> i p k c", p=P, k=2)[key[1]]
            elif kind == "wout":
                w = A["w_out"][0] if key[1] == 0 else A["w_out_2"][key[1] - 1]
                src = w.rearrange("(k p) (n c) -> n p k c", p=P, c=256)[key[2]]
            elif kind == "uq":
                src = A["w_uq_2"][key[1] - 1].rearrange("(k p) c -> p k c", p=P)[:, :, 192 * key[2]:192 * key[2] + 192]
            else:
                src = A["w_ukv_2"][key[1] - 1].rearrange("(k p) c -> p k c", p=P)
            k = src.shape[1]
            dst = raw[:, slot, 0:k * src.shape[2]].rearrange("p (k c) -> p k c", k=k)
            sp.dma_start(dst, src).then_inc(raw_ready[slot], 16)

        def width(s):
            key = slabs[s]
            if key[0] == "proj":
                return KD * sum(n for _, n in pieces(key[1], key[2]))
            return 6 * 192 if key[0] == "uq" else SLAB

        def cols(kind, f):
            w = {"g": lambda: A[f"ffn{f + 1}_gate"][0], "u": lambda: A[f"ffn{f + 1}_up"][0],
                 "f": lambda: A["w_ff1_2"][f - 1]}[kind]()
            return w.rearrange("(k p) (i c) -> i p k c", p=P, c=256)

        def rows(kind, f):
            w = A[f"ffn{f + 1}_down"][0] if kind == "d" else A["w_ff2_2"][f - 1]
            return w.rearrange("(i k p) c -> i p k c", p=P, k=2)

        block = ctx.enter_context(nc.Block())

        @block.sync
        def _(sp):
            sp.dma_start(xin, A["x"][0].rearrange("(t p) f -> p t f", p=P)).then_inc(x_in, 16)
            s = 0

            def body(first, it, kinds):
                for j in range(BODY):
                    n = first + j
                    kind, f, i = slabs[n]
                    step = kinds
                    sp.wait_ge(lo_ready, n - RING + 1 + BODY * it)
                    view = (cols if kind in ("g", "u", "f") else rows)(kind, f)
                    src = view[bass.ds(i + step * it, 1)].rearrange("o p k c -> (o p) k c")
                    dst = raw[:, n % RING, :].rearrange("p (k c) -> p k c", k=src.shape[1])
                    sp.dma_start(dst, src).then_inc(raw_ready[n % RING], 16)

            while s < NSLAB:
                kind = slabs[s][0]
                if kind == "g" and slabs[s][2] == 1:
                    bodies = (FF1 - 1) // 2
                    if s < RING:
                        for n in range(s, s + BODY):
                            load_slab(sp, n)
                        s, bodies = s + BODY, bodies - 1
                    with sp.Fori(0, bodies) as it:
                        body(s, it, 2)
                    s += BODY * bodies
                elif kind == "f" and slabs[s][2] == 1:
                    with sp.Fori(0, (FF2 - 1) // 3) as it:
                        body(s, it, 3)
                    s += BODY * ((FF2 - 1) // 3)
                else:
                    if slabs[s] == ("proj", 1, "misc"):
                        sp.wait_ge(merged, 4)
                        sp.dma_start(tables, const2).then_inc(tables_in, 16)
                    load_slab(sp, s)
                    s += 1
            for t in range(NT):
                sp.wait_ge(y_ready, 2 * t + 2)
                sp.dma_start(out[0, t * P:t * P + P, :], yout[:, t, :]).then_inc(y_out[t], 16)
            for t in range(NT):
                sp.wait_ge(y_out[t], 16)

        @block.gpsimd
        def _(pool):
            nc.gpsimd.memset(ones[:, :], 1.0).then_inc(pool_setup, 1)
            nc.gpsimd.memset(zerob[:, :], 0.0).then_inc(pool_setup, 1)
            nc.gpsimd.memset(bias1[:, 0:1], EPS).then_inc(pool_setup, 1)
            nc.gpsimd.memset(bias1[:, 1:2], PI / 2).then_inc(pool_setup, 1)
            nc.gpsimd.memset(gkT[:, :, :, :], 0.0).then_inc(pool_setup, 1)
            nc.gpsimd.memset(gvT[:, :, :, :, :], 0.0).then_inc(pool_setup, 1)
            nc.gpsimd.memset(kcR[:, :, :], 0.0).then_inc(pool_setup, 1)
            nc.gpsimd.memset(rsum[:, :, :, :], 0.0).then_inc(pool_setup, 1)
            for st in STEPS:
                if st[0] == "rope":
                    r = RO[st[1:]]
                    src, n, nrow, _, (cos, _), dst = rotation(*st[1:])
                    pool.wait_ge(*free_count(XSC[st[1:]][0]))
                    if r == 0:
                        pool.wait_ge(trig, 2)
                    if st[1] == 1:
                        pool.wait_ge(tables_in, 16)
                    if r >= 2:
                        pool.wait_ge(rope_done, r - 1)
                    if st[2] == "kc":
                        o = turn_c[:, r % 2, 0:32].rearrange("p (g c) -> p g c", g=2)[:, :, 0:NCMP]
                        i = xs1[:, 0, 0:32].rearrange("p (g c) -> p g c", g=2)[:, :, 0:NCMP]
                        c = cos[:, 31:T:16].unsqueeze(1).to_broadcast([P, 2, NCMP])
                    else:
                        o = turn_c[0:nrow, r % 2, 0:n * T].rearrange("p (a t) -> p a t", a=n)
                        i, c = src, cos.unsqueeze(1).to_broadcast([nrow, n, T])
                    nc.gpsimd.tensor_tensor(o, i, c, ALU.mult).then_inc(turnc_ready, 1)
                    if st[2] == "kr":
                        pool.wait_ge(rope_done, r + 1)
                        pool.wait_ge(pv_done, ON[(st[1], "dsa", 1)][1])
                        nc.gpsimd.tensor_copy(kfull[64:96, :, :], krR[64:96, 0, :].unsqueeze(1).to_broadcast([32, 8, T]))\
                            .then_inc(kr_done, 1)
                        pool.wait_ge(kr_done, st[1])

        @block.scalar
        def _(act):
            act.dma_start(cst[:, :], const1).then_inc(consts_in, 16)
            for name, n in GAINS:
                a = A[name]
                if name.startswith("cmp_pe"):
                    src = a[0].rearrange("(r two) d -> r (two d)", two=2)
                elif len(a.shape) == 1:
                    src = a.rearrange("(r c) -> r c", c=P)
                else:
                    src = a.rearrange("l (r c) -> (l r) c", c=P)
                act.dma_start(gain_rows[GROW[name]:GROW[name] + n, :], src).then_inc(small_in, 16)
            act.dma_start(pos_i, A["positions"][0:1, :].to_broadcast([P, T])).then_inc(small_in, 16)
            act.dma_start(sink[:, :], A["swa_sinks"][0:1, :].to_broadcast([P, 8])).then_inc(small_in, 16)
            for l in range(2):
                act.dma_start(gret[:, l, :], A["g_ret_2"][l:l + 1, :].to_broadcast([P, T])).then_inc(small_in, 16)
            for i in range(2):
                act.dma_start(cmp_w2k[:, :, i, :], A["cmp_k_w2"][0].rearrange("(m p) d -> p m d", p=P)).then_inc(small_in, 16)
            act.dma_start(cmp_w2v[:, :, :], A["cmp_v_w2"][0].rearrange("(m p) d -> p m d", p=P)).then_inc(small_in, 16)

            nxt = [0]

            def split(s, it=0, free=True):
                act.wait_ge(raw_ready[s % RING], RAWC[s] + 16 * (BODY // RING) * it)
                if free:
                    act.wait_ge(slab_done, s - SPLIT + 1 + BODY * it)
                n = width(s)
                nc.scalar.activation(w_hi[:, s % SPLIT, 0:n], raw[:, s % RING, 0:n], ACT.Copy).then_inc(hi_ready, 1)

            def ahead(s):
                while nxt[0] <= min(s + 2, NSLAB - 1):
                    split(nxt[0], free=nxt[0] >= SPLIT)
                    nxt[0] += 1

            def silu(st, i, buf, it=0):
                f = st[1]
                b = JOB[("g", f, i)][0]
                act.wait_ge(slab_done, SL[("g", f, i)] + 1 + BODY * it)
                nc.scalar.activation(silu_sb, bank[b][:, :], ACT.Silu).then_inc(bank_free[b], 1)
                b, frees = JOB[("u", f, i)]
                act.wait_ge(bank_free[b], frees + 1 + it)
                nc.scalar.activation(hid_hi[:, buf, :], hid[:, buf, :], ACT.Copy).then_inc(hidh_ready, 1)

            def relu(st, i, buf, it=0):
                b = JOB[("f", st[1], i)][0]
                act.wait_ge(slab_done, SL[("f", st[1], i)] + 1 + BODY * it)
                nc.scalar.activation(silu_sb, bank[b][:, :], ACT.Relu).then_inc(bank_free[b], 1)
                act.wait_ge(hid_ready, FFSQ[st] + i + 1 + 3 * it)
                nc.scalar.activation(hid_hi[:, buf, :], hid[:, buf, :], ACT.Copy).then_inc(hidh_ready, 1)

            ahead(-1)
            act.wait_ge(pool_setup, 8)
            act.wait_ge(setup, 5)
            nc.scalar.activation(sin_p[:, :], red, ACT.Sin).then_inc(trig, 1)
            nc.scalar.activation(cos_p[:, :], ang, ACT.Sin, bias=bias1[:, 1:2], scale=-1.0).then_inc(trig, 1)

            for st in STEPS:
                kind = st[0]
                if kind == "norm":
                    n = st[1]
                    nf, nh, _ = NB[st]
                    for b in range(4):
                        act.wait_ge(h_ready, HN[n] + b + 1)
                        nc.scalar.activation(sq[:, 2 * b:2 * b + 2, :], hT[:, 2 * b:2 * b + 2, :], ACT.Square).then_inc(sq_ready, 1)
                    pb = await_bank(act, st)
                    nc.scalar.activation(std[:, 0, :], pb[:, 0:T], ACT.Sqrt, bias=bias1[:, 0:1], scale=1.0 / D).then_inc(freed(st), 1)
                    if n not in (3, 8):
                        for k in range(KD):
                            act.wait_ge(norm_f, nf + k + 1)
                            nc.scalar.activation(n_hi[:, k, :], work[:, k, :], ACT.Copy).then_inc(norm_h, 1)
                elif kind == "ffn1":
                    s0 = SL[("g", st[1], 0)]
                    body = 2

                    def turn(first, it):
                        for i in range(first, first + body):
                            s = SL[("g", st[1], i)]
                            split(s, it, free=s > 2)
                            split(s + 1, it)
                            silu(st, i - 1, (i - 1) % 2, it)
                            split(s + 2, it)

                    first, bodies = 1, (FF1 - 1) // body
                    if s0 < RING:
                        turn(first, 0)
                        first, bodies = first + body, bodies - 1
                    with act.Fori(0, bodies) as it:
                        turn(first, it)
                    silu(st, FF1 - 1, (FF1 - 1) % 2)
                    nxt[0] = s0 + 3 * FF1 - 1
                    ahead(s0 + 3 * FF1 - 1)
                elif kind == "ffn2":
                    s0 = SL[("f", st[1], 0)]
                    with act.Fori(0, (FF2 - 1) // 3) as it:
                        for i in range(1, 4):
                            relu(st, i - 1, (i - 1) % 3, it)
                            split(s0 + 2 * i, it)
                            split(s0 + 2 * i + 1, it)
                    relu(st, FF2 - 1, (FF2 - 1) % 3)
                    nxt[0] = s0 + 2 * FF2
                    ahead(s0 + 2 * FF2 - 1)
                elif kind == "proj":
                    _, l, name = st
                    ahead(SL[st])
                    for r in BEFORE.get(st, []):
                        act.wait_ge(rope_done, RO[r] + 1)
                    pb = await_bank(act, st)
                    if name == "kcvc":
                        for v in range(2):
                            for g in range(2):
                                src = pb[64 * g:64 * g + 64, v * T:v * T + T]
                                nc.scalar.activation(x2[0:64, v, g, :], src, ACT.Copy)
                                last = nc.scalar.activation(x2[64:128, v, g, 0:T - 1], src[:, 1:T], ACT.Copy)
                        last.then_inc(freed(st), 1)
                    elif name == "misc" and l == 0:
                        for r in range(0, P, 64):
                            nc.scalar.activation(xs1[r:r + 64, 0, :], pb[0:64, 0:T], ACT.Copy)
                        tok = pb[:, T:T + 176].rearrange("p (t c) -> p t c", t=NT)
                        nc.scalar.activation(svt, tok[:, :, 0:HD], ACT.Copy)
                        nc.scalar.activation(gates[:, :, :], tok[:, :, HD:HD + 24], ACT.Sigmoid).then_inc(freed(st), 1)
                    elif name in ("ksl", "kwn"):
                        half = 0 if name == "ksl" else T
                        nc.scalar.activation(xs[:, 0, half:half + T], pb[:, 0:T], ACT.Copy)
                        nc.scalar.activation(vsl if name == "ksl" else vwn, halves(pb[:, T:2 * T]), ACT.Copy).then_inc(freed(st), 1)
                    elif name == "misc":
                        for r in range(0, P, 64):
                            nc.scalar.activation(xs[r:r + 64, 0, 0:T], pb[0:64, 0:T], ACT.Copy)
                        for r in range(0, P, 32):
                            nc.scalar.activation(xs[r:r + 32, 0, T:2 * T], pb[64:96, 0:T], ACT.Copy)
                        for r in BEFORE[st + ("b",)]:
                            act.wait_ge(rope_done, RO[r] + 1)
                        nc.scalar.activation(xs1[0:MLA_Q, 0, :], pb[0:MLA_Q, T:2 * T], ACT.Copy).then_inc(freed(st), 1)
                        tok_job = st + ("b",)
                        tok = await_bank(act, tok_job)[:, 0:144].rearrange("p (t c) -> p t c", t=NT)
                        nc.scalar.activation(avt, tok[:, :, 0:HD], ACT.Copy)
                        nc.scalar.activation(wit, tok[:, :, HD:HD + 8], ACT.Copy, scale=1.0 / 16).then_inc(freed(tok_job), 1)
                    elif name == "rv":
                        nc.scalar.activation(rvt[:, :, :], halves(pb[:, :]), ACT.Copy).then_inc(freed(st), 1)
                    elif name == "rg":
                        nc.scalar.activation(rgt[:, :, :], halves(pb[:, :]), ACT.Silu).then_inc(freed(st), 1)
                    elif name in ("cq0", "cq1", "cq2", "ckv"):
                        k = 2 * ("cq0", "cq1", "cq2", "ckv").index(name)
                        nc.scalar.activation(work[:, k:k + 2, :], halves(pb[:, :]), ACT.Copy)
                        nc.scalar.activation(sq[:, k:k + 2, :], halves(pb[:, :]), ACT.Square).then_inc(freed(st), 1)
                    else:
                        buf = XSC[(l, name)][1]
                        scale = 0.125 if name in ("nq0", "nq1", "sq0", "sq1", "aq", "rk") else 1.0
                        nc.scalar.activation(xs[:, buf, :], pb[:, :], ACT.Copy, scale=scale).then_inc(freed(st), 1)
                elif kind == "uq":
                    _, l, n = st
                    ahead(SL[st])
                    for r in BEFORE[st]:
                        act.wait_ge(rope_done, RO[r] + 1)
                    pb = await_bank(act, st)
                    buf = XSC[(l, f"uq{n}")][1]
                    nc.scalar.activation(xs[0:MLA_Q, buf, :], pb[0:MLA_Q, :], ACT.Copy, scale=MLA_Q ** -0.5).then_inc(freed(st), 1)
                elif kind == "ukv":
                    ahead(SL[st])
                    for n in range(4):
                        pb = await_bank(act, st + (n,))
                        nc.scalar.activation(kfull[0:64, 2 * n:2 * n + 2, :], halves(pb[0:64, :]), ACT.Copy).then_inc(freed(st + (n,)), 1)
                    for t in range(NT):
                        pb = await_bank(act, st + (4 + t,))
                        nc.scalar.activation(vm[:, t, :], pb[:, :], ACT.Copy).then_inc(freed(st + (4 + t,)), 1)
                elif kind == "cmp1":
                    v = "kv".index(st[1])
                    act.wait_ge(xpe_ready, v + 1)
                    nc.scalar.activation(xpe_hi[:, v, :], xpe, ACT.Copy).then_inc(xpeh_ready, 1)
                    ahead(SL[st + (0,)])
                    ahead(SL[st + (1,)])
                    pb = await_bank(act, st)
                    src = pb[:, 0:60].rearrange("p (m c) -> p m c", m=2)
                    for m in range(2):
                        tile = src[:, m, :].rearrange("p (g c) -> p g c", g=2)
                        if v == 0:
                            last = nc.scalar.activation(gkT[:, m, :, 0:NCMP], tile, ACT.Gelu_apprx_tanh)
                        else:
                            last = nc.scalar.activation(gvT[:, m, :, :, 0:NCMP], tile.unsqueeze(2).to_broadcast([P, 2, 4, NCMP]),
                                                        ACT.Gelu_apprx_tanh)
                    last.then_inc(freed(st), 1)
                elif kind == "cmp2" and st[1] == "k":
                    for r in BEFORE[st]:
                        act.wait_ge(rope_done, RO[r] + 1)
                    pb = await_bank(act, st)
                    nc.scalar.activation(xs1[:, 0, 0:32], pb[:, 0:32], ACT.Copy).then_inc(freed(st), 1)
                elif kind == "gate":
                    n = st[1]
                    ahead(SL[st])
                    pb = await_bank(act, st)
                    nc.scalar.activation(sig_gate[:, 2 * n:2 * n + 2, :], halves(pb[:, :]), ACT.Sigmoid).then_inc(freed(st), 1)
                elif kind == "s":
                    _, l, a, t, g = st
                    q, nk = ATT[st[1:]], P * (t + 1)
                    heads = groups(a, t)[g]
                    buf = q % 3
                    act.wait_ge(negm_ready, q + 1)
                    if q >= 3:
                        await_bank(act, ("t",) + ATTLIST[q - 3])
                    if a == "dsa":
                        act.wait_ge(retv_done, l)
                    pb = bank[JOB[st][0]]
                    if a == "swa":
                        hs = slice(heads[0], heads[-1] + 1, 2)
                        nc.scalar.activation(esink[:, t, hs], dsink[:, t, hs], ACT.Exp)
                    for i, h in enumerate(heads):
                        c = slice(i * nk, i * nk + nk)
                        last = nc.scalar.activation(probs[:, buf, c], pb[:, c], ACT.Exp, bias=negm[:, buf, i:i + 1],
                                                    accum_out=rsum[:, RSLOT[a], t, h:h + 1])
                    last.then_inc(freed(st), 1)
                elif kind == "cs":
                    t = st[1]
                    act.wait_ge(cs_ready, t + 1)
                    nc.scalar.activation(cmp_e[:, t, :], cmp_e[:, t, :], ACT.Exp).then_inc(cexp_ready, 1)
                elif kind == "rank":
                    nf, nh, _ = NB[st]
                    for n, (part, dim) in enumerate((("q", 768), ("kv", 256))):
                        pb = await_bank(act, st + (part,))
                        nc.scalar.activation(std[:, n, :], pb[:, 0:T], ACT.Sqrt, bias=bias1[:, 0:1], scale=1.0 / dim).then_inc(freed(st + (part,)), 1)
                    for k in range(KD):
                        act.wait_ge(norm_f, nf + k + 1)
                        nc.scalar.activation(n_hi[:, k, :], work[:, k, :], ACT.Copy).then_inc(norm_h, 1)
                elif kind == "retv":
                    act.wait_ge(ret_ready, st[1])
                    nc.scalar.activation(gn[:, 3, :], gn[:, 2, :], ACT.Sqrt, bias=bias1[:, 0:1], scale=1.0 / HD).then_inc(act_step, 1)
                elif kind in ("ot", "mixt"):
                    for key, k0, t in split_jobs(st):
                        pb = await_bank(act, key)
                        nc.scalar.activation(n_hi[:, k0:k0 + 4, t * P:t * P + P], pb[:, :].rearrange("p (k c) -> p k c", k=4),
                                             ACT.Copy).then_inc(ot_hi, 1)
                elif kind == "branch":
                    for key in ("wa", "wb"):
                        ahead(SL[(key, 0)])
                        ahead(SL[(key, 1)])
                    act.wait_ge(slab_done, SL[("wb", 1)] + 1)
                    for b in range(4):
                        act.wait_ge(merged, b + 1)
                        nc.scalar.activation(n_hi[:, 2 * b:2 * b + 2, :], work[:, 2 * b:2 * b + 2, :], ACT.Copy).then_inc(ot_hi, 1)
                elif kind == "wout":
                    ahead(SL[st])

        @block.vector
        def _(dve):
            V = nc.vector
            chain = [0]

            def link(ins):
                ins.then_inc(dve_step, 1)
                chain[0] += 1
                dve.wait_ge(dve_step, chain[0])

            turn_used = [None]

            def take_turn():
                if turn_used[0]:
                    dve.wait_ge(*turn_used[0])

            nxt = [0]

            def split(s, it=0):
                dve.wait_ge(hi_ready, s + 1 + BODY * it)
                n = width(s)
                V.tensor_tensor(w_lo[:, s % SPLIT, 0:n], raw[:, s % RING, 0:n], w_hi[:, s % SPLIT, 0:n].bitcast(f32),
                                ALU.subtract).then_inc(lo_ready, 1)

            def ahead(s):
                while nxt[0] <= min(s + 2, NSLAB - 1):
                    split(nxt[0])
                    nxt[0] += 1

            def swish(st, i, buf, it=0):
                f = st[1]
                b, frees = JOB[("g", f, i)]
                dve.wait_ge(bank_free[b], frees + 1 + it)
                b = JOB[("u", f, i)][0]
                dve.wait_ge(slab_done, SL[("u", f, i)] + 1 + BODY * it)
                V.tensor_tensor(hid[:, buf, :], silu_sb, bank[b][:, :], ALU.mult).then_inc(bank_free[b], 1)
                rest(FF[st][0] + i, buf, 2 * it)

            def square(st, i, buf, it=0):
                b, frees = JOB[("f", st[1], i)]
                dve.wait_ge(bank_free[b], frees + 1 + it)
                V.tensor_tensor(hid[:, buf, :], silu_sb, silu_sb, ALU.mult).then_inc(hid_ready, 1)
                rest(FF[st][0] + i, buf, 3 * it)

            def rest(n, buf, turn):
                dve.wait_ge(hidh_ready, n + 1 + turn)
                V.tensor_tensor(hid_lo[:, buf, :], hid[:, buf, :], hid_hi[:, buf, :].bitcast(f32), ALU.subtract).then_inc(hidl_ready, 1)

            dve.wait_ge(consts_in, 16)
            at = C1["causal"][0]
            V.tensor_copy(identb[:, :], con("ident")).then_inc(setup, 1)
            V.tensor_copy(masks[:, :], cst[:, at:at + 768]).then_inc(setup, 1)
            dve.wait_ge(small_in, 16 * (len(GAINS) + 7))
            V.tensor_scalar(nsink[:, :], sink[:, :], -1.0, None, ALU.mult).then_inc(setup, 1)
            link(V.tensor_copy(turns, pos_i))
            link(V.tensor_scalar(ang, turns, con("inv64"), None, ALU.mult))
            link(V.tensor_scalar(turns, ang, 0.5 / PI, ROUND, ALU.mult, ALU.add))
            link(V.tensor_scalar(turns, turns, ROUND, None, ALU.subtract))
            link(V.scalar_tensor_tensor(red, turns, -TWO_PI_1, ang, ALU.mult, ALU.add))
            link(V.scalar_tensor_tensor(red, turns, -TWO_PI_2, red, ALU.mult, ALU.add))
            link(V.scalar_tensor_tensor(red, turns, -TWO_PI_3, red, ALU.mult, ALU.add))
            V.tensor_scalar(red, red, PI_LOW, -PI_LOW, ALU.min, ALU.max).then_inc(setup, 1)
            dve.wait_ge(setup, 4)
            V.scalar_tensor_tensor(ang, red, -1.0, red, ALU.mult, ALU.max).then_inc(setup, 1)
            ahead(-1)

            def bc(ap, n, m):
                return ap.unsqueeze(2).to_broadcast([P, n, m])

            def weigh(dst, src, c, n):
                return V.tensor_tensor(dst.rearrange("p (h d) -> p h d", h=n), src.rearrange("p (h d) -> p h d", h=n),
                                       bc(c, n, HD), ALU.mult)

            for st in STEPS:
                kind = st[0]
                if kind == "gains":
                    pb = await_bank(dve, st)
                    V.tensor_copy(gains[:, :], pb[:, 0:NGAIN]).then_inc(freed(st), 1)
                elif kind == "x":
                    b = st[1]
                    pb = await_bank(dve, st)
                    V.tensor_copy(hT[:, 2 * b:2 * b + 2, :], halves(pb[:, :])).then_inc(h_ready, 1)
                elif kind == "norm":
                    n = st[1]
                    _, nh, _ = NB[st]
                    g0 = GROW[NORM_GAIN[n][0]] + NORM_GAIN[n][1]
                    dve.wait_ge(*free_count(st))
                    if n == 0:
                        dve.wait_ge(*free_count(("gains",)))
                    link(V.reciprocal(rstd[:, 0, :], std[:, 0, :]))
                    for k in range(KD):
                        ins = V.scalar_tensor_tensor((hT if n == 3 else work)[:, k, :], hT[:, k, :], gains[:, g0 + k:g0 + k + 1],
                                                     rstd[:, 0, :], ALU.mult, ALU.mult)
                        if n != 3:
                            ins.then_inc(norm_f, 1)
                        elif k % 2:
                            ins.then_inc(h_ready, 1)
                    if n not in (3, 8):
                        for k in range(KD):
                            dve.wait_ge(norm_h, nh + k + 1)
                            V.tensor_tensor(n_lo[:, k, :], work[:, k, :], n_hi[:, k, :].bitcast(f32), ALU.subtract).then_inc(norm_l, 1)
                elif kind == "ffn1":
                    s0 = SL[("g", st[1], 0)]
                    with dve.Fori(0, (FF1 - 1) // 2) as it:
                        for i in (1, 2):
                            s = SL[("g", st[1], i)]
                            split(s, it)
                            split(s + 1, it)
                            swish(st, i - 1, (i - 1) % 2, it)
                            split(s + 2, it)
                    swish(st, FF1 - 1, (FF1 - 1) % 2)
                    nxt[0] = s0 + 3 * FF1 - 1
                    ahead(s0 + 3 * FF1 - 1)
                    dve.wait_ge(slab_done, SL[("d", st[1], FF1 - 1) if kind == "ffn1" else ("e", st[1], FF2 - 1)] + 1)
                    for b in range(4):
                        V.scalar_tensor_tensor(hT[:, 2 * b:2 * b + 2, :], halves(acc[b][:, :]), 0.5, hT[:, 2 * b:2 * b + 2, :],
                                               ALU.mult, ALU.add).then_inc(h_ready, 1)
                elif kind == "ffn2":
                    s0 = SL[("f", st[1], 0)]
                    with dve.Fori(0, (FF2 - 1) // 3) as it:
                        for i in range(1, 4):
                            square(st, i - 1, (i - 1) % 3, it)
                            split(s0 + 2 * i, it)
                            split(s0 + 2 * i + 1, it)
                    square(st, FF2 - 1, (FF2 - 1) % 3)
                    nxt[0] = s0 + 2 * FF2
                    ahead(s0 + 2 * FF2 - 1)
                    dve.wait_ge(slab_done, SL[("d", st[1], FF1 - 1) if kind == "ffn1" else ("e", st[1], FF2 - 1)] + 1)
                    for b in range(4):
                        V.tensor_tensor(hT[:, 2 * b:2 * b + 2, :], halves(acc[b][:, :]), hT[:, 2 * b:2 * b + 2, :], ALU.add).then_inc(h_ready, 1)
                elif kind in ("proj", "uq", "ukv", "gate"):
                    ahead(SL[st])
                elif kind == "rope":
                    r = RO[st[1:]]
                    _, n, nrow, _, (_, sin), dst = rotation(*st[1:])
                    pb = await_bank(dve, st)
                    if r == 0:
                        dve.wait_ge(trig, 2)
                    if st[1] == 1:
                        dve.wait_ge(tables_in, 16)
                    if st[2] == "kc":
                        view = [x[:, 0:32].rearrange("p (g c) -> p g c", g=2)[:, :, 0:NCMP] for x in (turn_s, pb, turn_c[:, r % 2])]
                        s_ = sin[:, 31:T:16].unsqueeze(1).to_broadcast([P, 2, NCMP])
                        dst = kcR[:, :, 0:NCMP]
                    else:
                        view = [x[0:nrow, 0:n * T].rearrange("p (a t) -> p a t", a=n) for x in (turn_s, pb, turn_c[:, r % 2])]
                        s_ = sin.unsqueeze(1).to_broadcast([nrow, n, T])
                    take_turn()
                    V.tensor_tensor(view[0], view[1], s_, ALU.mult).then_inc(freed(st), 1)
                    dve.wait_ge(*free_count(st))
                    dve.wait_ge(turnc_ready, r + 1)
                    V.tensor_tensor(dst, view[2], view[0], ALU.add).then_inc(rope_done, 1)
                    turn_used[0] = (rope_done, r + 1)
                elif kind == "cmp1":
                    v = "kv".index(st[1])
                    if v == 0:
                        dve.wait_ge(*free_count(("proj", 0, "kcvc")))
                    if v:
                        dve.wait_ge(xpel_ready, v)
                    pe0 = GROW["cmp_pe_" + st[1]]
                    out_v = xpe.rearrange("p (a b g c) -> p a b g c", a=2, b=8, g=2)
                    for g in range(2):
                        for a in range(2):
                            src = x2[:, v, g, 16 * a:16 * a + 240].rearrange("p (c b e) -> p b c e", b=8, e=2)[:, :, :, 0]
                            last = V.tensor_tensor(out_v[:, a, :, g, :], src, bc(gains[:, pe0 + 8 * a:pe0 + 8 * a + 8], 8, NCMP), ALU.add)
                    last.then_inc(xpe_ready, 1)
                    dve.wait_ge(xpeh_ready, v + 1)
                    V.tensor_tensor(xpe_lo[:, v, :], xpe, xpe_hi[:, v, :].bitcast(f32), ALU.subtract).then_inc(xpel_ready, 1)
                    ahead(SL[st + (0,)])
                    ahead(SL[st + (1,)])
                elif kind == "cmp2" and st[1] == "v":
                    pb = await_bank(dve, st)
                    V.tensor_tensor(vblk.rearrange("p (h d) -> p h d", h=8), pb[:, 0:HD].unsqueeze(1).to_broadcast([P, 8, HD]),
                                    bc(con("blk"), 8, HD), ALU.mult).then_inc(freed(st), 1)
                elif kind == "s":
                    _, l, a, t, g = st
                    q, nk = ATT[st[1:]], P * (t + 1)
                    heads = groups(a, t)[g]
                    nh, buf = len(heads), q % 3
                    pb = await_bank(dve, st)
                    ins = V.tensor_reduce(negm[:, buf, 0:nh], pb[:, :].rearrange("p (h k) -> p h k", h=nh), AX.X, ALU.max, negate=True)
                    if a == "swa":
                        hs = slice(heads[0], heads[-1] + 1, 2)
                        link(ins)
                        link(V.tensor_tensor(negm[:, buf, 0:nh], negm[:, buf, 0:nh], nsink[:, hs], ALU.min))
                        ins = V.tensor_tensor(dsink[:, t, hs], negm[:, buf, 0:nh], sink[:, hs], ALU.add)
                    ins.then_inc(negm_ready, 1)
                elif kind == "t":
                    n = PVN[st[1:]]
                    pb = await_bank(dve, st)
                    if n >= 2:
                        dve.wait_ge(pv_done, n - 1)
                    V.tensor_copy(probsT[:, n % 2, :], pb[:, :]).then_inc(freed(st), 1)
                elif kind == "o":
                    _, l, a, t = st
                    o, done = ON[st[1:]]
                    ob = acc[o % 4]
                    dve.wait_ge(pv_done, done)
                    if o:
                        dve.wait_ge(o_free, o)
                    sums = rsum[:, RSLOT[a], t, :]
                    if a == "swa":
                        link(V.tensor_tensor(rinv8[:, :], sums, esink[:, t, :], ALU.add))
                        link(V.reciprocal(coef[:, :], rinv8[:, :]))
                        weigh(o_sum[:, 1, t, :], ob[:, :], coef[:, :], 8).then_inc(o_free, 1)
                    elif a in GATE:
                        link(V.reciprocal(rinv8[:, :], sums))
                        link(V.tensor_tensor(coef[:, :], rinv8[:, :], gates[:, t, 8 * GATE[a]:8 * GATE[a] + 8], ALU.mult))
                        if a == "slc":
                            weigh(o_sum[:, 0, t, :], ob[:, :], coef[:, :], 8).then_inc(o_free, 1)
                        else:
                            take_turn()
                            weigh(o_tmp[:, :], ob[:, :], coef[:, :], 8).then_inc(o_free, 1)
                            dve.wait_ge(o_free, o + 1)
                            ins = V.tensor_tensor(o_sum[:, 0, t, :], o_sum[:, 0, t, :], o_tmp[:, :], ALU.add)
                            if a == "cmp":
                                ins.then_inc(oc_ready, 1)
                                turn_used[0] = (oc_ready, t + 1)
                            else:
                                link(ins)
                                turn_used[0] = None
                    else:
                        nh = HEADS[a]
                        c0 = 0 if a == "mla" else 512
                        link(V.reciprocal(rinv8[:, 0:nh], sums[:, 0:nh]))
                        weigh(mix[:, t, c0:c0 + nh * HD], ob[:, 0:nh * HD], rinv8[:, 0:nh], nh).then_inc(o_free, 1)
                elif kind == "cs":
                    t = st[1]
                    pb = await_bank(dve, st)
                    s3 = pb[:, 0:P].rearrange("p (h c) -> p h c", h=8)
                    e3 = cmp_e[:, t, :].rearrange("p (h c) -> p h c", h=8)
                    link(V.tensor_reduce(cneg[:, t, :], s3, AX.X, ALU.max, negate=True))
                    V.tensor_tensor(e3, s3, bc(cneg[:, t, :], 8, CP), ALU.add).then_inc(cs_ready, 1)
                    dve.wait_ge(cexp_ready, t + 1)
                    V.tensor_reduce(rsum[:, RSLOT["cmp"], t, :], e3, AX.X, ALU.add).then_inc(freed(st), 1)
                    V.tensor_tensor(cmp_p[:, t, :], cmp_e[:, t, :], con("cmp_vis")[:, t * P:t * P + P], ALU.mult).then_inc(cp_ready, 1)
                elif kind == "ct":
                    n = PVN[(0, "cmp", st[1], 0)]
                    pb = await_bank(dve, st)
                    dve.wait_ge(pv_done, n - 1)
                    V.tensor_copy(probsT[:, n % 2, 0:P], pb[:, 0:P]).then_inc(freed(st), 1)
                elif kind == "idx":
                    _, l, n = st
                    t, heads = IDX[n]
                    nh, nk = len(heads), P * (t + 1)
                    pb = await_bank(dve, st)
                    if n == 0:
                        dve.wait_ge(*free_count(("proj", l, "misc", "b")))
                    rw = turn_s[:, 0:nh * nk].rearrange("p (h k) -> p h k", h=nh)
                    take_turn()
                    V.scalar_tensor_tensor(rw, pb[:, 0:nh * nk].rearrange("p (h k) -> p h k", h=nh), 0.0,
                                           bc(wit[:, t, heads[0]::4], nh, nk), ALU.max, ALU.mult).then_inc(freed(st), 1)
                    dve.wait_ge(*free_count(st))
                    part = score[:, t, 256:256 + nk]
                    link(V.tensor_reduce(part, rw.rearrange("p h k -> p k h"), AX.X, ALU.add))
                    turn_used[0] = None
                    first = heads[0] == 0
                    causal = con("causal")[:, 256 - nk:256]
                    link(V.tensor_tensor(score[:, t, 0:nk], part, causal if first else score[:, t, 0:nk], ALU.add))
                elif kind == "topk":
                    _, l, t, r0, r1 = st
                    nk = P * (t + 1)
                    sc = score[:, t, 0:nk]
                    for r in range(r0, r1):
                        link(V.max(out=m8[:, :], in_=sc))
                        link(V.match_replace(out=sc, in_to_replace=m8[:, :], in_values=sc, imm_value=TAKEN))
                    if r1 == TOP_ROUNDS:
                        part = score[:, t, 256:256 + nk]
                        link(V.tensor_scalar(part, sc, 0.75 * TAKEN, NEG, ALU.is_gt, ALU.mult))
                        V.tensor_tensor(selb[:, t, 0:nk], part, con("causal")[:, 256 - nk:256], ALU.add).then_inc(sel_ready, 1)
                elif kind == "rank":
                    l = st[1]
                    _, nh, _ = NB[st]
                    for n, part in enumerate(("q", "kv")):
                        dve.wait_ge(*free_count(st + (part,)))
                        link(V.reciprocal(rstd[:, n, :], std[:, n, :]))
                    for k in range(KD):
                        g = GROW["g_q_2"] + 6 * (l - 1) + k if k < 6 else GROW["g_kv_2"] + 2 * (l - 1) + k - 6
                        V.scalar_tensor_tensor(work[:, k, :], work[:, k, :], gains[:, g:g + 1], rstd[:, k // 6, :],
                                               ALU.mult, ALU.mult).then_inc(norm_f, 1)
                    for k in range(KD):
                        dve.wait_ge(norm_h, nh + k + 1)
                        V.tensor_tensor(n_lo[:, k, :], work[:, k, :], n_hi[:, k, :].bitcast(f32), ALU.subtract).then_inc(norm_l, 1)
                elif kind == "ret":
                    _, l, n = st
                    pb = await_bank(dve, st)
                    if n < 2:
                        V.tensor_tensor(halves(probs[:, n, :]), halves(pb[:, :]), con("decay").rearrange("p (h q) -> p h q", h=4)[:, n::2, :],
                                        ALU.mult).then_inc(freed(st), 1)
                    else:
                        V.tensor_tensor(probs[:, n, :].rearrange("p (h q) -> p h q", h=4), pb[:, :].rearrange("p (h q) -> p h q", h=4),
                                        decay[:, :, 0, :], ALU.mult).then_inc(freed(st), 1)
                elif kind == "retv":
                    l = st[1]
                    o, _ = ON[(l, "ret")]
                    ob = acc[o % 4][:, :].rearrange("p (h d) -> p h d", h=8)
                    xc = o_tmp[:, :].rearrange("p (h d) -> p h d", h=8)
                    xc2 = scr[:, 4096:4608].rearrange("p (h d) -> p h d", h=8)
                    dve.wait_ge(retv_done, l)
                    take_turn()
                    link(V.tensor_reduce(gn[:, 0, :], ob, AX.X, ALU.add))
                    link(V.tensor_scalar(gn[:, 1, :], gn[:, 0, :], -1.0 / HD, None, ALU.mult))
                    V.tensor_tensor(xc, ob, bc(gn[:, 1, :], 8, HD), ALU.add).then_inc(o_free, 1)
                    dve.wait_ge(o_free, o + 1)
                    link(V.tensor_tensor(xc2, xc, xc, ALU.mult))
                    V.tensor_reduce(gn[:, 2, :], xc2, AX.X, ALU.add).then_inc(ret_ready, 1)
                    dve.wait_ge(act_step, l)
                    link(V.reciprocal(gn[:, 0, :], gn[:, 3, :]))
                    link(V.tensor_tensor(xc, xc, bc(gn[:, 0, :], 8, HD), ALU.mult))
                    tok = halves(o_tmp[:, :])
                    link(V.tensor_tensor(tok, tok, gret[:, l - 1, :].unsqueeze(1).to_broadcast([P, NT, T]), ALU.mult))
                    dve.wait_ge(*free_count(("proj", l, "rg")))
                    V.tensor_tensor(mix[:, :, 768:1024], tok, rgt[:, :, :], ALU.mult).then_inc(oc_ready, 1)
                    turn_used[0] = (oc_ready, NT + l)
                elif kind in ("ot", "mixt"):
                    for key, k0, t in split_jobs(st):
                        pb = bank[JOB[key][0]]
                        dve.wait_ge(ot_hi, OT[key] + 1)
                        c = slice(t * P, t * P + P)
                        V.tensor_tensor(n_lo[:, k0:k0 + 4, c], pb[:, :].rearrange("p (k c) -> p k c", k=4),
                                        n_hi[:, k0:k0 + 4, c].bitcast(f32), ALU.subtract).then_inc(freed(key), 1)
                elif kind == "branch":
                    for key in ("wa", "wb"):
                        ahead(SL[(key, 0)])
                        ahead(SL[(key, 1)])
                    dve.wait_ge(slab_done, SL[("wa", 1)] + 1)
                    for b in range(4):
                        link(V.tensor_tensor(work[:, 2 * b:2 * b + 2, :], halves(acc[b][:, :]), sig_gate[:, 2 * b:2 * b + 2, :], ALU.mult))
                    for b in range(4):
                        pb = await_bank(dve, ("wb", b))
                        take_turn()
                        V.tensor_tensor(halves(o_tmp[:, :]), halves(pb[:, :]), sig_gate[:, 8 + 2 * b:10 + 2 * b, :], ALU.mult)\
                            .then_inc(freed(("wb", b)), 1)
                        dve.wait_ge(*free_count(("wb", b)))
                        V.tensor_tensor(work[:, 2 * b:2 * b + 2, :], work[:, 2 * b:2 * b + 2, :], halves(o_tmp[:, :]), ALU.add).then_inc(merged, 1)
                        turn_used[0] = (merged, b + 1)
                    for b in range(4):
                        dve.wait_ge(ot_hi, OT[st] + b + 1)
                        V.tensor_tensor(n_lo[:, 2 * b:2 * b + 2, :], work[:, 2 * b:2 * b + 2, :], n_hi[:, 2 * b:2 * b + 2, :].bitcast(f32),
                                        ALU.subtract).then_inc(ot_lo, 1)
                elif kind == "wout":
                    n = st[2]
                    ahead(SL[st])
                    pb = await_bank(dve, st)
                    V.tensor_tensor(hT[:, 2 * n:2 * n + 2, :], halves(pb[:, :]), hT[:, 2 * n:2 * n + 2, :], ALU.add).then_inc(h_ready, 1)
                elif kind == "y":
                    _, t, h = st
                    pb = await_bank(dve, st)
                    V.tensor_copy(yout[:, t, 512 * h:512 * h + 512], pb[:, :]).then_inc(y_ready, 1)

        @block.tensor
        def _(pe):
            MM = nc.tensor.matmul
            fresh = [None]

            def group(out, K, stat, mov, first=True, last=True):
                for k in range(K):
                    if fresh[0] is not None:
                        pe.wait_ge(norm_l, fresh[0] + k + 1)
                    for n, (a, b) in enumerate(((0, 0), (0, 1), (1, 0))):
                        mm = MM(out, stat(k, a), mov(k, b), start=(first and k == 0 and n == 0),
                                stop=(last and k == K - 1 and n == 2), skip_group_check=True)
                if K == KD:
                    fresh[0] = None
                return mm

            settled = [0]

            def settle(mm):
                settled[0] += 1
                mm.then_inc(rows_done, 1)
                pe.wait_ge(rows_done, settled[0])

            def weights(s):
                pe.wait_ge(lo_ready, s + 1)

            def w(s, lo):
                return (wl if lo else wh)(s)

            def xn(k, lo):
                return (n_lo if lo else n_hi)[:, k, :]

            def features(out, s, wide, c0, n, K=KD, k0=0):
                return group(out, K, lambda k, lo: w(s, lo)[:, k * wide + c0:k * wide + c0 + n], lambda k, lo: xn(k0 + k, lo))

            def tokens(out, s, wide, c0, n, t):
                return group(out, KD, lambda k, lo: xn(k, lo)[:, t * P:t * P + P],
                             lambda k, lo: w(s, lo)[:, k * wide + c0:k * wide + c0 + n])

            def pair(pb, s):
                for m in range(2):
                    mm = features(pb[:, m * T:m * T + T], s, 256, m * P, P)
                return mm

            def up(key, it=0):
                s = SL[key]
                b, frees = JOB[key]
                pe.wait_ge(lo_ready, s + 1 + BODY * it)
                if frees:
                    pe.wait_ge(bank_free[b], frees + it)
                if key in SPECIAL:
                    pe.wait_ge(BYNAME[SPECIAL[key][0]], SPECIAL[key][1])
                pair(bank[b], s).then_inc(slab_done, 1)

            def down(key, n, buf, it=0, turn=0):
                s = SL[key]
                pe.wait_ge(lo_ready, s + 1 + BODY * it)
                pe.wait_ge(hidl_ready, n + 1 + turn)
                for m in range(KD):
                    mm = group(acc[m // 2][:, (m % 2) * T:(m % 2) * T + T], 2,
                               lambda k, lo: w(s, lo)[:, k * D + m * P:k * D + m * P + P],
                               lambda k, lo: (hid_lo if lo else hid_hi)[:, buf, k * T:k * T + T], first=False)
                mm.then_inc(slab_done, 1)

            def clear():
                for b in range(4):
                    MM(acc[b][:, :], zerob[:, 0:P], zerob[:, :], start=True, stop=True, skip_group_check=True)

            pe.wait_ge(consts_in, 16)
            pe.wait_ge(pool_setup, 8)
            pe.wait_ge(setup, 2)
            ident = con("ident")
            for st in STEPS:
                kind = st[0]
                if kind == "gains":
                    pe.wait_ge(small_in, 16 * (len(GAINS) + 7))
                    pb = take(pe, st)
                    nc.tensor.transpose(pb[:, 0:NGAIN], gain_rows[0:NGAIN, :], ident[0:NGAIN, 0:NGAIN]).then_inc(filled(st), 1)
                elif kind == "x":
                    b = st[1]
                    if b == 0:
                        pe.wait_ge(x_in, 16)
                    pb = take(pe, st)
                    for k in range(2):
                        for t in range(NT):
                            mm = nc.tensor.transpose(pb[:, k * T + t * P:k * T + t * P + P], xin[:, t, (2 * b + k) * P:(2 * b + k + 1) * P], ident)
                    mm.then_inc(filled(st), 1)
                elif kind == "norm":
                    pb = take(pe, st)
                    for k in range(KD):
                        if k % 2 == 0:
                            pe.wait_ge(sq_ready, 4 * st[1] + k // 2 + 1)
                        mm = MM(pb[:, 0:T], ones[:, :], sq[:, k, :], start=(k == 0), stop=(k == KD - 1))
                    mm.then_inc(filled(st), 1)
                    fresh[0] = NB[st][1]
                elif kind == "ffn1":
                    f = st[1]
                    base = FF[st][0]
                    clear()
                    for c in "gu":
                        up((c, f, 0))
                    with pe.Fori(0, (FF1 - 1) // 2) as it:
                        for i in (1, 2):
                            for c in "gu":
                                up((c, f, i), it)
                            down(("d", f, i - 1), base + i - 1, (i - 1) % 2, it, 2 * it)
                    down(("d", f, FF1 - 1), base + FF1 - 1, (FF1 - 1) % 2)
                elif kind == "ffn2":
                    l = st[1]
                    base = FF[st][0]
                    clear()
                    up(("f", l, 0))
                    with pe.Fori(0, (FF2 - 1) // 3) as it:
                        for i in (1, 2, 3):
                            up(("f", l, i), it)
                            down(("e", l, i - 1), base + i - 1, (i - 1) % 3, it, 3 * it)
                    down(("e", l, FF2 - 1), base + FF2 - 1, (FF2 - 1) % 3)
                elif kind == "proj":
                    _, l, name = st
                    s = SL[st]
                    weights(s)
                    pb = take(pe, st)
                    if name == "misc" and l == 0:
                        features(pb[:, 0:T], s, 152, 0, P)
                        for t in range(NT):
                            mm = tokens(pb[:, T + 88 * t:T + 88 * t + 88], s, 152, HD, 88, t)
                    elif name in ("ksl", "kwn"):
                        features(pb[:, 0:T], s, 256, 0, P)
                        for t in range(NT):
                            mm = tokens(pb[:, T + P * t:T + P * t + P], s, 256, P, P, t)
                    elif name == "misc":
                        features(pb[0:MLA_Q, 0:T], s, 200, 0, MLA_Q)
                        features(pb[0:MLA_Q, T:2 * T], s, 200, 104, MLA_Q).then_inc(filled(st), 1)
                        st = st + ("b",)
                        pb = take(pe, st)
                        for t in range(NT):
                            mm = tokens(pb[:, 72 * t:72 * t + 72], s, 200, 96, 72, t)
                    elif name in ("rv", "rg"):
                        for t in range(NT):
                            mm = tokens(pb[:, T * t:T * t + T], s, 256, 0, 256, t)
                    else:
                        mm = pair(pb, s)
                    mm.then_inc(filled(st), 1)
                elif kind == "uq":
                    if st[2] == 0:
                        fresh[0] = NB[("rank", st[1])][1]
                    s = SL[st]
                    weights(s)
                    pb = take(pe, st)
                    for i in range(2):
                        mm = features(pb[0:MLA_Q, i * T:i * T + T], s, 192, i * MLA_Q, MLA_Q, K=6)
                    fresh[0] = None
                    mm.then_inc(filled(st), 1)
                elif kind == "ukv":
                    s = SL[st]
                    weights(s)
                    pe.wait_ge(norm_l, NB[("rank", st[1])][1] + KD)
                    for n in range(4):
                        pb = take(pe, st + (n,))
                        for i in range(2):
                            mm = features(pb[:, i * T:i * T + T], s, D, (2 * n + i) * P, P, K=2, k0=6)
                        mm.then_inc(filled(st + (n,)), 1)
                    for t in range(NT):
                        pb = take(pe, st + (4 + t,))
                        mm = group(pb[:, :], 2, lambda k, lo: xn(6 + k, lo)[:, t * P:t * P + P],
                                   lambda k, lo: w(s, lo)[:, k * D:k * D + D].rearrange("p (h c) -> p h c", h=8)[:, :, 64:128])
                        mm.then_inc(filled(st + (4 + t,)), 1)
                elif kind == "rope":
                    src, n, nrow, perm, _, _ = rotation(*st[1:])
                    pe.wait_ge(*free_count(XSC[st[1:]][0]))
                    pb = take(pe, st)
                    if st[2] == "kc":
                        mm = MM(pb[:, 0:32], perm, xs1[:, 0, 0:32], start=True, stop=True)
                    else:
                        mm = MM(pb[0:nrow, 0:n * T], perm, src, start=True, stop=True)
                    mm.then_inc(filled(st), 1)
                elif kind == "cmp1":
                    v = "kv".index(st[1])
                    pb = take(pe, st)
                    pe.wait_ge(xpel_ready, v + 1)
                    for half in range(2):
                        s = SL[st + (half,)]
                        weights(s)
                        for i in range(8):
                            for m in range(2):
                                c = (8 * half + i) * 30
                                mm = group(pb[:, 30 * m:30 * m + 30], 1, lambda k, lo: w(s, lo)[:, i * 256 + m * P:i * 256 + m * P + P],
                                           lambda k, lo: (xpe_lo if lo else xpe_hi)[:, v, c:c + 30], first=(half == 0 and i == 0 and m == 0))
                        mm.then_inc(slab_done, 1)
                elif kind == "cmp2":
                    v = "kv".index(st[1])
                    pe.wait_ge(*free_count(("cmp1", st[1])))
                    pb = take(pe, st)
                    for m in range(2):
                        if v == 0:
                            mm = MM(pb[:, 0:32], cmp_w2k[:, m, :, :].rearrange("p a d -> p (a d)"), gkT[:, m, :, :],
                                    start=(m == 0), stop=(m == 1))
                        else:
                            mm = MM(pb[:, 0:HD], gvT[:, m, :, :, :].rearrange("p g h c -> p (g h c)"), cmp_w2v[:, m, :],
                                    start=(m == 0), stop=(m == 1))
                    mm.then_inc(filled(st), 1)
                elif kind == "gate":
                    s = SL[st]
                    weights(s)
                    pair(take(pe, st), s).then_inc(filled(st), 1)
                elif kind == "s":
                    _, l, a, t, g = st
                    heads, nk = groups(a, t)[g], P * (t + 1)
                    nh = len(heads)
                    if g == 0:
                        need = {"slc": ("k", "nq1"), "win": ("k", "nq1"), "swa": ("sk", "sq1"), "dsa": ("ak", "aq"), "mla": ("uq3",)}[a]
                        pe.wait_ge(rope_done, max(RO[(l, u)] for u in need) + 1)
                        if a == "mla":
                            pe.wait_ge(kr_done, l)
                            pe.wait_ge(*free_count(("ukv", l, 3)))
                        if a == "dsa":
                            pe.wait_ge(sel_ready, 2 * (l - 1) + t + 1)
                    pb = take(pe, st)
                    MM(pb[:, 0:nh * nk], identb[:, :], mask_of(a, t).unsqueeze(1).to_broadcast([P, nh, nk]), start=True, stop=False,
                       skip_group_check=True)
                    for i, h in enumerate(heads):
                        if a == "dsa" and t == 0 and i == 2:
                            settle(mm)
                        q_, k_ = operands(l, a, t, h)
                        mm = MM(pb[:, i * nk:i * nk + nk], q_, k_[:, 0:nk], start=False, stop=True, skip_group_check=True)
                    mm.then_inc(filled(st), 1)
                elif kind == "t":
                    q = ATT[st[1:]]
                    pe.wait_ge(*free_count(("s",) + st[1:]))
                    pb = take(pe, st)
                    for c in range(4):
                        mm = nc.tensor.transpose(pb[:, c * P:c * P + P], probs[:, q % 3, c * P:c * P + P], ident)
                    mm.then_inc(filled(st), 1)
                elif kind == "pv":
                    _, l, a, t, g = st
                    heads, n, o = groups(a, t)[g], PVN[st[1:]], ON[st[1:4]][0]
                    if g == 0:
                        src = {"slc": ("proj", 0, "ksl"), "win": ("proj", 0, "kwn"), "swa": ("proj", 0, "misc"),
                               "dsa": ("proj", l, "misc", "b"), "mla": ("ukv", l, 5)}[a]
                        pe.wait_ge(*free_count(src))
                        if o >= 4:
                            pe.wait_ge(o_free, o - 3)
                    pe.wait_ge(*free_count(("t",) + st[1:]))
                    for i, h in enumerate(heads):
                        for blk in range(t + 1):
                            c = (i * (t + 1) + blk) * P
                            mm = MM(acc[o % 4][:, h * HD:h * HD + HD], probsT[:, n % 2, c:c + P], values(a, h, blk),
                                    start=(blk == 0), stop=(blk == t))
                    mm.then_inc(pv_done, 1)
                elif kind == "cs":
                    t = st[1]
                    pe.wait_ge(rope_done, RO[(0, "kc")] + 1)
                    pb = take(pe, st)
                    MM(pb[:, 0:P], identb[:, :], masks[:, 512 + t * P:512 + t * P + P], start=True, stop=False, skip_group_check=True)
                    for h in range(8):
                        if h == 4:
                            settle(mm)
                        r = slice(64 * (h // 4), 64 * (h // 4) + 64)
                        mm = MM(pb[:, h * CP:h * CP + CP], nqT[r, h % 4, t * P:t * P + P], kcR[r, h // 4, :], start=False, stop=True,
                                skip_group_check=True)
                    mm.then_inc(filled(st), 1)
                elif kind == "ct":
                    t = st[1]
                    n, o = PVN[(0, "cmp", t, 0)], ON[(0, "cmp", t)][0]
                    pe.wait_ge(cp_ready, t + 1)
                    pb = take(pe, st)
                    nc.tensor.transpose(pb[:, 0:P], cmp_p[:, t, :], ident).then_inc(filled(st), 1)
                    pe.wait_ge(o_free, o - 3)
                    pe.wait_ge(*free_count(("cmp2", "v")))
                    pe.wait_ge(*free_count(st))
                    MM(acc[o % 4][:, :], probsT[:, n % 2, 0:P], vblk, start=True, stop=True).then_inc(pv_done, 1)
                elif kind == "idx":
                    _, l, n = st
                    t, heads = IDX[n]
                    nk = P * (t + 1)
                    if n == 0:
                        pe.wait_ge(rope_done, max(RO[(l, "ki")], RO[(l, "qi")]) + 1)
                    pb = take(pe, st)
                    for i, h in enumerate(heads):
                        r = slice(32 * (h % 4), 32 * (h % 4) + 32)
                        mm = MM(pb[:, i * nk:i * nk + nk], qiT[r, h // 4, t * P:t * P + P], kiT[r, 0, 0:nk], start=True, stop=True)
                    mm.then_inc(filled(st), 1)
                elif kind == "rank":
                    for name in ("cq0", "cq1", "cq2", "ckv"):
                        pe.wait_ge(*free_count(("proj", st[1], name)))
                    for part, k0, k1 in (("q", 0, 6), ("kv", 6, 8)):
                        pb = take(pe, st + (part,))
                        for k in range(k0, k1):
                            mm = MM(pb[:, 0:T], ones[:, :], sq[:, k, :], start=(k == k0), stop=(k == k1 - 1))
                        mm.then_inc(filled(st + (part,)), 1)
                elif kind == "ret":
                    _, l, n = st
                    if n == 0:
                        pe.wait_ge(rope_done, max(RO[(l, "rk")], RO[(l, "rq")]) + 1)
                    pb = take(pe, st)
                    blk, first, n_q = (0, 0, T) if n < 2 else (1, P, P)
                    for h in (n, n + 2) if n < 2 else (0, 2, 1, 3):
                        i = h // 2 if n < 2 else h
                        if n == 2 and h == 1:
                            settle(mm)
                        r = slice(64 * (h % 2), 64 * (h % 2) + 64)
                        mm = MM(pb[:, i * n_q:i * n_q + n_q], rkT[r, h // 2, blk * P:blk * P + P], rqT[r, h // 2, first:T], start=True, stop=True)
                    mm.then_inc(filled(st), 1)
                elif kind == "retv":
                    l = st[1]
                    o = ON[(l, "ret")][0]
                    for n in range(3):
                        pe.wait_ge(*free_count(("ret", l, n)))
                    pe.wait_ge(*free_count(("proj", l, "rv")))
                    pe.wait_ge(o_free, o - 3)
                    for t in range(NT):
                        for h in range(4):
                            oc = acc[o % 4][:, (4 * t + h) * HD:(4 * t + h) * HD + HD]
                            c = (h // 2) * T + t * P
                            v_ = rvt[:, :, h * HD:h * HD + HD]
                            mm = MM(oc, probs[:, h % 2, c:c + P], v_[:, 0], start=True, stop=(t == 0))
                            if t:
                                mm = MM(oc, probs[:, 2, h * P:h * P + P], v_[:, 1], start=False, stop=True)
                    mm.then_inc(retv_done, 1)
                elif kind in ("ot", "mixt"):
                    if kind == "ot":
                        if st[1] == "a":
                            pe.wait_ge(oc_ready, st[2] + 1)
                        pe.wait_ge(o_free, max(ON[(0, "swa", 1)][0], ON[(0, "cmp", st[2])][0]) + 1)
                    else:
                        pe.wait_ge(oc_ready, 2 + st[1])
                        pe.wait_ge(o_free, ON[(st[1], "mla", st[2])][0] + 1)
                    for key, k0, t in split_jobs(st):
                        pb = take(pe, key)
                        src = o_sum[:, 0 if st[1] == "a" else 1, t, :] if kind == "ot" else mix[:, t, k0 * P:k0 * P + 512]
                        for c in range(4):
                            mm = nc.tensor.transpose(pb[:, c * P:c * P + P], src[:, c * P:c * P + P], ident)
                        mm.then_inc(filled(key), 1)
                elif kind == "branch":
                    for x, key in enumerate(("wa", "wb")):
                        for t in range(NT):
                            pe.wait_ge(*free_count(("ot", key[1], t)))
                        banks = acc if x == 0 else [take(pe, ("wb", b)) for b in range(4)]
                        for i in range(2):
                            s = SL[(key, i)]
                            weights(s)
                            for m in range(KD):
                                mm = group(banks[m // 2][:, (m % 2) * T:(m % 2) * T + T], 2,
                                           lambda k, lo: w(s, lo)[:, k * D + m * P:k * D + m * P + P],
                                           lambda k, lo: xn(4 * x + 2 * i + k, lo), first=(i == 0 and m % 2 == 0), last=(i == 1))
                            mm.then_inc(slab_done, 1)
                elif kind == "wout":
                    _, l, n = st
                    s = SL[st]
                    weights(s)
                    if n == 0:
                        if l == 0:
                            pe.wait_ge(ot_lo, 4)
                        else:
                            for t in range(NT):
                                for b in range(2):
                                    pe.wait_ge(*free_count(("mixt", l, t, b)))
                    pair(take(pe, st), s).then_inc(filled(st), 1)
                elif kind == "y":
                    _, t, h = st
                    pe.wait_ge(norm_f, NB[("norm", 8)][0] + KD)
                    pb = take(pe, st)
                    for c in range(4):
                        mm = nc.tensor.transpose(pb[:, c * P:c * P + P], work[:, 4 * h + c, t * P:t * P + P], ident)
                    mm.then_inc(filled(st), 1)


_OUTS = [((1, 256, 1024), "float32")]


def kernel(**inputs):
    import numpy as _np
    import concourse.bacc as _bacc
    from concourse import mybir as _mybir
    from concourse.bass_utils import run_bass_kernel_spmd as _run

    nc = _bacc.Bacc("TRN2", target_bir_lowering=False, num_devices=1)
    arrays, given = {}, {}
    const1, const2 = constants()
    for name, a in dict(inputs, const1=const1, const2=const2).items():
        a = _np.ascontiguousarray(a)
        arrays[f"in_{name}_dram"] = a
        given[name] = nc.dram_tensor(f"in_{name}_dram", a.shape, _mybir.dt.from_np(a.dtype), kind="ExternalInput").ap()
    const1, const2 = given.pop("const1"), given.pop("const2")
    shape, dtype = _OUTS[0]
    out = nc.dram_tensor("out_0_dram", shape, _mybir.dt.from_np(_np.dtype(dtype)), kind="ExternalOutput").ap()
    two_blocks(nc, given, const1, const2, out)
    r = _run(nc, [arrays], core_ids=[0])
    return r.results[0]["out_0_dram"]
```

```python
import numpy as np
import concourse.bass as bass
from concourse import mybir
from contextlib import ExitStack

P = 128
T = 256
NT = T // P
D = 1024
KD = D // P
HD = 64
RING = 3
BODY = 6
SPLIT = 3
SLAB = 2048
FF1 = 2816 // T
FF2 = 4096 // T
NCMP = T // 16 - 1
CP = 16
NEG = -1e30
TAKEN = -3e38
MLA_Q = 96
EPS = 1e-6
PI = float(np.pi)
PI_LOW = 3.1415925
TWO_PI_1 = 6.28125
TWO_PI_2 = float(np.float32(2 * np.pi - 6.28125))
TWO_PI_3 = float(2 * np.pi - 6.28125 - float(np.float32(2 * np.pi - 6.28125)))
ROUND = 12582912.0
TOPK = 64
TOP_ROUNDS = TOPK // 8

GAINS = [("norm_ffn1", 8), ("norm_mix", 8), ("norm_ffn2", 8), ("norm_final", 8), ("g_mix_2", 16),
         ("g_mlp_2", 16), ("g_final_2", 8), ("g_q_2", 12), ("g_kv_2", 4), ("cmp_pe_k", 16), ("cmp_pe_v", 16)]
GROW, _at = {}, 0
for _name, _n in GAINS:
    GROW[_name] = _at
    _at += _n
NGAIN = _at

CONST1 = [("ident", 128), ("perm64", 128), ("perm32", 128), ("perm96", 128), ("inv64", 1), ("blk", 8),
          ("causal", 256), ("band", 256), ("cmp_mask", 256), ("cmp_vis", 256), ("cos_a", 256), ("sin_a", 256)]
CONST2 = [("decay", 1024), ("cos_i", 256), ("sin_i", 256), ("cos_m", 256), ("sin_m", 256)]


def columns(table):
    out, at = {}, 0
    for name, n in table:
        out[name] = (at, n)
        at += n
    return out, at


C1, NC1 = columns(CONST1)
C2, NC2 = columns(CONST2)


def constants():
    c1, c2 = np.zeros((P, NC1), np.float32), np.zeros((P, NC2), np.float32)

    def put(name, value):
        where, (at, n) = (c1, C1[name]) if name in C1 else (c2, C2[name])
        where[:value.shape[0], at:at + n] = value

    def perm(half, first=0):
        m = np.zeros((P, P), np.float32)
        for c in range(first, P):
            if (c // half) % 2 == 0:
                m[c + half, c] = -1.0
            else:
                m[c - half, c] = 1.0
        return m

    put("ident", np.eye(P, dtype=np.float32))
    put("perm64", perm(32))
    put("perm32", perm(16))
    put("perm96", perm(16, 64))

    def inv(half):
        return (10000.0 ** (-(np.arange(half, dtype=np.float32) / np.float32(half))).astype(np.float64)).astype(np.float32)

    def angles(half, rows):
        return (np.arange(T, dtype=np.float32)[None, :] * inv(half)[rows % half][:, None]).astype(np.float64)

    rows = np.arange(P)
    put("inv64", inv(32)[rows % 32][:, None])
    put("blk", (rows[:, None] // CP == np.arange(8)[None, :]).astype(np.float32))
    q, k = np.arange(P)[:, None], np.arange(P)[None, :]
    causal = np.where(k <= q, 0.0, NEG)
    put("causal", np.concatenate([np.zeros((P, P)), causal], 1))
    put("band", np.concatenate([np.where(k > q, 0.0, NEG), causal], 1))
    c = np.arange(P)[None, :] % CP
    seen = [(c < NCMP) & (c * 16 + 31 <= q + t * P) for t in range(NT)]
    put("cmp_mask", np.concatenate([np.where(s, 0.0, NEG) for s in seen], 1))
    put("cmp_vis", np.concatenate([s.astype(np.float32) for s in seen], 1))
    put("cos_a", np.cos(angles(32, rows)))
    put("sin_a", np.sin(angles(32, rows)))
    put("cos_i", np.cos(angles(16, rows)))
    put("sin_i", np.sin(angles(16, rows)))
    turned = (rows >= 64)[:, None]
    put("cos_m", np.where(turned, np.cos(angles(16, rows)), 1.0))
    put("sin_m", np.where(turned, np.sin(angles(16, rows)), 0.0))
    gamma = np.log1p(-np.exp2(-5.0 - np.arange(4)))
    rel = q.T - k.T
    decay = [np.concatenate([np.where(rel >= 0, np.exp(np.maximum(rel, 0) * g), 0.0), np.exp((rel + P) * g)], 1)
             for g in gamma]
    put("decay", np.concatenate(decay, 1))
    return c1, c2


def schedule():
    S = [("gains", 0)] + [("x", b) for b in range(4)]
    S += [("split", 0), ("stat", 0), ("gains", 1), ("ffn1", 0), ("split", 1)]
    S += [("proj", 0, "nq0"), ("stat", 1), ("proj", 0, "kcvc"), ("rtok", 1), ("proj", 0, "misc"), ("proj", 0, "kk"), ("toks", 0),
          ("rope", 0, "nq0"), ("proj", 0, "vv"), ("rope", 0, "sk"), ("proj", 0, "sq0"), ("rope", 0, "k"),
          ("xpe", "k"), ("proj", 0, "nq1"), ("rope", 0, "sq0"), ("xpe", "v"), ("proj", 0, "sq1"), ("rope", 0, "nq1"), ("rope", 0, "sq1")]
    fill = [("cmp1", "k"), ("cmp1", "v")] + [("gate", n) for n in range(8)]
    after = {("cmp1", "v"): [("cmpt", "k")], ("gate", 0): [("cmp2", "k"), ("cmpt", "v")],
             ("gate", 1): [("cmp2", "v"), ("rope", 0, "kc")], ("gate", 5): [("cs", 0), ("cs", 1)],
             ("gate", 6): [("ct", 0), ("o", 0, "cmp", 0)], ("gate", 7): [("ct", 1), ("o", 0, "cmp", 1)]}
    S += attention(0, [("slc", 0), ("slc", 1), ("win", 0), ("win", 1), ("swa", 0), ("swa", 1)], fill, after, 2)
    S += [("ot", "a", 0), ("ot", "a", 1), ("ot", "b", 0), ("ot", "b", 1), ("branch",)]
    S += [("wout", 0, n) for n in range(4)]
    S += [("split", 2), ("stat", 2), ("ffn1", 1)]
    for l in (1, 2):
        n = 2 + 2 * l
        S += [("split", n), ("proj", l, "qi"), ("proj", l, "misc"), ("stat", n), ("proj", l, "cq0"), ("proj", l, "cq1"), ("rtok", n),
              ("proj", l, "cq2"), ("rope", l, "qi"), ("toks", l), ("rope", l, "ki"), ("rope", l, "ak"),
              ("proj", l, "ckv"), ("idx", l, 0), ("proj", l, "aq"), ("idx", l, 1), ("rank", l), ("idx", l, 2),
              ("proj", l, "rk"), ("rope", l, "aq"), ("idx", l, 3), ("idx", l, 4), ("proj", l, "rq"), ("rope", l, "rk"),
              ("topk", l, 0, 0, 8), ("idx", l, 5), ("idx", l, 6), ("proj", l, "rv"), ("rope", l, "rq"), ("idx", l, 7),
              ("proj", l, "rg"), ("rtok", -l), ("rope", l, "kr"), ("topk", l, 1, 0, 4), ("uq", l, 0),
              ("ret", l, 0), ("ret", l, 1), ("ret", l, 2), ("topk", l, 1, 4, 8), ("uq", l, 1), ("rope", l, "uq0"),
              ("uq", l, 2), ("retv", l), ("rope", l, "uq1")]
        S += attention(l, [("dsa", 0), ("dsa", 1)], [("retn", l), ("uq", l, 3)], {}, 1)
        S += [("rety", l), ("rope", l, "uq2"), ("rope", l, "uq3")]
        S += [("krope", l), ("ukv", l)]
        S += attention(l, [("mla", 0), ("mla", 1)], [], {}, 2)
        S += [("mixt", l, 0), ("mixt", l, 1)] + [("wout", l, n) for n in range(4)]
        S += [("split", 3 + 2 * l), ("stat", 3 + 2 * l), ("ffn2", l)]
    S += [("norm", 8)] + [("y", t, h) for h in range(2) for t in range(NT)]
    return S


HEADS = {"slc": 8, "win": 8, "swa": 8, "dsa": 4, "mla": 8}


def groups(a, t):
    per = 4 if t == 0 else 2
    order = list(range(HEADS[a]))
    if a in ("swa", "dsa"):
        order = order[::2] + order[1::2]
    return [order[g:g + per] for g in range(0, HEADS[a], per)]


def attention(l, tiles, fill, after, every):
    jobs = [(a, t, g) for a, t in tiles for g in range(len(groups(a, t)))]
    last = {(a, t): len(groups(a, t)) - 1 for a, t in tiles}
    fill = list(fill)
    S = [("s", l) + j for j in jobs[:2]]
    for n, job in enumerate(jobs):
        if n + 2 < len(jobs):
            S.append(("s", l) + jobs[n + 2])
        if fill and n % every == 0:
            S.append(fill[0])
            S += after.get(fill.pop(0), [])
        S.append(("t", l) + job)
        if n:
            S.append(("pv", l) + jobs[n - 1])
            if jobs[n - 1][2] == last[jobs[n - 1][:2]]:
                S.append(("o", l) + jobs[n - 1][:2])
    S += [("pv", l) + jobs[-1], ("o", l) + jobs[-1][:2]]
    for f in fill:
        S += [f] + after.get(f, [])
    return S


PROJ = {(0, "kcvc"): [(512, 256)], (0, "misc"): [(1816, 128), (1280, 24)], (0, "kk"): [(768, 128), (1024, 128)],
        (0, "vv"): [(896, 128), (1152, 128)], (0, "nq0"): [(0, 64), (256, 64), (64, 64), (320, 64)],
        (0, "nq1"): [(128, 64), (384, 64), (192, 64), (448, 64)],
        (0, "sq0"): [(1304, 256)], (0, "sq1"): [(1560, 256)],
        "misc": [(1312, 64), (1696, 32), (1024, 32), (1376, 64), (1728, 8)], "qi": [(1440, 256)], "aq": [(1056, 256)],
        "rk": [(1992, 256)], "rq": [(1736, 256)], "rv": [(2248, 256)], "rg": [(2504, 256)],
        "cq0": [(0, 256)], "cq1": [(256, 256)], "cq2": [(512, 256)], "ckv": [(768, 256)]}


def pieces(l, name):
    return PROJ[(0, name)] if l == 0 else PROJ[name]


NORM_GAIN = [("norm_ffn1", 0), ("norm_mix", 0), ("norm_ffn2", 0), ("norm_final", 0), ("g_mix_2", 0), ("g_mlp_2", 0),
             ("g_mix_2", 8), ("g_mlp_2", 8), ("g_final_2", 0)]


def two_blocks(nc, A, const1, const2, out):
    f32, f32r, bf16, i32 = mybir.dt.float32, mybir.dt.float32r, mybir.dt.bfloat16, mybir.dt.int32
    ALU, ACT, AX = mybir.AluOpType, mybir.ActivationFunctionType, mybir.AxisListType
    STEPS = schedule()
    ctx = ExitStack()
    with ctx:
        def sb(name, shape, dt=f32):
            return ctx.enter_context(nc.sbuf_tensor(name, shape, dt))

        def sem(name):
            return ctx.enter_context(nc.semaphore(name))

        raw = sb("raw", [P, RING, SLAB])
        w_hi, w_lo = sb("w_hi", [P, SPLIT, SLAB], f32r), sb("w_lo", [P, SPLIT, SLAB], f32r)
        hT = sb("hT", [P, KD, T])
        n_hi, n_lo = sb("n_hi", [P, KD, T], f32r), sb("n_lo", [P, KD, T], f32r)
        work = sb("work", [P, KD, T])
        hid_hi, hid_lo = sb("hid_hi", [P, 4, 512], f32r), sb("hid_lo", [P, 4, 512], f32r)
        cst = sb("cst", [P, NC1])
        masks = sb("masks", [P, 3 * 256], bf16)
        on_hi, on_lo = [x[:, :, :].rearrange("p a (b t) -> p (a b) t", b=2) for x in (hid_hi, hid_lo)]
        identb, zerob = sb("identb", [P, P], bf16), sb("zerob", [P, 512], bf16)
        ones = sb("ones", [P, P])
        gains = sb("gains", [P, NGAIN + KD])
        cos_p, sin_p = sb("cos_p", [P, T]), sb("sin_p", [P, T])
        gret = sb("gret", [P, 2, T])
        sink, nsink = sb("sink", [P, 8]), sb("nsink", [P, 8])
        xs = sb("xs", [P, 2, 512])
        xs1 = sb("xs1", [P, 1, T])
        turn_c, turn_s = sb("turn_c", [P, 2, 512]), sb("turn_s", [P, 512])
        probs, probsT = sb("probs", [P, 3, 512]), sb("probsT", [P, 2, 512])
        negm, dsink, esink = sb("negm", [P, 3, 8]), sb("dsink", [P, 2, 8]), sb("esink", [P, 2, 8])
        rsum, coef, rinv8 = sb("rsum", [P, 8, 2, 8]), sb("coef", [P, 8]), sb("rinv8", [P, 8])
        gates = sb("gates", [P, NT, 24])
        rstd = sb("rstd", [P, 3, T])
        rtok = sb("rtok", [P, 3, NT])
        m8, cneg, gn = sb("m8", [P, 8]), sb("cneg", [P, 2, 8]), sb("gn", [P, 4, 8])
        cmp_w2k, cmp_w2v = sb("cmp_w2k", [P, 2, 2, HD]), sb("cmp_w2v", [P, 2, HD])
        bias1 = sb("bias1", [P, 2])
        gkT = sb("gkT", [P, 2, 2, CP])
        gvT = sb("gvT", [P, 2, 2, 4, CP])
        kcR = sb("kcR", [P, 2, CP])
        xpe_hi, xpe_lo = hid_hi[:, 0:2, 0:480], hid_lo[:, 0:2, 0:480]
        scr = sb("scr", [P, 9728])

        def region(at, *shape):
            n = int(np.prod(shape))
            ap = scr[:, at:at + n]
            if len(shape) == 2:
                ap = ap.rearrange("p (a b) -> p a b", a=shape[0])
            if len(shape) == 3:
                ap = ap.rearrange("p (a b c) -> p a b c", a=shape[0], b=shape[1])
            return ap

        sig_gate = region(0, 16, T)
        sq = region(0, KD, T)
        qm = region(0, 8, T)
        tables = scr[:, 2048:4096]
        nqT, sqT = region(4096, 4, T), region(5120, 4, T)
        kT, skT = region(6144, 2, T), region(6656, 1, T)
        vsl, vwn, svt = region(6912, 2, P), region(7168, 2, P), region(7424, 2, HD)
        o_sum = region(7552, 2, NT, 512)
        silu_sb, hid = region(4096, 512), region(4608, 3, 512)
        qiT, kiT = region(4096, 2, T), region(4608, 1, T)
        aqT, akT = region(4864, 2, T), region(5376, 1, T)
        kfull = region(4096, 8, T)
        rqT, rkT = region(6144, 2, T), region(6656, 2, T)
        vm = region(6144, 2, 512)
        avt, wit = region(7168, 2, HD), region(7296, 2, 8)
        krR = region(7312, 1, T)
        mix = region(7568, 2, D)
        by_feature = region(7568, T)
        rvt = sb("rvt", [P, 2, T])
        rgt = sb("rgt", [P, 2, T])
        cmp_h = rgt[0:2 * NCMP, :, :]
        o_tmp = turn_s
        selb = sb("selb", [P, NT, T], bf16)
        score = probsT
        wflat = work[:, :, :].rearrange("p a b -> p (a b)")
        x2 = wflat[:, 0:1024].rearrange("p (v g t) -> p v g t", v=2, g=2)[:, :, :, :]
        xpe = wflat[:, 1024:1024 + 480]
        vblk = wflat[:, 1536:2048]
        xin = wflat.rearrange("p (t f) -> p t f", t=NT)
        yout = raw[:, 0, :].rearrange("p (t f) -> p t f", t=NT)
        gain_rows = scr[:, 8600:8728]
        cmp_e = turn_c[:, 0, 0:256].rearrange("p (t c) -> p t c", t=2)
        cmp_p = turn_c[:, 1, 0:256].rearrange("p (t c) -> p t c", t=2)
        pos_i = region(7552, T).bitcast(i32)
        ang, red, turns = region(7808, T), region(8064, T), region(8320, T)
        tab = {0: {"64": (rvt[:, 0, :], rvt[:, 1, :])}}
        for i, name in enumerate(("64", "32", "96", "q")):
            tab.setdefault(1, {})[name] = tab.setdefault(2, {})[name] = (work[:, 2 * i, :], work[:, 2 * i + 1, :])

        def con(name, rows=P):
            if name in C1:
                at, n = C1[name]
                return cst[0:rows, at:at + n]
            at, n = C2[name]
            return tables[0:rows, at:at + n]

        decay = con("decay").rearrange("p (h b q) -> p h b q", h=4, b=2)
        bank = [ctx.enter_context(nc.psum_tensor(f"bank{i}", [P, 512], f32)) for i in range(8)]
        acc = bank[0:4]

        raw_ready = [sem(f"raw_ready{i}") for i in range(RING)]
        hi_ready, lo_ready = sem("hi_ready"), sem("lo_ready")
        slab_done = sem("slab_done")
        bank_ready = [sem(f"bank_ready{i}") for i in range(8)]
        bank_free = [sem(f"bank_free{i}") for i in range(8)]
        ident_in, gain0_in, x_in = sem("ident_in"), sem("gain0_in"), sem("x_in")
        consts_in, pos_in, small_in = sem("consts_in"), sem("pos_in"), sem("small_in")
        setup = sem("setup")
        pool_setup = sem("pool_setup")
        trig, tables_in = sem("trig"), sem("tables_in")
        h_ready = sem("h_ready")
        sq_ready_final = sem("sq_ready_final")
        sq_ready, sq_sum, pool_step = sem("sq_ready"), sem("sq_sum"), sem("pool_step")
        r_ready, tab_ready = sem("r_ready"), sem("tab_ready")
        acc_full = sem("acc_full")
        norm_f, norm_h, norm_l = sem("norm_f"), sem("norm_h"), sem("norm_l")
        silu_ready, hid_ready, hidh_ready, hidl_ready = sem("silu_ready"), sem("hid_ready"), sem("hidh_ready"), sem("hidl_ready")
        turnc_ready, rope_done = sem("turnc_ready"), sem("rope_done")
        negm_ready, pv_done, o_free = sem("negm_ready"), sem("pv_done"), sem("o_free")
        xpe_ready, xpeh_ready, xpel_ready = sem("xpe_ready"), sem("xpeh_ready"), sem("xpel_ready")
        cs_ready, cexp_ready, cp_ready = sem("cs_ready"), sem("cexp_ready"), sem("cp_ready")
        merged, sig_ready = sem("merged"), sem("sig_ready")
        dve_step = sem("dve_step")
        act_step = sem("act_step")
        sel_ready, ret_ready, retv_done = sem("sel_ready"), sem("ret_ready"), sem("retv_done")
        kr_done, idx_done = sem("kr_done"), sem("idx_done")
        rank_mean, rank_std = sem("rank_mean"), sem("rank_std")
        rows_done = sem("rows_done")
        oc_ready, ot_hi, ot_lo = sem("oc_ready"), sem("ot_hi"), sem("ot_lo")
        y_ready, y_out = [sem("y_ready0"), sem("y_ready1")], [sem("y_out0"), sem("y_out1")]

        slabs, SL = [], {}
        RAWC, _fill = [], [0] * RING

        def slab(key, loads=1):
            s = len(slabs)
            SL[key] = s
            slabs.append(key)
            _fill[s % RING] += 16 * loads
            RAWC.append(_fill[s % RING])

        idle, _small = [False], [0]
        JOB = {}
        READY = {}
        _use, _free, _next = [0] * 8, [0] * 8, [0]
        LASTFREE = {}

        SPECIAL = {}

        def job(key, b=None, freed_by=None, of_slab=False):
            if b is None and idle[0] and key[0] in ("rope", "rtok", "toks", "idx", "rank"):
                b = _small[0] % 4
                _small[0] += 1
            if b is None:
                b = 4 + _next[0] % 4
                _next[0] += 1
            if of_slab:
                READY[key] = (slab_done, len(slabs))
            else:
                _use[b] += 1
                READY[key] = (bank_ready[b], _use[b])
            JOB[key] = (b, _free[b])
            if b in LASTFREE:
                SPECIAL[key] = LASTFREE.pop(b)
            if freed_by is None:
                _free[b] += 1
            else:
                LASTFREE[b] = freed_by

        XSC, RO, BUFUSE = {}, {}, {}
        ATT, PVN, ON = {}, {}, {}
        OO = {}
        _att, _o = [0], [0]
        hcount = [0]
        HN = {}
        NB, nh = {}, [0]
        RN, SS, TB = {}, {}, {}
        OT, ohi, nact = {}, [0], [0]
        FF = {}

        BEFORE = {}

        def bring(key, units, buf):
            BEFORE[key] = BUFUSE.get(buf, [])
            for u in units:
                XSC[u] = (key, buf)
            BUFUSE[buf] = list(units)

        for st in STEPS:
            kind = st[0]
            if kind == "x":
                job(st, freed_by=("h_ready", st[1] + 1))
            elif kind == "gains":
                job(st)
            elif kind in ("split", "norm"):
                idle[0] = st[1] in (1, 4, 6)
                HN[st[1]] = hcount[0]
                hcount[0] += 4
                NB[st] = nh[0]
                if kind == "split":
                    nh[0] += 8
                else:
                    job(st)
                    RN[st] = len(RN)
            elif kind == "stat":
                job(st, 7 if st[1] in (5, 7) else None)
                RN[st] = len(RN)
                SS[st] = len(SS)
                if st[1] == 4:
                    SS[st + ("final",)] = len(SS)
            elif kind in ("rtok", "toks"):
                job(st)
            elif kind == "ffn1":
                f = st[1]
                FF[st] = (nact[0], len(FF))
                nact[0] += FF1
                for i in range(FF1 + 1):
                    if i < FF1:
                        slab(("g", f, i))
                        job(("g", f, i), of_slab=True)
                        slab(("u", f, i))
                        job(("u", f, i), of_slab=True)
                    if i:
                        slab(("d", f, i - 1))
            elif kind == "ffn2":
                l = st[1]
                FF[st] = (nact[0], len(FF))
                nact[0] += FF2
                for i in range(FF2 + 1):
                    if i < FF2:
                        slab(("f", l, i))
                        job(("f", l, i), 4 + i % 3, of_slab=True)
                    if i:
                        slab(("e", l, i - 1))
            elif kind == "proj":
                _, l, name = st
                slab(st, len(pieces(l, name)))
                job(st, of_slab=True)
                if name == "misc":
                    if l:
                        bring(st, [(l, "ak"), (l, "ki")], 0)
                        bring(st + ("b",), [(l, "kr")], 2)
                        XSC[(l, "kr")] = (st, 2)
                    else:
                        bring(st, [(0, "sk")], 2)
                elif name in ("cq0", "cq1", "cq2", "ckv"):
                    OT[st] = ohi[0]
                    ohi[0] += 1
                elif name == "kk":
                    bring(st, [(0, "k")], 0)
                elif name in ("nq0", "nq1", "sq0", "sq1"):
                    bring(st, [(0, name)], {"nq0": 1, "nq1": 0, "sq0": 1, "sq1": 1}[name])
                elif name in ("qi", "aq", "rk", "rq"):
                    bring(st, [(l, name)], {"qi": 1, "aq": 0, "rk": 1, "rq": 0}[name])
            elif kind == "uq":
                _, l, n = st
                slab(st)
                job(st, of_slab=True)
                bring(st, [(l, f"uq{n}")], (n + 1) % 2)
            elif kind == "ukv":
                slab(st)
                for n in range(6):
                    job(st + (n,), of_slab=(n == 5))
            elif kind == "rope":
                RO[st[1:]] = len(RO)
                job(st)
            elif kind == "cmp1":
                slab(st + (0,))
                slab(st + (1,))
                job(st, of_slab=True)
            elif kind == "cmpt":
                job(st)
            elif kind == "cmp2":
                job(st)
                if st[1] == "k":
                    bring(st, [(0, "kc")], 2)
            elif kind == "gate":
                slab(st)
                job(st, of_slab=True)
            elif kind == "s":
                idle[0] = False
                ATT[st[1:]] = _att[0]
                _att[0] += 1
                job(st)
            elif kind == "t":
                job(st)
            elif kind == "pv":
                PVN[st[1:]] = len(PVN)
                if (st[1], st[2], st[3]) not in ON:
                    ON[st[1:4]] = [_o[0], 0]
                    _o[0] += 1
                ON[st[1:4]][1] = len(PVN)
            elif kind in ("cs", "ct"):
                job(st)
                if kind == "ct":
                    PVN[(0, "cmp", st[1], 0)] = len(PVN)
                    ON[(0, "cmp", st[1])] = [_o[0], len(PVN)]
                    _o[0] += 1
            elif kind in ("ot", "idx", "ret"):
                if kind == "ret":
                    idle[0] = False
                job(st)
                if kind == "ot":
                    OT[st] = ohi[0]
                    ohi[0] += 1
            elif kind == "retn":
                OO[(st[1], "ret")] = len(OO)
            elif kind == "o":
                OO[st[1:]] = len(OO)
            elif kind == "retv":
                ON[(st[1], "ret")] = [_o[0], 0]
                _o[0] += 1
            elif kind == "rank":
                job(st)
                RN[st] = len(RN)
                SS[st] = len(SS)
            elif kind == "branch":
                for n in range(2):
                    slab(("wa", n))
                    slab(("wb", n))
                    job(("wb", 2 * n))
                    job(("wb", 2 * n + 1), of_slab=True)
                OT[st] = ohi[0]
                ohi[0] += 4
            elif kind == "wout":
                slab(st)
                job(st, freed_by=("h_ready", hcount[0] + st[2] + 1), of_slab=True)
            elif kind == "mixt":
                for b in range(2):
                    job(st + (b,))
                    OT[st + (b,)] = ohi[0]
                    ohi[0] += 1
            elif kind == "y":
                job(st)
        OWNER = {o: key for key, (o, _) in ON.items()}
        NSLAB = len(slabs)
        ATTLIST = sorted(ATT, key=ATT.get)
        IDX = [(t, [j, j + 4]) for t in range(NT) for j in range(4)]
        PREV = {st[1]: prev for prev, st in zip(STEPS, STEPS[1:]) if st[0] in ("split", "norm")}
        PREV[1] = ("ffn1", 0)

        def gain(n, k):
            at = NGAIN + k if n == 4 else GROW[NORM_GAIN[n][0]] + NORM_GAIN[n][1] + k
            return gains[:, at:at + 1]

        FFN = {2: ("g", 1, 0), 5: ("f", 1, 0), 7: ("f", 2, 0)}
        for n, name in ((1, 0), (4, 1), (6, 2)):
            TB[n] = {0: 2, 1: 2 + 6, 2: 2 + 14}[name]
            TB[-name] = {0: 0, 1: 2 + 8, 2: 2 + 16}[name]
        BYNAME = {"h_ready": h_ready}

        def take(pe, key):
            b, frees = JOB[key]
            if frees:
                pe.wait_ge(bank_free[b], frees)
            if key in SPECIAL:
                pe.wait_ge(BYNAME[SPECIAL[key][0]], SPECIAL[key][1])
            return bank[b]

        def filled(key):
            return READY[key][0]

        def await_bank(eng, key):
            eng.wait_ge(*READY[key])
            return bank[JOB[key][0]]

        def freed(key):
            return bank_free[JOB[key][0]]

        def free_count(key):
            b, frees = JOB[key]
            return bank_free[b], frees + 1

        def rank_gain(l, k):
            g = GROW["g_q_2"] + 6 * (l - 1) + k if k < 6 else GROW["g_kv_2"] + 2 * (l - 1) + k - 6
            return gains[:, g:g + 1]

        def table_count(l, name):
            return TB[-l] if l and name.startswith("uq") else TB[2 * l + 2 if l else 1]

        def wh(s):
            return w_hi[:, s % SPLIT, :]

        def wl(s):
            return w_lo[:, s % SPLIT, :]

        def halves(ap):
            return ap.rearrange("p (a t) -> p a t", a=2)

        def split_jobs(st):
            if st[0] == "ot":
                return [(st, 0 if st[1] == "a" else 4, st[2])]
            return [(st + (b,), 4 * b, st[2]) for b in range(2)]

        def rotation(l, name):
            buf = XSC[(l, "k" if name == "kk" else name)][1]
            src = xs1 if buf == 2 else xs[:, buf, :].rearrange("p (a t) -> p a t", a=2)
            c64, c32, c96 = tab[l]["64"], tab[l].get("32"), tab[l].get("96")
            if name == "kc":
                c64 = (cos_p[:, :], sin_p[:, :])
            pick = {"sk": (src, 1, P, "perm64", c64, skT), "kc": (src, 1, P, "perm64", c64, kcR), "k": (src, 2, P, "perm64", c64, kT),
                    "nq0": (src, 2, P, "perm64", c64, nqT[:, 0:2]), "nq1": (src, 2, P, "perm64", c64, nqT[:, 2:4]),
                    "sq0": (src, 2, P, "perm64", c64, sqT[:, 0:2]), "sq1": (src, 2, P, "perm64", c64, sqT[:, 2:4]),
                    "ak": (src[:, 0:1], 1, P, "perm64", c64, akT), "ki": (src[:, 1:2] if buf != 2 else src, 1, P, "perm32", c32, kiT),
                    "qi": (src, 2, P, "perm32", c32, qiT), "aq": (src, 2, P, "perm64", c64, aqT),
                    "rk": (src, 2, P, "perm64", c64, rkT), "rq": (src, 2, P, "perm64", c64, rqT),
                    "kr": (src, 1, MLA_Q, "perm96", c96, krR)}
            if name.startswith("uq"):
                n = int(name[2])
                return src[0:MLA_Q], 2, MLA_Q, con("perm96")[0:MLA_Q, 0:MLA_Q], [x[0:MLA_Q] for x in tab[l]["q"]], qm[0:MLA_Q, 2 * n:2 * n + 2]
            a, n, rows, perm, tabs, dst = pick[name]
            return a[0:rows], n, rows, con(perm)[0:rows, 0:rows], (tabs[0][0:rows], tabs[1][0:rows]), dst[0:rows]

        def operands(l, a, t, h):
            tok = slice(t * P, t * P + P)
            if a in ("slc", "win"):
                r = slice(64 * (h // 4), 64 * (h // 4) + 64)
                return nqT[r, h % 4, tok], kT[r, 0 if a == "slc" else 1, :]
            if a == "swa":
                r = slice(64 * (h % 2), 64 * (h % 2) + 64)
                return sqT[r, h // 2, tok], skT[r, 0, :]
            if a == "dsa":
                r = slice(64 * (h % 2), 64 * (h % 2) + 64)
                return aqT[r, h // 2, tok], akT[r, 0, :]
            return qm[0:MLA_Q, h, tok], kfull[0:MLA_Q, h, :]

        def values(a, h, blk):
            if a in ("slc", "win"):
                return (vsl if a == "slc" else vwn)[:, blk, 64 * (h // 4):64 * (h // 4) + 64]
            if a == "swa":
                return svt[:, blk, :]
            if a == "dsa":
                return avt[:, blk, :]
            return vm[:, blk, 64 * h:64 * h + 64]

        def mask_of(a, t):
            if a == "dsa":
                return selb[:, t, 0:P * (t + 1)]
            at = 256 if a == "swa" else 0
            return masks[:, at + 128:at + 256] if t == 0 else masks[:, at:at + 256]

        RSLOT = {"slc": 0, "win": 1, "swa": 2, "cmp": 3, "mla": 4, "dsa": 5}
        GATE = {"cmp": 0, "slc": 1, "win": 2}

        def load_slab(sp, s):
            if s >= RING:
                sp.wait_ge(lo_ready, s - RING + 1)
            key, slot = slabs[s], s % RING
            kind = key[0]
            if kind == "proj":
                _, l, name = key
                src = (A["w_in"][0] if l == 0 else A["w_in_2"][l - 1]).rearrange("(k p) c -> p k c", p=P)
                width = sum(n for _, n in pieces(l, name))
                dst = raw[:, slot, 0:KD * width].rearrange("p (k c) -> p k c", k=KD)
                at = 0
                for c0, n in pieces(l, name):
                    sp.dma_start(dst[:, :, at:at + n], src[:, :, c0:c0 + n]).then_inc(raw_ready[slot], 16)
                    at += n
                return
            if kind in ("g", "u", "f"):
                src = cols(key[0], key[1])[key[2]]
            elif kind in ("d", "e"):
                src = rows(key[0], key[1])[key[2]]
            elif kind == "gate":
                c0 = 1944 + 256 * key[1]
                src = A["w_in"][0].rearrange("(k p) c -> p k c", p=P)[:, :, c0:c0 + 256]
            elif kind == "cmp1":
                src = A[f"cmp_{key[1]}_w1"][0].rearrange("(k p) c -> p k c", p=P)[:, 8 * key[2]:8 * key[2] + 8, :]
            elif kind in ("wa", "wb"):
                name = "w_branch_a" if kind == "wa" else "w_branch_b"
                src = A[name][0].rearrange("(k p) (n c) -> n p k c", p=P, c=512)[key[1]]
            elif kind == "wout":
                w = A["w_out"][0] if key[1] == 0 else A["w_out_2"][key[1] - 1]
                src = w.rearrange("(k p) (n c) -> n p k c", p=P, c=256)[key[2]]
            elif kind == "uq":
                src = A["w_uq_2"][key[1] - 1].rearrange("(k p) c -> p k c", p=P)[:, :, 192 * key[2]:192 * key[2] + 192]
            else:
                src = A["w_ukv_2"][key[1] - 1].rearrange("(k p) c -> p k c", p=P)
            k = src.shape[1]
            dst = raw[:, slot, 0:k * src.shape[2]].rearrange("p (k c) -> p k c", k=k)
            sp.dma_start(dst, src).then_inc(raw_ready[slot], 16)

        def width(s):
            key = slabs[s]
            if key[0] == "proj":
                return KD * sum(n for _, n in pieces(key[1], key[2]))
            return 6 * 192 if key[0] == "uq" else SLAB

        def cols(kind, f):
            w = {"g": lambda: A[f"ffn{f + 1}_gate"][0], "u": lambda: A[f"ffn{f + 1}_up"][0],
                 "f": lambda: A["w_ff1_2"][f - 1]}[kind]()
            return w.rearrange("(k p) (i c) -> i p k c", p=P, c=256)

        def rows(kind, f):
            w = A[f"ffn{f + 1}_down"][0] if kind == "d" else A["w_ff2_2"][f - 1]
            return w.rearrange("(i k p) c -> i p k c", p=P, k=2)

        block = ctx.enter_context(nc.Block())

        @block.sync
        def _(sp):
            for t in range(NT):
                sp.dma_start(xin[:, t, :], A["x"][0, t * P:t * P + P, :]).then_inc(x_in, 16)
            s = 0

            def body(first, it, kinds):
                for j in range(BODY):
                    n = first + j
                    kind, f, i = slabs[n]
                    step = kinds
                    sp.wait_ge(lo_ready, n - RING + 1 + BODY * it)
                    view = (cols if kind in ("g", "u", "f") else rows)(kind, f)
                    src = view[bass.ds(i + step * it, 1)].rearrange("o p k c -> (o p) k c")
                    dst = raw[:, n % RING, :].rearrange("p (k c) -> p k c", k=src.shape[1])
                    sp.dma_start(dst, src).then_inc(raw_ready[n % RING], 16)

            while s < NSLAB:
                kind = slabs[s][0]
                if kind == "g" and slabs[s][2] == 1:
                    bodies = (FF1 - 1) // 2
                    if s < RING:
                        for n in range(s, s + BODY):
                            load_slab(sp, n)
                        s, bodies = s + BODY, bodies - 1
                    with sp.Fori(0, bodies) as it:
                        body(s, it, 2)
                    s += BODY * bodies
                elif kind == "f" and slabs[s][2] == 1:
                    with sp.Fori(0, (FF2 - 1) // 3) as it:
                        body(s, it, 3)
                    s += BODY * ((FF2 - 1) // 3)
                else:
                    if slabs[s] == ("proj", 1, "misc"):
                        sp.wait_ge(merged, 4)
                        sp.dma_start(tables, const2).then_inc(tables_in, 16)
                    load_slab(sp, s)
                    if s == 1:
                        sp.dma_start(cst[:, P:NC1], const1[:, P:NC1]).then_inc(consts_in, 16)
                        for name, n in GAINS[1:]:
                            a = A[name]
                            if name.startswith("cmp_pe"):
                                src = a[0].rearrange("(r two) d -> r (two d)", two=2)
                            elif len(a.shape) == 1:
                                src = a.rearrange("(r c) -> r c", c=P)
                            else:
                                src = a.rearrange("l (r c) -> (l r) c", c=P)
                            sp.dma_start(gain_rows[GROW[name]:GROW[name] + n, :], src).then_inc(small_in, 16)
                        sp.dma_start(sink[:, :], A["swa_sinks"][0:1, :].to_broadcast([P, 8])).then_inc(small_in, 16)
                        for l in range(2):
                            sp.dma_start(gret[:, l, :], A["g_ret_2"][l:l + 1, :].to_broadcast([P, T])).then_inc(small_in, 16)
                        for i in range(2):
                            sp.dma_start(cmp_w2k[:, :, i, :], A["cmp_k_w2"][0].rearrange("(m p) d -> p m d", p=P)).then_inc(small_in, 16)
                        sp.dma_start(cmp_w2v[:, :, :], A["cmp_v_w2"][0].rearrange("(m p) d -> p m d", p=P)).then_inc(small_in, 16)
                    s += 1
            for t in range(NT):
                sp.wait_ge(y_ready[t], 2)
                sp.dma_start(out[0, t * P:t * P + P, :], yout[:, t, :]).then_inc(y_out[t], 16)
            for t in range(NT):
                sp.wait_ge(y_out[t], 16)

        @block.gpsimd
        def _(pool):
            nc.gpsimd.memset(ones[:, :], 1.0).then_inc(pool_setup, 1)
            nc.gpsimd.memset(zerob[:, :], 0.0).then_inc(pool_setup, 1)
            nc.gpsimd.memset(bias1[:, 0:1], EPS).then_inc(pool_setup, 1)
            nc.gpsimd.memset(bias1[:, 1:2], PI / 2).then_inc(pool_setup, 1)
            nc.gpsimd.memset(gkT[:, :, :, :], 0.0).then_inc(pool_setup, 1)
            nc.gpsimd.memset(gvT[:, :, :, :, :], 0.0).then_inc(pool_setup, 1)
            nc.gpsimd.memset(kcR[:, :, :], 0.0).then_inc(pool_setup, 1)
            nc.gpsimd.memset(rsum[:, :, :, :], 0.0).then_inc(pool_setup, 1)
            stepped = [0]

            def scaled(l, name, table, r):
                for dst, src in zip(tab[l][name], table):
                    nc.gpsimd.tensor_tensor(dst, src, r, ALU.mult).then_inc(tab_ready, 1)

            def add_up(parts, quarters=None, sq=sq):
                for n, (a, b) in enumerate(parts):
                    if quarters is not None and n < 3:
                        pool.wait_ge(sq_ready, quarters + n + 2)
                    ins = nc.gpsimd.tensor_tensor(sq[:, a, :], sq[:, a, :], sq[:, b, :], ALU.add)
                    if n < len(parts) - 1:
                        ins.then_inc(pool_step, 1)
                        stepped[0] += 1
                        pool.wait_ge(pool_step, stepped[0])
                    else:
                        ins.then_inc(sq_sum, 1)

            for st in STEPS:
                if st[0] == "stat":
                    n = st[1]
                    add_up([(slice(0, 2), slice(2, 4)), (slice(0, 2), slice(4, 6)), (slice(0, 2), slice(6, 8)), (0, 1)], HN[n])
                    if n == 4:
                        pool.wait_ge(sq_ready_final, 1)
                        add_up([(slice(0, 4), slice(4, 8)), (slice(0, 2), slice(2, 4)), (0, 1)], sq=work)
                    if n in (1, 4, 6):
                        l = n // 2 - 1 if n > 1 else 0
                        pool.wait_ge(r_ready, RN[st] + 1)
                        if l == 0:
                            pool.wait_ge(trig, 2)
                            scaled(l, "64", (cos_p[:, :], sin_p[:, :]), rstd[:, 0, :])
                        else:
                            if l == 1:
                                pool.wait_ge(tables_in, 16)
                            for name, c in (("32", "i"), ("64", "a"), ("96", "m")):
                                scaled(l, name, (con("cos_" + c), con("sin_" + c)), rstd[:, 0, :])
                if st[0] == "rank":
                    for name in ("cq0", "cq1", "cq2", "ckv"):
                        pool.wait_ge(*free_count(("proj", st[1], name)))
                    add_up([(slice(0, 3), slice(3, 6)), (0, 1), (0, 2), (6, 7)])
                    pool.wait_ge(r_ready, RN[st] + 1)
                    scaled(st[1], "q", (con("cos_m"), con("sin_m")), rstd[:, 1, :])
                if st[0] == "rope":
                    r = RO[st[1:]]
                    src, n, nrow, _, (cos, _), dst = rotation(*st[1:])
                    pool.wait_ge(*free_count(XSC[st[1:]][0]))
                    pool.wait_ge(tab_ready, table_count(*st[1:]))
                    if r >= 2:
                        pool.wait_ge(rope_done, r - 1)
                    if st[2] == "kc":
                        o = turn_c[:, r % 2, 0:32].rearrange("p (g c) -> p g c", g=2)[:, :, 0:NCMP]
                        i = xs1[:, 0, 0:32].rearrange("p (g c) -> p g c", g=2)[:, :, 0:NCMP]
                        c = cos[:, 31:T:16].unsqueeze(1).to_broadcast([P, 2, NCMP])
                    else:
                        o = turn_c[0:nrow, r % 2, 0:n * T].rearrange("p (a t) -> p a t", a=n)
                        i, c = src, cos.unsqueeze(1).to_broadcast([nrow, n, T])
                    nc.gpsimd.tensor_tensor(o, i, c, ALU.mult).then_inc(turnc_ready, 1)
                if st[0] == "krope":
                    l = st[1]
                    pool.wait_ge(rope_done, RO[(l, "kr")] + 1)
                    pool.wait_ge(turnc_ready, RO[(l, "uq3")] + 1)
                    pool.wait_ge(pv_done, ON[(l, "dsa", 1)][1])
                    nc.gpsimd.tensor_copy(kfull[64:96, :, :], krR[64:96, 0, :].unsqueeze(1).to_broadcast([32, 8, T])).then_inc(kr_done, 1)
                    pool.wait_ge(kr_done, l)

        @block.scalar
        def _(act):
            act.dma_start(cst[:, 0:P], const1[:, 0:P]).then_inc(ident_in, 16)
            act.dma_start(gain_rows[0:KD, :], A["norm_ffn1"][0].rearrange("(r c) -> r c", c=P)).then_inc(gain0_in, 16)
            act.dma_start(pos_i, A["positions"][0:1, :].to_broadcast([P, T])).then_inc(pos_in, 16)
            nxt = [0]

            def split(s, it=0, free=True):
                act.wait_ge(raw_ready[s % RING], RAWC[s] + 16 * (BODY // RING) * it)
                if free:
                    act.wait_ge(slab_done, s - SPLIT + 1 + BODY * it)
                n = width(s)
                nc.scalar.activation(w_hi[:, s % SPLIT, 0:n], raw[:, s % RING, 0:n], ACT.Copy).then_inc(hi_ready, 1)

            def ahead(s, by=2):
                while nxt[0] <= min(s + by, NSLAB - 1):
                    split(nxt[0], free=nxt[0] >= SPLIT)
                    nxt[0] += 1

            def silu(st, i, it=0):
                b, frees = JOB[("g", st[1], i)]
                act.wait_ge(bank_free[b], frees + 1 + it)
                nc.scalar.activation(silu_sb, silu_sb, ACT.Silu).then_inc(silu_ready, 1)

            def hidden(st, i, buf, it=0):
                act.wait_ge(hid_ready, FF[st][0] + i + 1 + 2 * it)
                nc.scalar.activation(hid_hi[:, buf, :], hid[:, buf, :], ACT.Copy).then_inc(hidh_ready, 1)

            def squares(st, i, buf, it=0):
                b, frees = JOB[("f", st[1], i)]
                act.wait_ge(bank_free[b], frees + 1 + it)
                nc.scalar.activation(hid[:, buf, :], silu_sb, ACT.Square)
                nc.scalar.activation(hid_hi[:, buf, :], silu_sb, ACT.Square).then_inc(hidh_ready, 1)

            act.wait_ge(pool_setup, 8)
            nc.scalar.activation(esink[:, 0, 0:2], bias1[:, :], ACT.Copy)
            for st in STEPS:
                kind = st[0]
                if kind == "split":
                    n = st[1]
                    act.wait_ge(*free_count(("gains", 0 if n == 0 else 1)))
                    if n == 4:
                        act.wait_ge(setup, 6)
                    for b in range(4):
                        if b == 2 and n == 0:
                            ahead(-2)
                        if b == 2 and PREV[n][0] == "wout":
                            ahead(SL[("wout", PREV[n][1], 3)])
                        act.wait_ge(h_ready, HN[n] + b + 1)
                        for k in (2 * b, 2 * b + 1):
                            nc.scalar.activation(n_hi[:, k, :], hT[:, k, :], ACT.Copy, scale=gain(n, k)).then_inc(norm_h, 1)
                        for c in {0: (), 1: (0,), 2: (1,), 3: (2, 3)}[b]:
                            nc.scalar.activation(sq[:, 2 * c:2 * c + 2, :], hT[:, 2 * c:2 * c + 2, :], ACT.Square).then_inc(sq_ready, 1)
                    if n == 0:
                        ahead(-1)
                    elif n in (2, 5, 7):
                        ahead(SL[FFN[n]])
                    elif n == 4:
                        ahead(SL[("proj", 1, "qi")], 1)
                        for k in range(KD):
                            last = nc.scalar.activation(work[:, k, :], hT[:, k, :], ACT.Square, scale=gain(3, k))
                        last.then_inc(sq_ready_final, 1)
                elif kind == "norm":
                    n = st[1]
                    for b in range(4):
                        act.wait_ge(h_ready, HN[n] + b + 1)
                        nc.scalar.activation(sq[:, 2 * b:2 * b + 2, :], hT[:, 2 * b:2 * b + 2, :], ACT.Square).then_inc(sq_ready, 1)
                    pb = await_bank(act, st)
                    nc.scalar.activation(rtok[:, 0, :], pb[:, 0:NT], ACT.Sqrt, bias=bias1[:, 0:1], scale=1.0 / D).then_inc(freed(st), 1)
                elif kind == "stat":
                    pb = await_bank(act, st)
                    if st[1] == 4:
                        nc.scalar.activation(rstd[:, 2, :], pb[:, 0:T], ACT.Sqrt, bias=bias1[:, 0:1], scale=1.0 / D).then_inc(rank_std, 1)
                        act.wait_ge(rank_mean, 1)
                        nc.scalar.activation(rstd[:, 0, :], rstd[:, 0, :], ACT.Sqrt, bias=bias1[:, 0:1], scale=1.0 / D).then_inc(rank_std, 1)
                    else:
                        nc.scalar.activation(rstd[:, 0, :], pb[:, 0:T], ACT.Sqrt, bias=bias1[:, 0:1], scale=1.0 / D).then_inc(freed(st), 1)
                elif kind == "toks":
                    l = st[1]
                    w_ = 88 if l == 0 else 72
                    act.wait_ge(*free_count(("rtok", 2 * l + 2 if l else 1)))
                    pb = await_bank(act, st)
                    for t in range(NT):
                        tok, r = pb[:, t * w_:t * w_ + w_], rtok[:, 0, t:t + 1]
                        if l == 0:
                            nc.scalar.activation(svt[:, t, :], tok[:, 0:HD], ACT.Copy, scale=r)
                            last = nc.scalar.activation(gates[:, t, :], tok[:, HD:HD + 24], ACT.Sigmoid, scale=r)
                        else:
                            nc.scalar.activation(avt[:, t, :], tok[:, 0:HD], ACT.Copy, scale=r)
                            last = nc.scalar.activation(wit[:, t, :], tok[:, HD:HD + 8], ACT.Copy, scale=rtok[:, 1, t:t + 1])
                    last.then_inc(freed(st), 1)
                elif kind == "rtok":
                    pb = await_bank(act, st)
                    if st[1] > 0:
                        nc.scalar.activation(rtok[:, 0, :], pb[:, 0:T:P], ACT.Copy)
                        nc.scalar.activation(rtok[:, 1, :], pb[:, 0:T:P], ACT.Copy, scale=1.0 / 16).then_inc(freed(st), 1)
                    else:
                        nc.scalar.activation(rtok[:, 2, :], pb[:, 0:T:P], ACT.Copy).then_inc(freed(st), 1)
                elif kind == "ffn1":
                    s0 = SL[("g", st[1], 0)]
                    body = 2

                    def turn(first, it, peeled=False):
                        for i in range(first, first + body):
                            s = SL[("g", st[1], i)]
                            if s >= nxt[0] or not peeled:
                                split(s, it, free=s >= SPLIT)
                            silu(st, i - 1, it)
                            split(s + 1, it)
                            hidden(st, i - 1, (i - 1) % 2, it)
                            split(s + 2, it)

                    turn(1, 0, peeled=True)
                    if st[1] == 0:
                        act.wait_ge(setup, 4)
                        nc.scalar.activation(sin_p[:, :], red, ACT.Sin).then_inc(trig, 1)
                        nc.scalar.activation(cos_p[:, :], ang, ACT.Sin, bias=bias1[:, 1:2], scale=-1.0).then_inc(trig, 1)
                    with act.Fori(0, (FF1 - 1) // body - 1) as it:
                        turn(1 + body, it)
                    nxt[0] = s0 + 3 * FF1 - 1
                    ahead(nxt[0], 0)
                    silu(st, FF1 - 1)
                    hidden(st, FF1 - 1, (FF1 - 1) % 2)
                    ahead(s0 + 3 * FF1 - 1, 1)
                elif kind == "ffn2":
                    s0 = SL[("f", st[1], 0)]

                    def turn(first, it, peeled=False):
                        for i in range(first, first + 3):
                            if not peeled or s0 + 2 * i >= nxt[0]:
                                split(s0 + 2 * i, it)
                            squares(st, i - 1, (i - 1) % 3, it)
                            split(s0 + 2 * i + 1, it)

                    turn(1, 0, peeled=True)
                    with act.Fori(0, (FF2 - 1) // 3 - 1) as it:
                        turn(4, it)
                    squares(st, FF2 - 1, (FF2 - 1) % 3)
                    nxt[0] = s0 + 2 * FF2
                    ahead(s0 + 2 * FF2 - 1, 1)
                elif kind == "proj":
                    _, l, name = st
                    ahead(SL[st])
                    for r in BEFORE.get(st, []):
                        act.wait_ge(rope_done, RO[r] + 1)
                    if name == "kcvc":
                        continue
                    pb = await_bank(act, st)
                    if name == "misc" and l == 0:
                        for r in range(0, P, 64):
                            nc.scalar.activation(xs1[r:r + 64, 0, :], pb[0:64, 0:T], ACT.Copy)
                        nc.scalar.activation(by_feature[0:88, :], pb[0:88, T:2 * T], ACT.Copy).then_inc(freed(st), 1)
                    elif name == "vv":
                        for t in range(NT):
                            for i, dst in enumerate((vsl, vwn)):
                                c = t * T + i * P
                                last = nc.scalar.activation(dst[:, t, :], pb[:, c:c + P], ACT.Copy, scale=rtok[:, 0, t:t + 1])
                        last.then_inc(freed(st), 1)
                    elif name == "misc":
                        for r in range(0, P, 64):
                            nc.scalar.activation(xs[r:r + 64, 0, 0:T], pb[0:64, 0:T], ACT.Copy)
                        for r in range(0, P, 32):
                            nc.scalar.activation(xs[r:r + 32, 0, T:2 * T], pb[64:96, 0:T], ACT.Copy)
                        for r in BEFORE[st + ("b",)]:
                            act.wait_ge(rope_done, RO[r] + 1)
                        nc.scalar.activation(xs1[0:64, 0, :], pb[0:64, 0:T], ACT.Copy)
                        nc.scalar.activation(xs1[64:96, 0, :], pb[96:128, 0:T], ACT.Copy)
                        nc.scalar.activation(by_feature[0:72, :], pb[0:72, T:2 * T], ACT.Copy).then_inc(freed(st), 1)
                    elif name in ("rv", "rg"):
                        for t in range(NT):
                            last = nc.scalar.activation((rvt if name == "rv" else rgt)[:, t, :], pb[:, t * T:t * T + T],
                                                        ACT.Copy if name == "rv" else ACT.Silu, scale=rtok[:, 0, t:t + 1])
                        last.then_inc(freed(st), 1)
                    elif name in ("cq0", "cq1", "cq2", "ckv"):
                        if name == "cq0":
                            act.wait_ge(sq_sum, SS[("stat", 2 + 2 * l)] + 1)
                            act.wait_ge(r_ready, RN[("stat", 2 + 2 * l)] + 1)
                        k = 2 * ("cq0", "cq1", "cq2", "ckv").index(name)
                        nc.scalar.activation(sq[:, k:k + 2, :], halves(pb[:, :]), ACT.Square)
                        for i in range(2):
                            last = nc.scalar.activation(on_hi[:, k + i, :], pb[:, i * T:i * T + T], ACT.Copy, scale=rank_gain(l, k + i))
                        last.then_inc(ot_hi, 1)
                    else:
                        buf = XSC[(l, "k" if name == "kk" else name)][1]
                        scale = 0.125 if name in ("nq0", "nq1", "sq0", "sq1", "aq", "rk") else 1.0
                        nc.scalar.activation(xs[:, buf, :], pb[:, :], ACT.Copy, scale=scale).then_inc(freed(st), 1)
                elif kind == "uq":
                    _, l, n = st
                    ahead(SL[st])
                    for r in BEFORE[st]:
                        act.wait_ge(rope_done, RO[r] + 1)
                    pb = await_bank(act, st)
                    buf = XSC[(l, f"uq{n}")][1]
                    nc.scalar.activation(xs[0:MLA_Q, buf, :], pb[0:MLA_Q, :], ACT.Copy, scale=MLA_Q ** -0.5).then_inc(freed(st), 1)
                elif kind == "ukv":
                    ahead(SL[st])
                    act.wait_ge(*free_count(("rtok", -st[1])))
                    for t in range(NT):
                        pb = await_bank(act, st + (4 + t,))
                        nc.scalar.activation(vm[:, t, :], pb[:, :], ACT.Copy, scale=rtok[:, 2, t:t + 1]).then_inc(freed(st + (4 + t,)), 1)
                elif kind == "xpe":
                    v = "kv".index(st[1])
                    act.wait_ge(xpe_ready, v + 1)
                    nc.scalar.activation(xpe_hi[:, v, :], xpe, ACT.Copy).then_inc(xpeh_ready, 1)
                elif kind == "cmp1":
                    v = "kv".index(st[1])
                    ahead(SL[st + (0,)])
                    ahead(SL[st + (1,)])
                    pb = await_bank(act, st)
                    nc.scalar.activation(cmp_h[:, v, :], pb[0:2 * NCMP, 0:T], ACT.Gelu_apprx_tanh).then_inc(freed(st), 1)
                elif kind == "cmpt":
                    pb = await_bank(act, st)
                    for m in range(2):
                        src = pb[:, m * P:m * P + 2 * NCMP].rearrange("p (g c) -> p g c", g=2)
                        if st[1] == "k":
                            last = nc.scalar.activation(gkT[:, m, :, 0:NCMP], src, ACT.Copy)
                        else:
                            last = nc.scalar.activation(gvT[:, m, :, :, 0:NCMP], src.unsqueeze(2).to_broadcast([P, 2, 4, NCMP]), ACT.Copy)
                    last.then_inc(freed(st), 1)
                elif kind == "cmp2" and st[1] == "k":
                    for r in BEFORE[st]:
                        act.wait_ge(rope_done, RO[r] + 1)
                    pb = await_bank(act, st)
                    nc.scalar.activation(xs1[:, 0, 0:32], pb[:, 0:32], ACT.Copy).then_inc(freed(st), 1)
                elif kind == "gate":
                    n = st[1]
                    ahead(SL[st])
                    act.wait_ge(*free_count(st))
                    nc.scalar.activation(sig_gate[:, 2 * n:2 * n + 2, :], sig_gate[:, 2 * n:2 * n + 2, :], ACT.Sigmoid).then_inc(sig_ready, 1)
                elif kind == "s":
                    _, l, a, t, g = st
                    q, nk = ATT[st[1:]], P * (t + 1)
                    heads = groups(a, t)[g]
                    buf = q % 3
                    act.wait_ge(negm_ready, q + 1)
                    if q >= 3:
                        await_bank(act, ("t",) + ATTLIST[q - 3])
                    if a == "dsa":
                        act.wait_ge(retv_done, l)
                    pb = bank[JOB[st][0]]
                    if a == "swa":
                        hs = slice(heads[0], heads[-1] + 1, 2)
                        nc.scalar.activation(esink[:, t, hs], dsink[:, t, hs], ACT.Exp)
                    for i, h in enumerate(heads):
                        c = slice(i * nk, i * nk + nk)
                        last = nc.scalar.activation(probs[:, buf, c], pb[:, c], ACT.Exp, bias=negm[:, buf, i:i + 1],
                                                    accum_out=rsum[:, RSLOT[a], t, h:h + 1])
                    last.then_inc(freed(st), 1)
                elif kind == "idx":
                    _, l, n = st
                    g = 8 * (l - 1) + n
                    nw = 2 * P * (IDX[n][0] + 1)
                    pb = await_bank(act, st)
                    if n >= 3:
                        act.wait_ge(idx_done, g - 2)
                    nc.scalar.activation(probs[:, n % 3, 0:nw], pb[:, 0:nw], ACT.Relu).then_inc(freed(st), 1)
                elif kind == "cs":
                    t = st[1]
                    act.wait_ge(cs_ready, t + 1)
                    nc.scalar.activation(cmp_e[:, t, :], cmp_e[:, t, :], ACT.Exp).then_inc(cexp_ready, 1)
                elif kind == "rank":
                    act.wait_ge(rank_mean, 1 + st[1])
                    for n, dim in enumerate((768, 256)):
                        last = nc.scalar.activation(rstd[:, 1 + n, :], rstd[:, 1 + n, :], ACT.Sqrt, bias=bias1[:, 0:1], scale=1.0 / dim)
                    last.then_inc(rank_std, 1)
                elif kind == "retn":
                    act.wait_ge(ret_ready, st[1])
                    nc.scalar.activation(gn[:, 3, :], gn[:, 2, :], ACT.Sqrt, bias=bias1[:, 0:1], scale=1.0 / HD).then_inc(act_step, 1)
                elif kind in ("ot", "mixt"):
                    for key, k0, t in split_jobs(st):
                        pb = await_bank(act, key)
                        nc.scalar.activation((n_hi if kind == "ot" else on_hi)[:, k0:k0 + 4, t * P:t * P + P],
                                             pb[:, :].rearrange("p (k c) -> p k c", k=4), ACT.Copy).then_inc(ot_hi, 1)
                elif kind == "branch":
                    for b in range(4):
                        if b % 2 == 0:
                            ahead(SL[("wb", 0) if b == 0 else ("wa", 1)])
                        act.wait_ge(merged, b + 1)
                        nc.scalar.activation(on_hi[:, 2 * b:2 * b + 2, :], work[:, 2 * b:2 * b + 2, :], ACT.Copy).then_inc(ot_hi, 1)
                elif kind == "wout" and st[2] < 3:
                    ahead(SL[st])
                elif kind == "y" and st[2] == 0:
                    t = st[1]
                    pb = await_bank(act, st)
                    act.wait_ge(r_ready, RN[("norm", 8)] + 1)
                    nc.scalar.activation(yout[:, t, 0:512], pb[:, :], ACT.Copy, scale=rtok[:, 0, t:t + 1]).then_inc(y_ready[t], 1)

        @block.vector
        def _(dve):
            V = nc.vector
            chain = [0]

            def link(ins):
                ins.then_inc(dve_step, 1)
                chain[0] += 1
                dve.wait_ge(dve_step, chain[0])

            turn_used = [None]

            def take_turn():
                if turn_used[0]:
                    dve.wait_ge(*turn_used[0])

            nxt = [0]

            def split(s, it=0):
                dve.wait_ge(hi_ready, s + 1 + BODY * it)
                n = width(s)
                V.tensor_tensor(w_lo[:, s % SPLIT, 0:n], raw[:, s % RING, 0:n], w_hi[:, s % SPLIT, 0:n].bitcast(f32),
                                ALU.subtract).then_inc(lo_ready, 1)

            def ahead(s, by=2):
                while nxt[0] <= min(s + by, NSLAB - 1):
                    split(nxt[0])
                    nxt[0] += 1

            def r2():
                return rstd[:, 0:1, :].to_broadcast([P, 2, T])

            def up_to_date(n, b):
                st = PREV[n]
                h = hT[:, 2 * b:2 * b + 2, :]
                if st[0] == "x":
                    pb = await_bank(dve, ("x", b))
                    ins = V.tensor_copy(h, halves(pb[:, :]))
                elif st[0] == "wout":
                    ahead(SL[("wout", st[1], b)])
                    pb = await_bank(dve, ("wout", st[1], b))
                    ins = V.tensor_tensor(h, halves(pb[:, :]), h, ALU.add)
                else:
                    if b < 3:
                        dve.wait_ge(acc_full, 3 * FF[st][1] + b + 1)
                    else:
                        dve.wait_ge(slab_done, SL[("d", st[1], FF1 - 1) if st[0] == "ffn1" else ("e", st[1], FF2 - 1)] + 1)
                    if st[0] == "ffn1":
                        ins = V.scalar_tensor_tensor(h, halves(acc[b][:, :]), 0.5, h, ALU.mult, ALU.add)
                    else:
                        ins = V.tensor_tensor(h, halves(acc[b][:, :]), h, ALU.add)
                ins.then_inc(h_ready, 1)

            def reciprocal(st):
                V.reciprocal(rstd[:, 0, :], rstd[:, 0, :]).then_inc(r_ready, 1)
                dve.wait_ge(r_ready, RN[st] + 1)

            def swish(st, i, buf, it=0):
                g, u = JOB[("g", st[1], i)][0], JOB[("u", st[1], i)]
                dve.wait_ge(slab_done, SL[("u", st[1], i)] + 1 + BODY * it)
                V.tensor_tensor(halves(silu_sb), halves(bank[g][:, :]), r2(), ALU.mult).then_inc(bank_free[g], 1)
                V.tensor_tensor(halves(hid[:, buf, :]), halves(bank[u[0]][:, :]), r2(), ALU.mult).then_inc(bank_free[u[0]], 1)

            def gated(st, i, buf, it=0):
                u, frees = JOB[("u", st[1], i)]
                dve.wait_ge(bank_free[u], frees + 1 + it)
                dve.wait_ge(silu_ready, FF[st][0] + i + 1 + 2 * it)
                V.tensor_tensor(hid[:, buf, :], silu_sb, hid[:, buf, :], ALU.mult).then_inc(hid_ready, 1)

            def relu(st, i, it=0):
                b, frees = JOB[("f", st[1], i)]
                dve.wait_ge(slab_done, SL[("f", st[1], i)] + 1 + BODY * it)
                V.scalar_tensor_tensor(halves(silu_sb), halves(bank[b][:, :]), 0.0, r2(), ALU.max, ALU.mult).then_inc(bank_free[b], 1)

            def rest(n, buf, turn):
                dve.wait_ge(hidh_ready, n + 1 + turn)
                V.tensor_tensor(hid_lo[:, buf, :], hid[:, buf, :], hid_hi[:, buf, :].bitcast(f32), ALU.subtract).then_inc(hidl_ready, 1)

            def prepare():
                dve.wait_ge(ident_in, 16)
                dve.wait_ge(consts_in, 16)
                at = C1["causal"][0]
                V.tensor_copy(identb[:, :], con("ident")).then_inc(setup, 1)
                V.tensor_copy(masks[:, :], cst[:, at:at + 768]).then_inc(setup, 1)
                dve.wait_ge(pos_in, 16)
                link(V.tensor_copy(turns, pos_i))
                link(V.tensor_scalar(ang, turns, con("inv64"), None, ALU.mult))
                link(V.tensor_scalar(turns, ang, 0.5 / PI, ROUND, ALU.mult, ALU.add))
                link(V.tensor_scalar(turns, turns, ROUND, None, ALU.subtract))
                link(V.scalar_tensor_tensor(red, turns, -TWO_PI_1, ang, ALU.mult, ALU.add))
                link(V.scalar_tensor_tensor(red, turns, -TWO_PI_2, red, ALU.mult, ALU.add))
                link(V.scalar_tensor_tensor(red, turns, -TWO_PI_3, red, ALU.mult, ALU.add))
                V.tensor_scalar(red, red, PI_LOW, -PI_LOW, ALU.min, ALU.max).then_inc(setup, 1)
                dve.wait_ge(setup, 3)
                V.scalar_tensor_tensor(ang, red, -1.0, red, ALU.mult, ALU.max).then_inc(setup, 1)
                dve.wait_ge(small_in, 16 * (len(GAINS) + 5))
                V.tensor_scalar(nsink[:, :], sink[:, :], -1.0, None, ALU.mult).then_inc(setup, 1)
                dve.wait_ge(*free_count(("gains", 1)))
                g3, g4 = GROW["norm_final"], GROW["g_mix_2"]
                V.tensor_tensor(gains[:, NGAIN:NGAIN + KD], gains[:, g3:g3 + KD], gains[:, g4:g4 + KD], ALU.mult).then_inc(setup, 1)

            def bc(ap, n, m):
                return ap.unsqueeze(2).to_broadcast([P, n, m])

            def weigh(dst, src, c, n):
                return V.tensor_tensor(dst.rearrange("p (h d) -> p h d", h=n), src.rearrange("p (h d) -> p h d", h=n),
                                       bc(c, n, HD), ALU.mult)

            for st in STEPS:
                kind = st[0]
                if kind == "gains":
                    if st[1]:
                        ahead(SL[("g", 0, 0)])
                    pb = await_bank(dve, st)
                    c = slice(0, KD) if st[1] == 0 else slice(KD, NGAIN)
                    V.tensor_copy(gains[:, c], pb[:, c]).then_inc(freed(st), 1)
                elif kind == "split":
                    n = st[1]
                    late = PREV[n][0] == "wout"
                    for b in range(5):
                        if b < (2 if late else 4):
                            up_to_date(n, b)
                        if b == 3 and n == 0:
                            ahead(-2)
                        for k in (2 * b - 2, 2 * b - 1) if b else ():
                            if late and k in (4, 6):
                                up_to_date(n, k // 2)
                            if late and k == 4:
                                ahead(SL[("wout", PREV[n][1], 3)])
                            dve.wait_ge(norm_h, NB[st] + k + 1)
                            V.scalar_tensor_tensor(n_lo[:, k, :], hT[:, k, :], gain(n, k), n_hi[:, k, :].bitcast(f32),
                                                   ALU.mult, ALU.subtract).then_inc(norm_l, 1)
                    if n == 0:
                        ahead(-1)
                    elif n in (2, 5, 7):
                        ahead(SL[FFN[n]])
                elif kind == "stat":
                    if st[1] == 4:
                        pb = bank[JOB[st][0]]
                        final, r = rstd[:, 2, :], rstd[:, 0, :]
                        dve.wait_ge(rank_std, 1)
                        link(V.reciprocal(final, final))
                        V.tensor_tensor(r, pb[:, T:2 * T], final, ALU.mult).then_inc(freed(st), 1)
                        dve.wait_ge(*free_count(st))
                        V.tensor_tensor(r, r, final, ALU.mult).then_inc(rank_mean, 1)
                        dve.wait_ge(rank_std, 2)
                        link(V.reciprocal(r, r))
                        V.tensor_tensor(r, r, final, ALU.mult).then_inc(r_ready, 1)
                        ahead(SL[("proj", 1, "cq0")])
                        for k in range(KD):
                            V.scalar_tensor_tensor(hT[:, k, :], hT[:, k, :], gain(3, k), final, ALU.mult, ALU.mult)
                    else:
                        dve.wait_ge(*free_count(st))
                        reciprocal(st)
                elif kind == "norm":
                    for b in range(4):
                        up_to_date(st[1], b)
                        dve.wait_ge(h_ready, HN[st[1]] + b + 1)
                        for k in (2 * b, 2 * b + 1):
                            V.tensor_scalar(work[:, k, :], hT[:, k, :], gain(8, k), None, ALU.mult).then_inc(norm_f, 1)
                    dve.wait_ge(*free_count(st))
                    V.reciprocal(rtok[:, 0, :], rtok[:, 0, :]).then_inc(r_ready, 1)
                elif kind == "ffn1":
                    s0 = SL[("g", st[1], 0)]

                    def turn(first, it, peeled=False):
                        for i in range(first, first + 2):
                            s = SL[("g", st[1], i)]
                            buf = (i - 1) % 2
                            if not peeled or s >= nxt[0]:
                                split(s, it)
                            swish(st, i - 1, buf, it)
                            split(s + 1, it)
                            gated(st, i - 1, buf, it)
                            split(s + 2, it)
                            rest(FF[st][0] + i - 1, buf, 2 * it)

                    turn(1, 0, peeled=True)
                    if st[1] == 0:
                        prepare()
                    with dve.Fori(0, (FF1 - 1) // 2 - 1) as it:
                        turn(3, it)
                    swish(st, FF1 - 1, (FF1 - 1) % 2)
                    nxt[0] = s0 + 3 * FF1 - 1
                    ahead(nxt[0], 0)
                    gated(st, FF1 - 1, (FF1 - 1) % 2)
                    rest(FF[st][0] + FF1 - 1, (FF1 - 1) % 2, 0)
                    ahead(s0 + 3 * FF1 - 1, 1)
                elif kind == "ffn2":
                    s0 = SL[("f", st[1], 0)]

                    def turn(first, it, peeled=False):
                        for i in range(first, first + 3):
                            relu(st, i - 1, it)
                            if not peeled or s0 + 2 * i >= nxt[0]:
                                split(s0 + 2 * i, it)
                            rest(FF[st][0] + i - 1, (i - 1) % 3, 3 * it)
                            split(s0 + 2 * i + 1, it)

                    turn(1, 0, peeled=True)
                    with dve.Fori(0, (FF2 - 1) // 3 - 1) as it:
                        turn(4, it)
                    relu(st, FF2 - 1)
                    rest(FF[st][0] + FF2 - 1, (FF2 - 1) % 3, 0)
                    nxt[0] = s0 + 2 * FF2
                    ahead(s0 + 2 * FF2 - 1, 1)
                elif kind in ("proj", "uq"):
                    ahead(SL[st])
                    if kind == "proj" and st[2] == "kcvc":
                        pb = await_bank(dve, st)
                        for v in range(2):
                            for g in range(2):
                                rows_, t0 = slice(64 * g, 64 * g + 64), v * T
                                V.tensor_tensor(x2[0:64, v, g, :], pb[rows_, t0:t0 + T], rstd[rows_, 0, :], ALU.mult)
                                last = V.tensor_tensor(x2[64:128, v, g, 0:T - 1], pb[rows_, t0 + 1:t0 + T], rstd[rows_, 0, 1:T], ALU.mult)
                        last.then_inc(freed(st), 1)
                    if kind == "proj" and st in OT:
                        pb = await_bank(dve, st)
                        k = 2 * ("cq0", "cq1", "cq2", "ckv").index(st[2])
                        dve.wait_ge(ot_hi, OT[st] + 1)
                        for i in range(2):
                            last = V.scalar_tensor_tensor(on_lo[:, k + i, :], pb[:, i * T:i * T + T], rank_gain(st[1], k + i),
                                                          on_hi[:, k + i, :].bitcast(f32), ALU.mult, ALU.subtract)
                        last.then_inc(freed(st), 1)
                elif kind == "gate":
                    ahead(SL[st])
                    pb = await_bank(dve, st)
                    V.tensor_tensor(sig_gate[:, 2 * st[1]:2 * st[1] + 2, :], halves(pb[:, :]), r2(), ALU.mult).then_inc(freed(st), 1)
                elif kind == "ukv":
                    ahead(SL[st])
                    for n in range(4):
                        pb = await_bank(dve, st + (n,))
                        V.tensor_tensor(kfull[0:64, 2 * n:2 * n + 2, :], halves(pb[0:64, :]), rstd[0:64, 2:3, :].to_broadcast([64, 2, T]),
                                        ALU.mult).then_inc(freed(st + (n,)), 1)
                elif kind == "rope":
                    r = RO[st[1:]]
                    _, n, nrow, _, (_, sin), dst = rotation(*st[1:])
                    pb = await_bank(dve, st)
                    dve.wait_ge(tab_ready, table_count(*st[1:]))
                    if st[2] == "kc":
                        view = [x[:, 0:32].rearrange("p (g c) -> p g c", g=2)[:, :, 0:NCMP] for x in (turn_s, pb, turn_c[:, r % 2])]
                        s_ = sin[:, 31:T:16].unsqueeze(1).to_broadcast([P, 2, NCMP])
                        dst = kcR[:, :, 0:NCMP]
                    else:
                        view = [x[0:nrow, 0:n * T].rearrange("p (a t) -> p a t", a=n) for x in (turn_s, pb, turn_c[:, r % 2])]
                        s_ = sin.unsqueeze(1).to_broadcast([nrow, n, T])
                    take_turn()
                    V.tensor_tensor(view[0], view[1], s_, ALU.mult).then_inc(freed(st), 1)
                    dve.wait_ge(*free_count(st))
                    dve.wait_ge(turnc_ready, r + 1)
                    V.tensor_tensor(dst, view[2], view[0], ALU.add).then_inc(rope_done, 1)
                    turn_used[0] = (rope_done, r + 1)
                elif kind == "xpe":
                    v = "kv".index(st[1])
                    if v == 0:
                        dve.wait_ge(*free_count(("proj", 0, "kcvc")))
                    if v:
                        dve.wait_ge(xpel_ready, v)
                    pe0 = GROW["cmp_pe_" + st[1]]
                    out_v = xpe.rearrange("p (a b g c) -> p a b g c", a=2, b=8, g=2)
                    for g in range(2):
                        for a in range(2):
                            src = x2[:, v, g, 16 * a:16 * a + 240].rearrange("p (c b e) -> p b c e", b=8, e=2)[:, :, :, 0]
                            last = V.tensor_tensor(out_v[:, a, :, g, :], src, bc(gains[:, pe0 + 8 * a:pe0 + 8 * a + 8], 8, NCMP), ALU.add)
                    last.then_inc(xpe_ready, 1)
                    dve.wait_ge(xpeh_ready, v + 1)
                    V.tensor_tensor(xpe_lo[:, v, :], xpe, xpe_hi[:, v, :].bitcast(f32), ALU.subtract).then_inc(xpel_ready, 1)
                elif kind == "cmp1":
                    ahead(SL[st + (0,)])
                    ahead(SL[st + (1,)])
                elif kind == "cmp2" and st[1] == "v":
                    pb = await_bank(dve, st)
                    V.tensor_tensor(vblk.rearrange("p (h d) -> p h d", h=8), pb[:, 0:HD].unsqueeze(1).to_broadcast([P, 8, HD]),
                                    bc(con("blk"), 8, HD), ALU.mult).then_inc(freed(st), 1)
                elif kind == "s":
                    _, l, a, t, g = st
                    q, nk = ATT[st[1:]], P * (t + 1)
                    heads = groups(a, t)[g]
                    nh, buf = len(heads), q % 3
                    pb = await_bank(dve, st)
                    ins = V.tensor_reduce(negm[:, buf, 0:nh], pb[:, :].rearrange("p (h k) -> p h k", h=nh), AX.X, ALU.max, negate=True)
                    if a == "swa":
                        hs = slice(heads[0], heads[-1] + 1, 2)
                        link(ins)
                        link(V.tensor_tensor(negm[:, buf, 0:nh], negm[:, buf, 0:nh], nsink[:, hs], ALU.min))
                        ins = V.tensor_tensor(dsink[:, t, hs], negm[:, buf, 0:nh], sink[:, hs], ALU.add)
                    ins.then_inc(negm_ready, 1)
                elif kind == "t":
                    n = PVN[st[1:]]
                    pb = await_bank(dve, st)
                    if n >= 2:
                        dve.wait_ge(pv_done, n - 1)
                    V.tensor_copy(probsT[:, n % 2, :], pb[:, :]).then_inc(freed(st), 1)
                elif kind == "o":
                    _, l, a, t = st
                    o, done = ON[st[1:]]
                    ob = acc[o % 4]
                    dve.wait_ge(pv_done, done)
                    if OO[st[1:]]:
                        dve.wait_ge(o_free, OO[st[1:]])
                    sums = rsum[:, RSLOT[a], t, :]
                    if a == "swa":
                        link(V.tensor_tensor(rinv8[:, :], sums, esink[:, t, :], ALU.add))
                        link(V.reciprocal(coef[:, :], rinv8[:, :]))
                        weigh(o_sum[:, 1, t, :], ob[:, :], coef[:, :], 8).then_inc(o_free, 1)
                    elif a in GATE:
                        link(V.reciprocal(rinv8[:, :], sums))
                        link(V.tensor_tensor(coef[:, :], rinv8[:, :], gates[:, t, 8 * GATE[a]:8 * GATE[a] + 8], ALU.mult))
                        if a == "slc":
                            weigh(o_sum[:, 0, t, :], ob[:, :], coef[:, :], 8).then_inc(o_free, 1)
                        else:
                            take_turn()
                            weigh(o_tmp[:, :], ob[:, :], coef[:, :], 8).then_inc(o_free, 1)
                            dve.wait_ge(o_free, OO[st[1:]] + 1)
                            ins = V.tensor_tensor(o_sum[:, 0, t, :], o_sum[:, 0, t, :], o_tmp[:, :], ALU.add)
                            if a == "cmp":
                                ins.then_inc(oc_ready, 1)
                                turn_used[0] = (oc_ready, t + 1)
                            else:
                                link(ins)
                                turn_used[0] = None
                    else:
                        nh = HEADS[a]
                        c0 = 0 if a == "mla" else 512
                        link(V.reciprocal(rinv8[:, 0:nh], sums[:, 0:nh]))
                        weigh(mix[:, t, c0:c0 + nh * HD], ob[:, 0:nh * HD], rinv8[:, 0:nh], nh).then_inc(o_free, 1)
                elif kind == "cs":
                    t = st[1]
                    pb = await_bank(dve, st)
                    s3 = pb[:, 0:P].rearrange("p (h c) -> p h c", h=8)
                    e3 = cmp_e[:, t, :].rearrange("p (h c) -> p h c", h=8)
                    link(V.tensor_reduce(cneg[:, t, :], s3, AX.X, ALU.max, negate=True))
                    V.tensor_tensor(e3, s3, bc(cneg[:, t, :], 8, CP), ALU.add).then_inc(cs_ready, 1)
                    dve.wait_ge(cexp_ready, t + 1)
                    V.tensor_reduce(rsum[:, RSLOT["cmp"], t, :], e3, AX.X, ALU.add).then_inc(freed(st), 1)
                    V.tensor_tensor(cmp_p[:, t, :], cmp_e[:, t, :], con("cmp_vis")[:, t * P:t * P + P], ALU.mult).then_inc(cp_ready, 1)
                elif kind == "ct":
                    n = PVN[(0, "cmp", st[1], 0)]
                    pb = await_bank(dve, st)
                    dve.wait_ge(pv_done, n - 1)
                    V.tensor_copy(probsT[:, n % 2, 0:P], pb[:, 0:P]).then_inc(freed(st), 1)
                elif kind == "idx":
                    _, l, n = st
                    t, heads = IDX[n]
                    nk = P * (t + 1)
                    if n == 0:
                        dve.wait_ge(*free_count(("toks", l)))
                    dve.wait_ge(*free_count(st))
                    part = score[:, t, 0:nk]
                    for i, h in enumerate(heads):
                        so_far = con("causal")[:, 256 - nk:256] if h == 0 else part
                        ins = V.scalar_tensor_tensor(part, probs[:, n % 3, i * nk:i * nk + nk], wit[:, t, h:h + 1], so_far,
                                                     ALU.mult, ALU.add)
                        if i == 0:
                            link(ins)
                    ins.then_inc(idx_done, 1)
                    dve.wait_ge(idx_done, 8 * (l - 1) + n + 1)
                elif kind == "topk":
                    _, l, t, r0, r1 = st
                    nk = P * (t + 1)
                    sc = score[:, t, 0:nk]
                    for r in range(r0, r1):
                        link(V.max(out=m8[:, :], in_=sc))
                        link(V.match_replace(out=sc, in_to_replace=m8[:, :], in_values=sc, imm_value=TAKEN))
                    if r1 == TOP_ROUNDS:
                        part = score[:, t, 256:256 + nk]
                        link(V.tensor_scalar(part, sc, 0.75 * TAKEN, NEG, ALU.is_gt, ALU.mult))
                        V.tensor_tensor(selb[:, t, 0:nk], part, con("causal")[:, 256 - nk:256], ALU.add).then_inc(sel_ready, 1)
                elif kind == "rank":
                    pb = await_bank(dve, st)
                    part = rstd[:, 1:3, :]
                    V.tensor_tensor(part, halves(pb[:, :]), r2(), ALU.mult).then_inc(freed(st), 1)
                    dve.wait_ge(*free_count(st))
                    V.tensor_tensor(part, part, r2(), ALU.mult).then_inc(rank_mean, 1)
                    dve.wait_ge(rank_std, 2 + st[1])
                    link(V.reciprocal(part, part))
                    V.tensor_tensor(part, part, r2(), ALU.mult).then_inc(r_ready, 1)
                elif kind == "ret":
                    _, l, n = st
                    pb = await_bank(dve, st)
                    if n < 2:
                        V.tensor_tensor(halves(probs[:, n, :]), halves(pb[:, :]), con("decay").rearrange("p (h q) -> p h q", h=4)[:, n::2, :],
                                        ALU.mult).then_inc(freed(st), 1)
                    else:
                        V.tensor_tensor(probs[:, n, :].rearrange("p (h q) -> p h q", h=4), pb[:, :].rearrange("p (h q) -> p h q", h=4),
                                        decay[:, :, 0, :], ALU.mult).then_inc(freed(st), 1)
                elif kind in ("retn", "rety"):
                    l = st[1]
                    o, _ = ON[(l, "ret")]
                    ob = acc[o % 4][:, :].rearrange("p (h d) -> p h d", h=8)
                    xc = o_tmp[:, :].rearrange("p (h d) -> p h d", h=8)
                    xc2 = scr[:, 6144:6656].rearrange("p (h d) -> p h d", h=8)
                    if kind == "retn":
                        dve.wait_ge(retv_done, l)
                        take_turn()
                        link(V.tensor_reduce(gn[:, 0, :], ob, AX.X, ALU.add))
                        link(V.tensor_scalar(gn[:, 1, :], gn[:, 0, :], -1.0 / HD, None, ALU.mult))
                        V.tensor_tensor(xc, ob, bc(gn[:, 1, :], 8, HD), ALU.add).then_inc(o_free, 1)
                        dve.wait_ge(o_free, OO[(l, "ret")] + 1)
                        link(V.tensor_tensor(xc2, xc, xc, ALU.mult))
                        V.tensor_reduce(gn[:, 2, :], xc2, AX.X, ALU.add).then_inc(ret_ready, 1)
                    else:
                        dve.wait_ge(act_step, l)
                        link(V.reciprocal(gn[:, 0, :], gn[:, 3, :]))
                        link(V.tensor_tensor(xc, xc, bc(gn[:, 0, :], 8, HD), ALU.mult))
                        tok = halves(o_tmp[:, :])
                        link(V.tensor_tensor(tok, tok, gret[:, l - 1, :].unsqueeze(1).to_broadcast([P, NT, T]), ALU.mult))
                        dve.wait_ge(*free_count(("proj", l, "rg")))
                        V.tensor_tensor(mix[:, :, 768:1024], tok, rgt[:, :, :], ALU.mult).then_inc(oc_ready, 1)
                        turn_used[0] = (oc_ready, NT + l)
                elif kind in ("ot", "mixt"):
                    for key, k0, t in split_jobs(st):
                        pb = bank[JOB[key][0]]
                        dve.wait_ge(ot_hi, OT[key] + 1)
                        c = slice(t * P, t * P + P)
                        hi, lo = (n_hi, n_lo) if kind == "ot" else (on_hi, on_lo)
                        V.tensor_tensor(lo[:, k0:k0 + 4, c], pb[:, :].rearrange("p (k c) -> p k c", k=4),
                                        hi[:, k0:k0 + 4, c].bitcast(f32), ALU.subtract).then_inc(freed(key), 1)
                elif kind == "branch":
                    ahead(SL[("wa", 0)])
                    dve.wait_ge(sig_ready, 8)
                    for b in range(5):
                        if b < 4:
                            part = work[:, 2 * b:2 * b + 2, :]
                            if b % 2 == 0:
                                dve.wait_ge(slab_done, SL[("wa", b // 2)] + 1)
                                for a in (b, b + 1):
                                    V.tensor_tensor(work[:, 2 * a:2 * a + 2, :], halves(acc[a][:, :]), sig_gate[:, 2 * a:2 * a + 2, :], ALU.mult)
                                ahead(SL[("wb", 0) if b == 0 else ("wa", 1)])
                            pb = await_bank(dve, ("wb", b))
                            take_turn()
                            V.tensor_tensor(halves(o_tmp[:, :]), halves(pb[:, :]), sig_gate[:, 8 + 2 * b:10 + 2 * b, :], ALU.mult)\
                                .then_inc(freed(("wb", b)), 1)
                            dve.wait_ge(*free_count(("wb", b)))
                            V.tensor_tensor(part, part, halves(o_tmp[:, :]), ALU.add).then_inc(merged, 1)
                            turn_used[0] = (merged, b + 1)
                        if b:
                            k = slice(2 * b - 2, 2 * b)
                            dve.wait_ge(ot_hi, OT[st] + b)
                            V.tensor_tensor(on_lo[:, k, :], work[:, k, :], on_hi[:, k, :].bitcast(f32), ALU.subtract).then_inc(ot_lo, 1)
                elif kind == "y":
                    _, t, h = st
                    if h == 1:
                        pb = await_bank(dve, st)
                        dve.wait_ge(r_ready, RN[("norm", 8)] + 1)
                        V.tensor_scalar(yout[:, t, 512:1024], pb[:, :], rtok[:, 0, t:t + 1], None, ALU.mult).then_inc(y_ready[t], 1)

        @block.tensor
        def _(pe):
            MM = nc.tensor.matmul
            fresh = [None]

            def group(out, K, stat, mov, first=True, last=True):
                for k in range(K):
                    if fresh[0] is not None:
                        pe.wait_ge(*fresh[0](k))
                    for n, (a, b) in enumerate(((0, 0), (0, 1), (1, 0))):
                        mm = MM(out, stat(k, a), mov(k, b), start=(first and k == 0 and n == 0),
                                stop=(last and k == K - 1 and n == 2), skip_group_check=True)
                if K == KD:
                    fresh[0] = None
                return mm

            def acc_read(o):
                if o >= 4:
                    pe.wait_ge(o_free, OO[OWNER[o - 4]] + 1)

            settled = [0]

            def settle(mm):
                settled[0] += 1
                mm.then_inc(rows_done, 1)
                pe.wait_ge(rows_done, settled[0])

            def weights(s):
                pe.wait_ge(lo_ready, s + 1)

            def w(s, lo):
                return (wl if lo else wh)(s)

            def xn(k, lo):
                return (n_lo if lo else n_hi)[:, k, :]

            def on(k, lo):
                return (on_lo if lo else on_hi)[:, k, :]

            def features(out, s, wide, c0, n, K=KD, k0=0, xn=xn):
                return group(out, K, lambda k, lo: w(s, lo)[:, k * wide + c0:k * wide + c0 + n], lambda k, lo: xn(k0 + k, lo))

            def tokens(out, s, wide, c0, n, t):
                return group(out, KD, lambda k, lo: xn(k, lo)[:, t * P:t * P + P],
                             lambda k, lo: w(s, lo)[:, k * wide + c0:k * wide + c0 + n])

            def pair(pb, s, xn=xn):
                for m in range(2):
                    mm = features(pb[:, m * T:m * T + T], s, 256, m * P, P, xn=xn)
                return mm

            def up(key, it=0):
                s = SL[key]
                b, frees = JOB[key]
                pe.wait_ge(lo_ready, s + 1 + BODY * it)
                if frees:
                    pe.wait_ge(bank_free[b], frees + it)
                if key in SPECIAL:
                    pe.wait_ge(BYNAME[SPECIAL[key][0]], SPECIAL[key][1])
                pair(bank[b], s).then_inc(slab_done, 1)

            def down(key, n, buf, it=0, turn=0, final=False):
                s = SL[key]
                pe.wait_ge(lo_ready, s + 1 + BODY * it)
                pe.wait_ge(hidl_ready, n + 1 + turn)
                for m in range(KD):
                    mm = group(acc[m // 2][:, (m % 2) * T:(m % 2) * T + T], 2,
                               lambda k, lo: w(s, lo)[:, k * D + m * P:k * D + m * P + P],
                               lambda k, lo: (hid_lo if lo else hid_hi)[:, buf, k * T:k * T + T], first=False)
                    if final and m in (1, 3, 5):
                        mm.then_inc(acc_full, 1)
                mm.then_inc(slab_done, 1)

            def clear():
                for b in range(4):
                    MM(acc[b][:, :], zerob[:, 0:P], zerob[:, :], start=True, stop=True, skip_group_check=True)

            def keep_warm(n):
                for _ in range(n):
                    MM(acc[0][:, :], zerob[:, 0:P], zerob[:, :], start=True, stop=True, skip_group_check=True)

            def turn_gains(st):
                n = KD if st[1] == 0 else NGAIN
                pe.wait_ge(gain0_in, 16)
                if st[1]:
                    pe.wait_ge(small_in, 16 * (len(GAINS) + 5))
                pb = take(pe, st)
                nc.tensor.transpose(pb[:, 0:n], gain_rows[0:n, :], ident[0:n, 0:n]).then_inc(filled(st), 1)

            def last_norm(st, quarters):
                pb = take(pe, st)
                for b in quarters:
                    pe.wait_ge(sq_ready, HN[8] + b + 1)
                    for k in (2 * b, 2 * b + 1):
                        for t in range(NT):
                            mm = MM(pb[:, t:t + 1], sq[:, k, t * P:t * P + P], ones[:, 0:1], start=(k == 0 and t == 0),
                                    stop=(k == KD - 1), skip_group_check=True)
                return mm

            def stat(st):
                pb = take(pe, st)
                pe.wait_ge(sq_sum, SS[st] + 1)
                mm = MM(pb[:, 0:T], ones[:, :], sq[:, 0, :], start=True, stop=True)
                if st[1] == 4:
                    pe.wait_ge(sq_sum, SS[st + ("final",)] + 1)
                    mm = MM(pb[:, T:2 * T], ones[:, :], work[:, 0, :], start=True, stop=True)
                mm.then_inc(filled(st), 1)

            pe.wait_ge(pool_setup, 8)
            keep_warm(10)
            pe.wait_ge(ident_in, 16)
            ident = con("ident")
            for st in STEPS:
                kind = st[0]
                if kind == "gains" and st[1] == 0:
                    turn_gains(st)
                elif kind == "x":
                    b = st[1]
                    if b == 0:
                        pe.wait_ge(x_in, 16 * NT)
                    pb = take(pe, st)
                    for k in range(2):
                        for t in range(NT):
                            mm = nc.tensor.transpose(pb[:, k * T + t * P:k * T + t * P + P], xin[:, t, (2 * b + k) * P:(2 * b + k + 1) * P], ident)
                    mm.then_inc(filled(st), 1)
                    if b == 3:
                        keep_warm(16)
                elif kind == "norm":
                    last_norm(st, range(0, 2))
                elif kind == "split":
                    if st[1] == 1:
                        pe.wait_ge(consts_in, 16)
                        pe.wait_ge(setup, 2)
                    fresh[0] = lambda k, n=NB[st]: (norm_l, n + k + 1)
                elif kind == "stat":
                    if st[1] in (1, 4, 6):
                        stat(st)
                elif kind == "toks":
                    w_ = 88 if st[1] == 0 else 72
                    pe.wait_ge(*free_count(("proj", st[1], "misc")))
                    pb = take(pe, st)
                    for t in range(NT):
                        mm = nc.tensor.transpose(pb[:, t * w_:t * w_ + w_], by_feature[0:w_, t * P:t * P + P], ident[0:w_, 0:w_])
                    mm.then_inc(filled(st), 1)
                elif kind == "rtok":
                    norm = ("stat", st[1]) if st[1] > 0 else ("rank", -st[1])
                    pe.wait_ge(r_ready, RN[norm] + 1)
                    pb = take(pe, st)
                    for t in range(NT):
                        mm = nc.tensor.transpose(pb[:, t * P:t * P + P], rstd[:, 0 if st[1] > 0 else 2, t * P:t * P + P], ident)
                    mm.then_inc(filled(st), 1)
                elif kind == "ffn1":
                    f = st[1]
                    base = FF[st][0]
                    up(("g", f, 0))
                    stat(("stat", 2 * f))
                    clear()
                    up(("u", f, 0))
                    if f == 0:
                        turn_gains(("gains", 1))
                    with pe.Fori(0, (FF1 - 1) // 2) as it:
                        for i in (1, 2):
                            for c in "gu":
                                up((c, f, i), it)
                            down(("d", f, i - 1), base + i - 1, (i - 1) % 2, it, 2 * it)
                    down(("d", f, FF1 - 1), base + FF1 - 1, (FF1 - 1) % 2, final=True)
                elif kind == "ffn2":
                    l = st[1]
                    base = FF[st][0]
                    up(("f", l, 0))
                    stat(("stat", 3 + 2 * l))
                    clear()
                    with pe.Fori(0, (FF2 - 1) // 3) as it:
                        for i in (1, 2, 3):
                            up(("f", l, i), it)
                            down(("e", l, i - 1), base + i - 1, (i - 1) % 3, it, 3 * it)
                    down(("e", l, FF2 - 1), base + FF2 - 1, (FF2 - 1) % 3, final=True)
                elif kind == "proj":
                    _, l, name = st
                    s = SL[st]
                    weights(s)
                    pb = take(pe, st)
                    if name == "misc":
                        wide, n = (152, 64) if l == 0 else (200, 128)
                        features(pb[0:n, 0:T], s, wide, 0, n)
                        mm = features(pb[0:wide - n, T:2 * T], s, wide, n, wide - n)
                    elif name in ("vv", "rv", "rg"):
                        for t in range(NT):
                            mm = tokens(pb[:, T * t:T * t + T], s, 256, 0, 256, t)
                    else:
                        mm = pair(pb, s)
                    mm.then_inc(filled(st), 1)
                elif kind == "uq":
                    if st[2] == 0:
                        for name in ("cq0", "cq1", "cq2", "ckv"):
                            pe.wait_ge(*free_count(("proj", st[1], name)))
                    s = SL[st]
                    weights(s)
                    pb = take(pe, st)
                    for i in range(2):
                        mm = features(pb[0:MLA_Q, i * T:i * T + T], s, 192, i * MLA_Q, MLA_Q, K=6, xn=on)
                    mm.then_inc(filled(st), 1)
                elif kind == "ukv":
                    s = SL[st]
                    weights(s)
                    for n in range(4):
                        pb = take(pe, st + (n,))
                        for i in range(2):
                            mm = features(pb[:, i * T:i * T + T], s, D, (2 * n + i) * P, P, K=2, k0=6, xn=on)
                        mm.then_inc(filled(st + (n,)), 1)
                    for t in range(NT):
                        pb = take(pe, st + (4 + t,))
                        mm = group(pb[:, :], 2, lambda k, lo: on(6 + k, lo)[:, t * P:t * P + P],
                                   lambda k, lo: w(s, lo)[:, k * D:k * D + D].rearrange("p (h c) -> p h c", h=8)[:, :, 64:128])
                        mm.then_inc(filled(st + (4 + t,)), 1)
                elif kind == "rope":
                    src, n, nrow, perm, _, _ = rotation(*st[1:])
                    pe.wait_ge(*free_count(XSC[st[1:]][0]))
                    pb = take(pe, st)
                    if st[2] == "kc":
                        mm = MM(pb[:, 0:32], perm, xs1[:, 0, 0:32], start=True, stop=True)
                    else:
                        mm = MM(pb[0:nrow, 0:n * T], perm, src, start=True, stop=True)
                    mm.then_inc(filled(st), 1)
                elif kind == "cmp1":
                    v = "kv".index(st[1])
                    pb = take(pe, st)
                    pe.wait_ge(xpel_ready, v + 1)
                    for half in range(2):
                        s = SL[st + (half,)]
                        weights(s)
                        for i in range(8):
                            c = (8 * half + i) * 30
                            mm = group(pb[0:2 * NCMP, 0:256], 1, lambda k, lo: (xpe_lo if lo else xpe_hi)[:, v, c:c + 30],
                                       lambda k, lo: w(s, lo)[:, i * 256:i * 256 + 256], first=(half == 0 and i == 0),
                                       last=(half == 1 and i == 7))
                        mm.then_inc(slab_done, 1)
                elif kind == "cmpt":
                    v = "kv".index(st[1])
                    pe.wait_ge(*free_count(("cmp1", st[1])))
                    pb = take(pe, st)
                    for m in range(2):
                        mm = nc.tensor.transpose(pb[:, m * P:m * P + 2 * NCMP], cmp_h[:, v, m * P:m * P + P], ident[0:2 * NCMP, 0:2 * NCMP])
                    mm.then_inc(filled(st), 1)
                elif kind == "cmp2":
                    v = "kv".index(st[1])
                    pe.wait_ge(*free_count(("cmpt", st[1])))
                    pb = take(pe, st)
                    for m in range(2):
                        if v == 0:
                            mm = MM(pb[:, 0:32], cmp_w2k[:, m, :, :].rearrange("p a d -> p (a d)"), gkT[:, m, :, :],
                                    start=(m == 0), stop=(m == 1))
                        else:
                            mm = MM(pb[:, 0:HD], gvT[:, m, :, :, :].rearrange("p g h c -> p (g h c)"), cmp_w2v[:, m, :],
                                    start=(m == 0), stop=(m == 1))
                    mm.then_inc(filled(st), 1)
                elif kind == "gate":
                    s = SL[st]
                    weights(s)
                    pair(take(pe, st), s).then_inc(filled(st), 1)
                elif kind == "s":
                    _, l, a, t, g = st
                    heads, nk = groups(a, t)[g], P * (t + 1)
                    nh = len(heads)
                    if g == 0:
                        need = {"slc": ("k", "nq1"), "win": ("k", "nq1"), "swa": ("sk", "sq1"), "dsa": ("ak", "aq"), "mla": ("uq3",)}[a]
                        pe.wait_ge(rope_done, max(RO[(l, u)] for u in need) + 1)
                        if a == "mla":
                            pe.wait_ge(kr_done, l)
                            pe.wait_ge(*free_count(("ukv", l, 3)))
                        if a == "dsa":
                            pe.wait_ge(sel_ready, 2 * (l - 1) + t + 1)
                    pb = take(pe, st)
                    MM(pb[:, 0:nh * nk], identb[:, :], mask_of(a, t).unsqueeze(1).to_broadcast([P, nh, nk]), start=True, stop=False,
                       skip_group_check=True)
                    for i, h in enumerate(heads):
                        if a == "dsa" and t == 0 and i == 2:
                            settle(mm)
                        q_, k_ = operands(l, a, t, h)
                        mm = MM(pb[:, i * nk:i * nk + nk], q_, k_[:, 0:nk], start=False, stop=True, skip_group_check=True)
                    mm.then_inc(filled(st), 1)
                elif kind == "t":
                    q = ATT[st[1:]]
                    pe.wait_ge(*free_count(("s",) + st[1:]))
                    pb = take(pe, st)
                    for c in range(4):
                        mm = nc.tensor.transpose(pb[:, c * P:c * P + P], probs[:, q % 3, c * P:c * P + P], ident)
                    mm.then_inc(filled(st), 1)
                elif kind == "pv":
                    _, l, a, t, g = st
                    heads, n, o = groups(a, t)[g], PVN[st[1:]], ON[st[1:4]][0]
                    if g == 0:
                        src = {"slc": ("proj", 0, "vv"), "win": ("proj", 0, "vv"), "swa": ("toks", 0),
                               "dsa": ("toks", l), "mla": ("ukv", l, 5)}[a]
                        pe.wait_ge(*free_count(src))
                        acc_read(o)
                    pe.wait_ge(*free_count(("t",) + st[1:]))
                    for i, h in enumerate(heads):
                        for blk in range(t + 1):
                            c = (i * (t + 1) + blk) * P
                            mm = MM(acc[o % 4][:, h * HD:h * HD + HD], probsT[:, n % 2, c:c + P], values(a, h, blk),
                                    start=(blk == 0), stop=(blk == t))
                    mm.then_inc(pv_done, 1)
                elif kind == "cs":
                    t = st[1]
                    pe.wait_ge(rope_done, RO[(0, "kc")] + 1)
                    pb = take(pe, st)
                    MM(pb[:, 0:P], identb[:, :], masks[:, 512 + t * P:512 + t * P + P], start=True, stop=False, skip_group_check=True)
                    for h in range(8):
                        if h == 4:
                            settle(mm)
                        r = slice(64 * (h // 4), 64 * (h // 4) + 64)
                        mm = MM(pb[:, h * CP:h * CP + CP], nqT[r, h % 4, t * P:t * P + P], kcR[r, h // 4, :], start=False, stop=True,
                                skip_group_check=True)
                    mm.then_inc(filled(st), 1)
                elif kind == "ct":
                    t = st[1]
                    n, o = PVN[(0, "cmp", t, 0)], ON[(0, "cmp", t)][0]
                    pe.wait_ge(cp_ready, t + 1)
                    pb = take(pe, st)
                    nc.tensor.transpose(pb[:, 0:P], cmp_p[:, t, :], ident).then_inc(filled(st), 1)
                    acc_read(o)
                    pe.wait_ge(*free_count(("cmp2", "v")))
                    pe.wait_ge(*free_count(st))
                    MM(acc[o % 4][:, :], probsT[:, n % 2, 0:P], vblk, start=True, stop=True).then_inc(pv_done, 1)
                elif kind == "idx":
                    _, l, n = st
                    t, heads = IDX[n]
                    nk = P * (t + 1)
                    if n == 0:
                        pe.wait_ge(rope_done, max(RO[(l, "ki")], RO[(l, "qi")]) + 1)
                    pb = take(pe, st)
                    for i, h in enumerate(heads):
                        r = slice(32 * (h % 4), 32 * (h % 4) + 32)
                        mm = MM(pb[:, i * nk:i * nk + nk], qiT[r, h // 4, t * P:t * P + P], kiT[r, 0, 0:nk], start=True, stop=True)
                    mm.then_inc(filled(st), 1)
                elif kind == "rank":
                    pe.wait_ge(sq_sum, SS[st] + 1)
                    pb = take(pe, st)
                    MM(pb[:, 0:T], ones[:, :], sq[:, 0, :], start=True, stop=True)
                    MM(pb[:, T:2 * T], ones[:, :], sq[:, 6, :], start=True, stop=True).then_inc(filled(st), 1)
                elif kind == "ret":
                    _, l, n = st
                    if n == 0:
                        pe.wait_ge(rope_done, max(RO[(l, "rk")], RO[(l, "rq")]) + 1)
                    pb = take(pe, st)
                    blk, first, n_q = (0, 0, T) if n < 2 else (1, P, P)
                    for h in (n, n + 2) if n < 2 else (0, 2, 1, 3):
                        i = h // 2 if n < 2 else h
                        if n == 2 and h == 1:
                            settle(mm)
                        r = slice(64 * (h % 2), 64 * (h % 2) + 64)
                        mm = MM(pb[:, i * n_q:i * n_q + n_q], rkT[r, h // 2, blk * P:blk * P + P], rqT[r, h // 2, first:T], start=True, stop=True)
                    mm.then_inc(filled(st), 1)
                elif kind == "retv":
                    l = st[1]
                    o = ON[(l, "ret")][0]
                    for n in range(3):
                        pe.wait_ge(*free_count(("ret", l, n)))
                    pe.wait_ge(*free_count(("proj", l, "rv")))
                    acc_read(o)
                    for t in range(NT):
                        for h in range(4):
                            oc = acc[o % 4][:, (4 * t + h) * HD:(4 * t + h) * HD + HD]
                            c = (h // 2) * T + t * P
                            v_ = rvt[:, :, h * HD:h * HD + HD]
                            mm = MM(oc, probs[:, h % 2, c:c + P], v_[:, 0], start=True, stop=(t == 0))
                            if t:
                                mm = MM(oc, probs[:, 2, h * P:h * P + P], v_[:, 1], start=False, stop=True)
                    mm.then_inc(retv_done, 1)
                elif kind in ("ot", "mixt"):
                    if kind == "ot":
                        if st[1] == "a":
                            pe.wait_ge(oc_ready, st[2] + 1)
                        pe.wait_ge(o_free, OO[(0, "cmp" if st[1] == "a" else "swa", st[2])] + 1)
                    else:
                        pe.wait_ge(oc_ready, 2 + st[1])
                        pe.wait_ge(o_free, OO[(st[1], "mla", st[2])] + 1)
                    for key, k0, t in split_jobs(st):
                        pb = take(pe, key)
                        src = o_sum[:, 0 if st[1] == "a" else 1, t, :] if kind == "ot" else mix[:, t, k0 * P:k0 * P + 512]
                        for c in range(4):
                            mm = nc.tensor.transpose(pb[:, c * P:c * P + P], src[:, c * P:c * P + P], ident)
                        mm.then_inc(filled(key), 1)
                elif kind == "branch":
                    for x in "ab":
                        for t in range(NT):
                            pe.wait_ge(*free_count(("ot", x, t)))
                    for n in range(2):
                        for x, key in enumerate(("wa", "wb")):
                            s = SL[(key, n)]
                            weights(s)
                            for m in range(4):
                                b = 2 * n + m // 2
                                if x and m % 2 == 0:
                                    take(pe, ("wb", b))
                                bk = acc[b] if x == 0 else bank[JOB[("wb", b)][0]]
                                mm = group(bk[:, (m % 2) * T:(m % 2) * T + T], 4, lambda k, lo: w(s, lo)[:, k * 512 + m * P:k * 512 + m * P + P],
                                           lambda k, lo: xn(4 * x + k, lo), first=(m % 2 == 0))
                                if x and m == 1:
                                    mm.then_inc(filled(("wb", b)), 1)
                            mm.then_inc(slab_done, 1)
                elif kind == "wout":
                    _, l, n = st
                    s = SL[st]
                    weights(s)
                    if n == 0:
                        if l == 0:
                            fresh[0] = lambda k: (ot_lo, k // 2 + 1)
                        else:
                            for b in range(2):
                                pe.wait_ge(*free_count(("mixt", l, 0, b)))
                            fresh[0] = lambda k: free_count(("mixt", l, 1, k // 4))
                    pair(take(pe, st), s, on).then_inc(filled(st), 1)
                elif kind == "y":
                    _, t, h = st
                    if t == 0 and h == 1:
                        last_norm(("norm", 8), range(2, 4)).then_inc(filled(("norm", 8)), 1)
                    pe.wait_ge(norm_f, 4 * h + 4)
                    pb = take(pe, st)
                    for c in range(4):
                        mm = nc.tensor.transpose(pb[:, c * P:c * P + P], work[:, 4 * h + c, t * P:t * P + P], ident)
                    mm.then_inc(filled(st), 1)


_OUTS = [((1, 256, 1024), "float32")]


def kernel(**inputs):
    import numpy as _np
    import concourse.bacc as _bacc
    from concourse import mybir as _mybir
    from concourse.bass_utils import run_bass_kernel_spmd as _run

    nc = _bacc.Bacc("TRN2", target_bir_lowering=False, num_devices=1)
    arrays, given = {}, {}
    const1, const2 = constants()
    for name, a in dict(inputs, const1=const1, const2=const2).items():
        a = _np.ascontiguousarray(a)
        arrays[f"in_{name}_dram"] = a
        given[name] = nc.dram_tensor(f"in_{name}_dram", a.shape, _mybir.dt.from_np(a.dtype), kind="ExternalInput").ap()
    const1, const2 = given.pop("const1"), given.pop("const2")
    shape, dtype = _OUTS[0]
    out = nc.dram_tensor("out_0_dram", shape, _mybir.dt.from_np(_np.dtype(dtype)), kind="ExternalOutput").ap()
    two_blocks(nc, given, const1, const2, out)
    r = _run(nc, [arrays], core_ids=[0])
    return r.results[0]["out_0_dram"]
```
